# Optimizing a Trainium2 kernel written in Bass

```python
import jax, jax.numpy as jnp
from jax import lax
import numpy as np
import math

D_MODEL = 1024
BATCH = 1
SEQ = 512
DEPTH = 2

N_A_LAYERS = DEPTH // 2
N_B_LAYERS = DEPTH - N_A_LAYERS
CHUNK = 128
GMLP_WIDTH = 2 * D_MODEL
GMLP_GROUPS = 16
GMLP_GROUP_DIM = GMLP_WIDTH // GMLP_GROUPS
N_HEADS = 16
HEAD_DIM = D_MODEL // N_HEADS
Q_BLOCK = 128
FFN_HIDDEN = -(-8 * D_MODEL // (3 * 256)) * 256
EPS = 1e-6


def rms_norm(x, g):
    xf = x.astype(jnp.float32)
    y = xf * lax.rsqrt(jnp.mean(xf * xf, axis=-1, keepdims=True) + EPS)
    return (y * g.astype(jnp.float32)).astype(x.dtype)

def layer_norm(x, g, b):
    xf = x.astype(jnp.float32)
    mu = jnp.mean(xf, axis=-1, keepdims=True)
    xc = xf - mu
    y = xc * lax.rsqrt(jnp.mean(xc * xc, axis=-1, keepdims=True) + EPS)
    return (y * g.astype(jnp.float32) + b.astype(jnp.float32)).astype(x.dtype)

def modulate(h, shift, scale):
    return h * (1 + scale[:, None, :]) + shift[:, None, :]

def swiglu(h, w_gu, w_down):
    gu = h @ w_gu
    g, u = jnp.split(gu, 2, axis=-1)
    return (jax.nn.silu(g) * u) @ w_down

def gmlp_mixer(h, w_in, b_in, ln_g, ln_b, w_s, b_s, w_out):
    B, S, _ = h.shape
    z = jax.nn.gelu(h @ w_in + b_in)
    u, v = jnp.split(z, 2, axis=-1)
    v = layer_norm(v, ln_g, ln_b)
    v = v.reshape(B, S // CHUNK, CHUNK, GMLP_GROUPS, GMLP_GROUP_DIM)
    causal = jnp.tril(jnp.ones((CHUNK, CHUNK), dtype=w_s.dtype))
    ws = w_s * causal[None]
    v = jnp.einsum('gts,bnsgc->bntgc', ws, v) + b_s.T[:, :, None]
    y = u * v.reshape(B, S, GMLP_WIDTH)
    return y @ w_out

def shared_kv(x, mod_kv, kv_norm_g, kv_w, kv_b_f, k_norm_g):
    B, S, _ = x.shape
    shift, scale = jnp.split(mod_kv, 2, axis=-1)
    h = modulate(rms_norm(x, kv_norm_g), shift, scale)
    kvf = h @ kv_w
    k = kvf[..., :D_MODEL].reshape(B, S, N_HEADS, HEAD_DIM)
    k = rms_norm(k, k_norm_g).transpose(0, 2, 1, 3)
    v = kvf[..., D_MODEL:2 * D_MODEL].reshape(B, S, N_HEADS, HEAD_DIM).transpose(0, 2, 1, 3)
    f_logit = kvf[..., 2 * D_MODEL:].astype(jnp.float32) + kv_b_f.astype(jnp.float32)
    dcum = jnp.cumsum(jax.nn.log_sigmoid(f_logit), axis=1).transpose(0, 2, 1)
    return k, v, dcum

def fox_attention(q, k, v, dcum):
    B, H, S, Dh = q.shape
    nb = S // Q_BLOCK
    qb = q.reshape(B, H, nb, Q_BLOCK, Dh).transpose(2, 0, 1, 3, 4)
    db = dcum.reshape(B, H, nb, Q_BLOCK).transpose(2, 0, 1, 3)
    kpos = jnp.arange(S)
    scale = HEAD_DIM ** -0.5

    def block(args):
        qi, di, i = args
        qpos = i * Q_BLOCK + jnp.arange(Q_BLOCK)
        logits = jnp.einsum('bhqd,bhkd->bhqk', qi, k).astype(jnp.float32) * scale
        logits = logits + di[..., :, None] - dcum[..., None, :]
        logits = jnp.where(kpos[None, :] <= qpos[:, None], logits, -jnp.inf)
        p = jax.nn.softmax(logits, axis=-1)
        return jnp.einsum('bhqk,bhkd->bhqd', p.astype(v.dtype), v)

    o = lax.map(block, (qb, db, jnp.arange(nb)))
    return o.transpose(1, 2, 0, 3, 4).reshape(B, H, S, Dh)

def fox_mixer(h, w_qg, q_norm_g, w_o, k, v, dcum):
    B, S, _ = h.shape
    qg = h @ w_qg
    q = qg[..., :D_MODEL].reshape(B, S, N_HEADS, HEAD_DIM)
    q = rms_norm(q, q_norm_g).transpose(0, 2, 1, 3)
    gate = jax.nn.sigmoid(qg[..., D_MODEL:])
    o = fox_attention(q, k, v, dcum).transpose(0, 2, 1, 3).reshape(B, S, D_MODEL)
    return (o * gate) @ w_o

def first_inputs(seed: int = 0) -> dict:
    key = jax.random.key(seed)
    ks = jax.random.split(key, 26)
    D, F, GW = D_MODEL, FFN_HIDDEN, GMLP_WIDTH

    def nrm(k, shape, scale):
        return jax.random.normal(k, shape, jnp.float32) * scale

    def gain(k, shape):
        return 1.0 + nrm(k, shape, 0.05)

    return {
        "x": nrm(ks[0], (BATCH, SEQ, D), 1.0),
        "c": nrm(ks[1], (BATCH, D), 1.0),
        "ada_w": nrm(ks[2], (DEPTH, D, 6 * D), 0.5 * D ** -0.5),
        "ada_b": nrm(ks[3], (DEPTH, 6 * D), 0.01),
        "pre_mix_g": gain(ks[4], (DEPTH, D)),
        "post_mix_g": gain(ks[5], (DEPTH, D)),
        "pre_ffn_g": gain(ks[6], (DEPTH, D)),
        "post_ffn_g": gain(ks[7], (DEPTH, D)),
        "ffn_w_gu": nrm(ks[8], (DEPTH, D, 2 * F), D ** -0.5),
        "ffn_w_down": nrm(ks[9], (DEPTH, F, D), F ** -0.5),
        "a_w_in": nrm(ks[10], (N_A_LAYERS, D, 2 * GW), D ** -0.5),
        "a_b_in": nrm(ks[11], (N_A_LAYERS, 2 * GW), 0.01),
        "a_ln_g": gain(ks[12], (N_A_LAYERS, GW)),
        "a_ln_b": nrm(ks[13], (N_A_LAYERS, GW), 0.01),
        "a_w_s": nrm(ks[14], (N_A_LAYERS, GMLP_GROUPS, CHUNK, CHUNK), 0.5 * CHUNK ** -0.5),
        "a_b_s": 1.0 + nrm(ks[15], (N_A_LAYERS, GMLP_GROUPS, CHUNK), 0.1),
        "a_w_out": nrm(ks[16], (N_A_LAYERS, GW, D), GW ** -0.5),
        "kv_ada_w": nrm(ks[17], (D, 2 * D), 0.5 * D ** -0.5),
        "kv_ada_b": nrm(ks[18], (2 * D,), 0.01),
        "kv_norm_g": gain(ks[19], (D,)),
        "kv_w": nrm(ks[20], (D, 2 * D + N_HEADS), D ** -0.5),
        "kv_b_f": jax.random.uniform(ks[21], (N_HEADS,), jnp.float32, 1.0, 5.0),
        "k_norm_g": gain(ks[22], (HEAD_DIM,)),
        "b_w_qg": nrm(ks[23], (N_B_LAYERS, D, 2 * D), D ** -0.5),
        "b_q_norm_g": gain(ks[24], (N_B_LAYERS, HEAD_DIM)),
        "b_w_o": nrm(ks[25], (N_B_LAYERS, D, D), D ** -0.5),
    }

def first_block(x, c, ada_w, ada_b, pre_mix_g, post_mix_g, pre_ffn_g, post_ffn_g,
              ffn_w_gu, ffn_w_down, a_w_in, a_b_in, a_ln_g, a_ln_b, a_w_s, a_b_s,
              a_w_out, kv_ada_w, kv_ada_b, kv_norm_g, kv_w, kv_b_f, k_norm_g,
              b_w_qg, b_q_norm_g, b_w_o):
    c_act = jax.nn.silu(c)
    k = v = dcum = None
    for layer in range(DEPTH):
        mod = c_act @ ada_w[layer] + ada_b[layer]
        sh_m, sc_m, g_m, sh_f, sc_f, g_f = jnp.split(mod, 6, axis=-1)
        h = modulate(rms_norm(x, pre_mix_g[layer]), sh_m, sc_m)
        if layer < N_A_LAYERS:
            i = layer
            y = gmlp_mixer(h, a_w_in[i], a_b_in[i], a_ln_g[i], a_ln_b[i],
                           a_w_s[i], a_b_s[i], a_w_out[i])
        else:
            j = layer - N_A_LAYERS
            y = fox_mixer(h, b_w_qg[j], b_q_norm_g[j], b_w_o[j], k, v, dcum)
        x = x + g_m[:, None, :] * rms_norm(y, post_mix_g[layer])
        h = modulate(rms_norm(x, pre_ffn_g[layer]), sh_f, sc_f)
        y = swiglu(h, ffn_w_gu[layer], ffn_w_down[layer])
        x = x + g_f[:, None, :] * rms_norm(y, post_ffn_g[layer])
        if layer == N_A_LAYERS - 1:
            k, v, dcum = shared_kv(x, c_act @ kv_ada_w + kv_ada_b, kv_norm_g,
                                   kv_w, kv_b_f, k_norm_g)
    return x


DEPTH_2 = 1

D_PLE = 256
M_HEADS = 4
M_QK = 128
M_V = 256
M_WIDTH = M_HEADS * M_V
M_CHUNK = 64
CONV_W = 4
A_HEADS = 8
A_DH = 64
A_WIDTH = A_HEADS * A_DH
IDX_HEADS = 8
IDX_DH = 64
TOPK_MAX = 256
REL_BUCKETS = 32
REL_MAX_DIST = 128
D_MIX = M_WIDTH + A_WIDTH

PROJ_SIZES = [
    M_HEADS * M_QK,
    M_HEADS * M_QK,
    M_WIDTH,
    M_WIDTH,
    M_WIDTH,
    2 * M_HEADS,
    A_WIDTH,
    A_WIDTH,
    A_WIDTH,
    A_WIDTH,
    IDX_HEADS * IDX_DH,
    IDX_DH,
    IDX_HEADS,
]
PROJ_TOTAL = int(sum(PROJ_SIZES))
SPLIT_POINTS = [int(v) for v in np.cumsum(PROJ_SIZES)[:-1]]


def rmsnorm(x, g):
    xf = x.astype(jnp.float32)
    y = xf * lax.rsqrt(jnp.mean(xf * xf, axis=-1, keepdims=True) + EPS)
    return (y * g.astype(jnp.float32)).astype(x.dtype)

def causal_dwconv(x, w):
    S = x.shape[1]
    xp = jnp.pad(x, ((0, 0), (CONV_W - 1, 0), (0, 0)))
    y = xp[:, 0:S] * w[0]
    for j in range(1, CONV_W):
        y = y + xp[:, j:j + S] * w[j]
    return y

def mlstm_chunkwise(q, k, v, log_i, log_f):
    f32 = jnp.float32
    B, S, H, Dk = q.shape
    Dv = v.shape[-1]
    L = M_CHUNK
    NC = S // L

    def to_chunks(a):
        return a.reshape((B, NC, L) + a.shape[2:]).swapaxes(0, 1)

    qc = to_chunks(q.astype(f32))
    kc = to_chunks(k.astype(f32) * (Dk ** -0.5))
    vc = to_chunks(v.astype(f32))
    ic = to_chunks(log_i.astype(f32))
    fc = to_chunks(log_f.astype(f32))
    causal = jnp.tril(jnp.ones((L, L), dtype=bool))

    def step(carry, inp):
        C, n, m = carry
        q_, k_, v_, li, lf = inp
        b = jnp.cumsum(lf, axis=1).transpose(0, 2, 1)
        li_h = li.transpose(0, 2, 1)
        D = b[:, :, :, None] - b[:, :, None, :] + li_h[:, :, None, :]
        D = jnp.where(causal, D, -jnp.inf)
        inter = b + m[:, :, None]
        m_t = jnp.maximum(inter, D.max(-1))
        s = jnp.einsum('blhd,bshd->bhls', q_, k_) * jnp.exp(D - m_t[..., None])
        w_inter = jnp.exp(inter - m_t)
        num = (jnp.einsum('bhls,bshv->blhv', s, v_)
               + w_inter.transpose(0, 2, 1)[..., None] * jnp.einsum('blhd,bhdv->blhv', q_, C))
        den = s.sum(-1) + w_inter * jnp.einsum('blhd,bhd->bhl', q_, n)
        den = jnp.maximum(jnp.abs(den), jnp.exp(-m_t))
        h = num / den.transpose(0, 2, 1)[..., None]
        b_L = b[:, :, -1]
        g = b_L[:, :, None] - b + li_h
        m_new = jnp.maximum(b_L + m, g.max(-1))
        wk = jnp.exp(g - m_new[..., None])
        decay = jnp.exp(b_L + m - m_new)
        C_new = decay[..., None, None] * C + jnp.einsum('bhs,bshd,bshv->bhdv', wk, k_, v_)
        n_new = decay[..., None] * n + jnp.einsum('bhs,bshd->bhd', wk, k_)
        return (C_new, n_new, m_new), h

    init = (jnp.zeros((B, H, Dk, Dv), f32), jnp.zeros((B, H, Dk), f32), jnp.zeros((B, H), f32))
    _, hs = lax.scan(step, init, (qc, kc, vc, ic, fc))
    return hs.swapaxes(0, 1).reshape(B, S, H, Dv)

def t5_bucket(dist):
    max_exact = REL_BUCKETS // 2
    large = max_exact + (jnp.log(jnp.maximum(dist, 1).astype(jnp.float32) / max_exact)
                         / math.log(REL_MAX_DIST / max_exact) * (REL_BUCKETS - max_exact)).astype(jnp.int32)
    large = jnp.minimum(large, REL_BUCKETS - 1)
    return jnp.where(dist < max_exact, dist, large)

def dsa_attention(q, k, v, iq, ik, iw, rel_bias):
    B, S, H, dh = q.shape
    topk = min(TOPK_MAX, S // 4)
    NB = S // Q_BLOCK
    key_pos = jnp.arange(S)
    iq = iq * (IDX_DH ** -0.5)
    iw = iw * (IDX_HEADS ** -0.5)

    def blockify(a):
        return a.reshape((B, NB, Q_BLOCK) + a.shape[2:]).swapaxes(0, 1)

    def one_block(args):
        qb, iqb, iwb, bi = args
        t = bi * Q_BLOCK + jnp.arange(Q_BLOCK)
        sc = jax.nn.relu(jnp.einsum('bthd,bsd->bths', iqb, ik))
        score = jnp.einsum('bths,bth->bts', sc, iwb).astype(jnp.float32)
        causal = key_pos[None, :] <= t[:, None]
        score = jnp.where(causal[None], score, -jnp.inf)
        _, idx = lax.top_k(score, topk)
        k_sel = jax.vmap(lambda kb, ib: kb[ib])(k, idx)
        v_sel = jax.vmap(lambda vb, ib: vb[ib])(v, idx)
        valid = idx <= t[None, :, None]
        bucket = t5_bucket(jnp.maximum(t[None, :, None] - idx, 0))
        bias = rel_bias[bucket].astype(jnp.float32).transpose(0, 1, 3, 2)
        logits = jnp.einsum('bthd,btkhd->bthk', qb, k_sel).astype(jnp.float32) * (dh ** -0.5) + bias
        logits = jnp.where(valid[:, :, None, :], logits, -jnp.inf)
        probs = jax.nn.softmax(logits, axis=-1).astype(v.dtype)
        return jnp.einsum('bthk,btkhd->bthd', probs, v_sel)

    out = lax.map(one_block, (blockify(q), blockify(iq), blockify(iw), jnp.arange(NB)))
    return out.swapaxes(0, 1).reshape(B, S, H, dh)

def second_inputs(seed: int = 0) -> dict:
    key = jax.random.key(seed)
    ks = jax.random.split(key, 16)
    f32 = jnp.float32
    x = jax.random.normal(ks[0], (BATCH, SEQ, D_MODEL), f32)
    p = jax.random.normal(ks[1], (DEPTH_2, BATCH, SEQ, D_PLE), f32)
    w_in = jax.random.normal(ks[2], (DEPTH_2, D_MODEL, PROJ_TOTAL), f32) * D_MODEL ** -0.5
    i_bias = 0.1 * jax.random.normal(ks[3], (DEPTH_2, M_HEADS), f32)
    f_bias = jnp.linspace(3.0, 6.0, M_HEADS, dtype=f32)[None] + 0.1 * jax.random.normal(ks[4], (DEPTH_2, M_HEADS), f32)
    b_gate = jnp.concatenate([i_bias, f_bias], axis=-1)
    conv_w = jax.random.normal(ks[5], (DEPTH_2, CONV_W, 2 * M_HEADS * M_QK), f32) * CONV_W ** -0.5
    w_out = jax.random.normal(ks[6], (DEPTH_2, D_MIX, D_MODEL), f32) * D_MIX ** -0.5
    norm_in = 1.0 + 0.1 * jax.random.normal(ks[7], (DEPTH_2, D_MODEL), f32)
    m_norm = 1.0 + 0.1 * jax.random.normal(ks[8], (DEPTH_2, M_WIDTH), f32)
    rel_bias = 0.5 * jax.random.normal(ks[9], (REL_BUCKETS, A_HEADS), f32)
    w_ple = jax.random.normal(ks[10], (DEPTH_2, D_PLE, D_MODEL), f32) * D_PLE ** -0.5
    w_ple_gate = jax.random.normal(ks[11], (DEPTH_2, D_MODEL, D_MODEL), f32) * D_MODEL ** -0.5
    norm_final = 1.0 + 0.1 * jax.random.normal(ks[12], (D_MODEL,), f32)
    return {"x": x, "p": p, "w_in": w_in, "b_gate": b_gate, "conv_w": conv_w, "w_out": w_out,
            "norm_in": norm_in, "m_norm": m_norm, "rel_bias": rel_bias, "w_ple": w_ple,
            "w_ple_gate": w_ple_gate, "norm_final": norm_final}

def second_block(x, p, w_in, b_gate, conv_w, w_out, norm_in, m_norm, rel_bias, w_ple, w_ple_gate, norm_final):
    B, S, _ = x.shape
    h = x
    for i in range(DEPTH_2):
        u = rmsnorm(h, norm_in[i])
        proj = u @ w_in[i]
        (m_q, m_k, m_v, m_o, m_z, m_if, a_q, a_k, a_v, a_z,
         ix_q, ix_k, ix_w) = jnp.split(proj, SPLIT_POINTS, axis=-1)

        qk = jax.nn.silu(causal_dwconv(jnp.concatenate([m_q, m_k], axis=-1), conv_w[i]))
        mq, mk = jnp.split(qk, 2, axis=-1)
        gates = (m_if + b_gate[i]).astype(jnp.float32)
        log_i = gates[..., :M_HEADS]
        log_f = jax.nn.log_sigmoid(gates[..., M_HEADS:])
        hm = mlstm_chunkwise(mq.reshape(B, S, M_HEADS, M_QK), mk.reshape(B, S, M_HEADS, M_QK),
                             m_v.reshape(B, S, M_HEADS, M_V), log_i, log_f)
        hm = hm * lax.rsqrt(jnp.mean(hm * hm, axis=-1, keepdims=True) + EPS)
        hm = hm.reshape(B, S, M_WIDTH) * m_norm[i].astype(jnp.float32)
        hm = jax.nn.sigmoid(m_o) * hm.astype(x.dtype) * jax.nn.silu(m_z)

        ha = dsa_attention(a_q.reshape(B, S, A_HEADS, A_DH), a_k.reshape(B, S, A_HEADS, A_DH),
                           a_v.reshape(B, S, A_HEADS, A_DH), ix_q.reshape(B, S, IDX_HEADS, IDX_DH),
                           ix_k, ix_w, rel_bias)
        ha = ha.reshape(B, S, A_WIDTH) * jax.nn.silu(a_z)

        h = h + jnp.concatenate([hm, ha], axis=-1) @ w_out[i]

        h = h + (p[i] @ w_ple[i]) * jax.nn.sigmoid(h @ w_ple_gate[i])
    return rmsnorm(h, norm_final)


def setup_inputs(seed=0):
    out = dict(first_inputs(seed))
    for name, value in second_inputs(seed + 1).items():
        if name != "x":
            out[name + "_2"] = value
    return out


def reference(
    x, c, ada_w, ada_b, pre_mix_g, post_mix_g, pre_ffn_g, post_ffn_g, ffn_w_gu, ffn_w_down,
    a_w_in, a_b_in, a_ln_g, a_ln_b, a_w_s, a_b_s, a_w_out, kv_ada_w, kv_ada_b, kv_norm_g, kv_w,
    kv_b_f, k_norm_g, b_w_qg, b_q_norm_g, b_w_o, p_2, w_in_2, b_gate_2, conv_w_2, w_out_2,
    norm_in_2, m_norm_2, rel_bias_2, w_ple_2, w_ple_gate_2, norm_final_2,
):
    x = first_block(
        x, c, ada_w, ada_b, pre_mix_g, post_mix_g, pre_ffn_g, post_ffn_g, ffn_w_gu, ffn_w_down,
        a_w_in, a_b_in, a_ln_g, a_ln_b, a_w_s, a_b_s, a_w_out, kv_ada_w, kv_ada_b, kv_norm_g,
        kv_w, kv_b_f, k_norm_g, b_w_qg, b_q_norm_g, b_w_o,
    )
    return second_block(
        x, p_2, w_in_2, b_gate_2, conv_w_2, w_out_2, norm_in_2, m_norm_2, rel_bias_2, w_ple_2,
        w_ple_gate_2, norm_final_2,
    )


_drawn_inputs = setup_inputs


def setup_inputs(seed=0):
    import zlib

    import numpy as np

    out = dict(_drawn_inputs(seed))
    spreads = {}
    factors = {'pre_mix_g': 2.991,
     'post_ffn_g': 2.735,
     'a_b_in': 8.0,
     'a_ln_g': 8.0,
     'a_ln_b': 48.082,
     'kv_ada_b': 7.92,
     'kv_norm_g': 3.852,
     'k_norm_g': 8.0,
     'b_q_norm_g': 6.575,
     'rel_bias_2': 3.218,
     'm_norm_2': 3.551}
    for name, (base, spread) in spreads.items():
        noise = np.random.default_rng([zlib.crc32(name.encode()), seed]).standard_normal(out[name].shape)
        drawn = base * np.exp(spread * noise) if base else spread * noise
        out[name] = __import__('jax').numpy.asarray(drawn.astype(out[name].dtype))
    for name, factor in factors.items():
        out[name] = (out[name] * factor).astype(out[name].dtype)
    return out
```

```python
from contextlib import ExitStack

import numpy as np

import concourse.bass as bass
from concourse import mybir
from concourse.alu_op_type import AluOpType as ALU

F32 = mybir.dt.float32
F32R = mybir.dt.float32r
ACT = mybir.ActivationFunctionType
ds = bass.ds

P = 128
T = 512
NB = T // P
D = 1024
DC = D // P
GW = 2 * D
GC = GW // P
F = 2816
FC = F // P
NH, DH = 16, 64
MH, MQK, MV = 4, 128, 256
AH = 8
IH = 8
TOPK = 128
DPLE = 256
EPS = 1e-6
NEG = -1e30
TAKEN = -3e38
COLS = 256
KU = 4
RING = 4
REL_BUCKETS, REL_MAX_DIST = 32, 128
UROW = 640

O_MQ, O_MV, O_MO, O_MZ = 0, 1024, 2048, 3072
O_IF, O_AQ, O_AV, O_AZ, O_IXQ, O_IXK, O_IXW = 4096, 4104, 5128, 5640, 6152, 6664, 6728


def distance_buckets():
    dist = np.maximum(T - 1 - np.arange(UROW), 0)
    exact = REL_BUCKETS // 2
    ratio = np.maximum(dist, 1).astype(np.float32) / np.float32(exact)
    scale = np.float32(np.log(REL_MAX_DIST / exact))
    large = exact + (np.log(ratio) / scale * np.float32(REL_BUCKETS - exact)).astype(np.int32)
    bucket = np.where(dist < exact, dist, np.minimum(large, REL_BUCKETS - 1))
    return (bucket[None, :] == np.arange(REL_BUCKETS)[:, None]).astype(np.float32)


class Stage:

    def __init__(self, name, iters, kchunks, reader, token_major=False, second=None):
        self.name, self.iters, self.reader, self.token_major = name, iters, reader, token_major
        def units(k):
            return [(a, min(KU, k - a)) for a in range(0, k, KU)]
        self.units = [units(kchunks), units(second or kchunks)]
        self.kchunks = [kchunks, second or kchunks]
        self.per_body = len(self.units[0]) + len(self.units[1])
        self.groups = 2 * iters


STAGES = [
    Stage("mlp_u", 4, DC, "act"), Stage("mlp_v", 4, DC, "dve", True), Stage("mlp_out", 2, GC, "act"),
    Stage("gu0", 11, DC, "dve"), Stage("down0", 2, FC, "act"),
    Stage("k", 2, DC, "act"), Stage("v", 2, DC, "act", True), Stage("q", 2, DC, "act"),
    Stage("gate", 2, DC, "act"), Stage("fox_out", 2, DC, "act"),
    Stage("gu1", 11, DC, "dve"), Stage("down1", 2, FC, "act"),
    Stage("ixq", 1, DC, "act"), Stage("mqk", 2, DC, "act"), Stage("mv", 2, DC, "act", True),
    Stage("aqk", 2, DC, "act"), Stage("av", 1, DC, "act", True),
    Stage("mo", 2, DC, "act"), Stage("mz", 2, DC, "act"), Stage("az", 1, DC, "act"),
    Stage("mix_out", 2, 12, "dve"), Stage("ple", 4, DC, "dve", second=DPLE // P),
]


def number_stages():
    unit = group = 0
    count = {"act": 0, "dve": 0}
    for s in STAGES:
        s.unit0, s.group0, s.read0 = unit, group, count[s.reader]
        unit += s.per_body * s.iters
        group += s.groups
        count[s.reader] += s.groups
        assert unit % RING == 0 and group % 2 == 0
    return {s.name: s for s in STAGES}


def build_program(nc, io):
    S = number_stages()
    ctx = ExitStack()
    with ctx:
        def sem(name):
            return ctx.enter_context(nc.semaphore(name))

        base = 16512
        cursor = [base]

        def place(name, shape, dt=F32, at=None):
            size = int(np.prod(shape[1:])) * 4
            if at is None:
                at = cursor[0]
                cursor[0] += (size + 31) // 32 * 32
            return nc.alloc_sbuf_tensor_at(name, shape, dt, offset=at)

        K = 1024
        ring_at = cursor[0]
        raw = place("raw", [P, RING, KU, COLS])
        w_lo = place("w_lo", [P, RING, KU, COLS], F32R, at=ring_at)
        w_hi = place("w_hi", [P, RING, KU, COLS], F32R)
        xT = place("xT", [P, DC, T])
        h_at = cursor[0]
        hh = place("hh", [P, DC, T], F32R)
        hl = place("hl", [P, DC, T], F32R)
        y_h = place("y_h", [P, DC, T], at=h_at)
        ident = place("ident", [P, P])
        tri = place("tri", [P, P])
        tri_t = place("tri_t", [P, P])
        ones = place("ones", [P, P])
        head_ones = place("head_ones", [P, P])
        par_a = place("par_a", [P, 112])
        par_b = place("par_b", [P, 112])
        par_c = place("par_c", [P, 80])
        mod = place("mod", [P, 112])
        scol = place("scol", [P, 8])
        bcol = place("bcol", [P, 8])
        c_act = place("c_act", [P, 8])
        eps = place("eps", [P, 1])
        qgain = place("qgain", [P, 1])
        small = place("small", [P, 64])
        stats = place("stats", [P, NB, 8, 6])
        moments = place("moments", [P, NB, 2])
        sq = place("sq", [P, 2, T])
        sq_sum = place("sq_sum", [P, T])
        rstd = place("rstd", [P, T])
        tmp = place("tmp", [P, 4, T])
        ada_acc = place("ada_acc", [P, 2, COLS])
        iw = place("iw", [P, NB, IH])
        mt = place("mt", [P, 2, NB, MH])
        kvbf = place("kvbf", [16, 1])
        bgate = place("bgate", [MH, 2])
        rel = place("rel", [REL_BUCKETS, AH])
        best = place("best", [P, 8])
        spacer = place("spacer", [P, 8])
        negmax = place("negmax", [P, 2, NB])
        rowsum = place("rowsum", [P, 2, NB])
        rowinv = place("rowinv", [P, 2, NB])
        sel = place("sel", [MH, MH, P])
        ph = cursor[0]
        room = 229344 - ph
        assert room >= 102 * K, room

        ada_raw = place("ada_raw", [P, 2, KU, COLS], at=ph + 88 * K)
        u = place("u", [P, GC, T], at=ph)
        y_hi = place("y_hi", [P, GC, T], F32R, at=ph)
        y_lo = place("y_lo", [P, GC, T], F32R, at=h_at)
        v = place("v", [P, NB, GW], at=ph + 32 * K)
        x_in = place("x_in", [P, NB, D], at=ph + 32 * K)
        ws_raw = place("ws_raw", [P, 16, P], at=ph + 48 * K)
        y_mlp = place("y_mlp", [P, DC, T], at=ph + 32 * K)
        ws_t = place("ws_t", [P, 16, P], at=ph + 64 * K)
        b_in = place("b_in", [P, GW], at=ph + 72 * K)
        q_bias = place("q_bias", [P, 16, P], at=ph + 72 * K)
        rows = place("rows", [P, 3, P], at=ph + 80 * K)
        act_hi = place("act_hi", [P, FC, T], F32R, at=ph)
        act_lo = place("act_lo", [P, FC, T], F32R, at=ph + 44 * K)
        k_fox = place("k_fox", [P, DC, T], at=ph)
        q_fox = place("q_fox", [P, DC, T], at=ph + 16 * K)
        v_fox = place("v_fox", [P, NB, D], at=ph + 32 * K)
        gate = place("gate", [P, DC, T], at=ph + 48 * K)
        fx = {
            "rb": place("fox_rb", [P, 2, T], at=ph + 64 * K), "mb": place("fox_mb", [P, 2, 1280], at=ph + 68 * K),
            "mask": place("fox_mask", [P, 1280], at=ph + 78 * K),
            "qs": place("fox_qs", [P, T], at=ph + 94 * K), "ks": place("fox_ks", [P, T], at=ph + 96 * K),
            "o": place("fox_o", [P, NB, D], at=h_at),
            "p": place("fox_p", [P, 2, 1280], at=h_at + 16 * K), "pT": place("fox_pT", [P, 1280], at=h_at + 26 * K),
        }
        gl_f = place("gl_f", [16, 5, T], at=ph + 83 * K)
        wf_raw = place("wf_raw", [P, DC, P], at=ph + 98 * K)
        wf_lo = place("wf_lo", [P, DC, P], F32R, at=ph + 98 * K)
        wf_hi = place("wf_hi", [P, DC, P], F32R, at=ph + 94 * K)
        og_hi = place("og_hi", [P, DC, T], F32R, at=ph)
        og_lo = place("og_lo", [P, DC, T], F32R, at=ph + 16 * K)
        y_fox = place("y_fox", [P, DC, T], at=ph + 32 * K)
        mq = place("mq", [P, MH, T], at=ph)
        mk = place("mk", [P, MH, T], at=ph + 8 * K)
        mv = place("mv", [P, NB, MH * MV], at=ph + 16 * K)
        ogate = place("ogate", [P, DC, T], at=ph + 34 * K)
        ixq = place("ixq", [P, 4, T], at=ph + 34 * K)
        ixk = place("ixk", [P, T], at=ph + 42 * K)
        aq = place("aq", [P, 4, T], at=ph + 50 * K)
        ak = place("ak", [P, 4, T], at=ph + 58 * K)
        av = place("av", [P, NB, AH * 64], at=ph + 66 * K)
        az = place("az", [P, 4, T], at=ph + 74 * K)
        dmask = place("dmask", [P, 1280], at=ph + 82 * K)
        score = place("score", [P, 1152], at=ph + 87 * K)
        p_in = place("p_in", [P, NB, DPLE], at=ph + 92 * K)
        XW = 264
        xw_raw = place("xw_raw", [P, DC, XW], at=ph)
        xw_lo = place("xw_lo", [P, DC, XW], F32R, at=ph)
        xw_hi = place("xw_hi", [P, DC, XW], F32R, at=ph + 87 * K)
        xpad = place("xpad", [P, 2, 516], at=ph + 87 * K + 4608)
        mks = place("mks", [P, T], at=h_at)
        sel_h = place("sel_h", [MH, P], at=h_at + 2 * K)
        m_e = place("m_e", [P, 1280], at=h_at + 3 * K)
        m_s = place("m_s", [P, 1280], at=h_at + 8 * K)
        hm = place("hm", [P, NB, MH * MV], at=h_at + 16 * K)
        dx = {
            "rb": place("dsa_rb", [P, 2, T], at=ph), "mb": place("dsa_mb", [P, 2, 1280], at=ph + 4 * K),
            "p": place("dsa_p", [P, 2, 1280], at=ph + 16 * K), "pT": place("dsa_pT", [P, 1280], at=ph + 26 * K),
            "qs": place("dsa_qs", [P, T], at=h_at), "ks": place("dsa_ks", [P, T], at=h_at + 2 * K),
            "o": place("dsa_o", [P, NB, AH * 64], at=h_at + 8 * K), "mask": dmask,
        }
        mix_hi = place("mix_hi", [P, 12, T], F32R, at=ph)
        mix_lo = place("mix_lo", [P, 12, T], F32R, at=ph + 50 * K)
        pt_hi = place("pt_hi", [P, 2, T], F32R, at=ph + 24 * K)
        pt_lo = place("pt_lo", [P, 2, T], F32R, at=ph + 28 * K)
        x_norm = place("x_norm", [P, DC, T], at=ph)
        x_out = place("x_out", [P, NB, D], at=ph + 16 * K)
        row_u = place("row_u", [AH, UROW], at=ph + 92 * K)
        one_hot = place("one_hot", [REL_BUCKETS, UROW], at=ph + 44 * K)

        acc = ctx.enter_context(nc.psum_tensor("acc", [P, 2, 2, T], F32))
        ms = ctx.enter_context(nc.psum_tensor("ms", [P, T], F32))
        ada_ps = ctx.enter_context(nc.psum_tensor("ada_ps", [P, T], F32))
        aux = ctx.enter_context(nc.psum_tensor("aux", [P, 2, T], F32))

        landed = [sem(f"w_landed{s}") for s in range(RING)]
        w_split_hi = sem("w_split_hi")
        w_split = sem("w_split")
        w_used = sem("w_used")
        acc_done = sem("acc_done")
        acc_read = {"act": sem("acc_read_act"), "dve": sem("acc_read_dve")}
        ada_landed = [sem("ada_landed0"), sem("ada_landed1")]
        par_in, x_landed, ws_in, b_in_in, q_bias_in, gates_in = (sem(n) for n in (
            "par_in", "x_landed", "ws_in", "b_in_in", "q_bias_in", "gates_in"))
        wf_in, fox_nd_out, xw_in, one_hot_in, rel_u_out, p_landed = (sem(n) for n in (
            "wf_in", "fox_nd_out", "xw_in", "one_hot_in", "rel_u_out", "p_landed"))
        stored, consts, par_t, par_ok, c_ok, xt_ps = (sem(n) for n in (
            "stored", "consts", "par_t", "par_ok", "c_ok", "xt_ps"))
        x_ready, ada_used, ada_ready, ada_sum, ada_col, sq_ready = (sem(n) for n in (
            "x_ready", "ada_used", "ada_ready", "ada_sum", "ada_col", "sq_ready"))
        sq_added, ms_ready, std_ready, t_ready, h_hi, h_ready = (sem(n) for n in (
            "sq_added", "ms_ready", "std_ready", "t_ready", "h_hi", "h_ready"))
        sg_ready, a_hi, act_ready, ws_masked, wst_ps, wst_ready = (sem(n) for n in (
            "sg_ready", "a_hi", "act_ready", "ws_masked", "wst_ps", "wst_ready"))
        v_added, v_gelu, ln_moments, ln_std, v_norm, r_ps = (sem(n) for n in (
            "v_added", "v_gelu", "ln_moments", "ln_std", "v_norm", "r_ps"))
        r_read, mix_ps, mix_read, hsq_ready, hs_ps, hstd = (sem(n) for n in (
            "r_read", "mix_ps", "mix_read", "hsq_ready", "hs_ps", "hstd"))
        kq_ready, wf_zero, wf_split_hi, wf_split, f_ps, f_read = (sem(n) for n in (
            "kq_ready", "wf_zero", "wf_split_hi", "wf_split", "f_ps", "f_read"))
        ls_abs, ls_log, fox_d_ready, og_ps, xw_zero, xw_split_hi = (sem(n) for n in (
            "ls_abs", "ls_log", "fox_d_ready", "og_ps", "xw_zero", "xw_split_hi"))
        xw_split, xw_ps, xw_read, ix_ps, ix_relu, ix_added = (sem(n) for n in (
            "xw_split", "xw_ps", "xw_read", "ix_ps", "ix_relu", "ix_added"))
        ix_done, xpad_zero, xpad_ready, conv_ready, conv_used, u_ps = (sem(n) for n in (
            "ix_done", "xpad_zero", "xpad_ready", "conv_ready", "conv_used", "u_ps"))
        row_u_ready, dmask_ready, mz_ready, ogate_ready, fg_ready, em_ready = (sem(n) for n in (
            "row_u_ready", "dmask_ready", "mz_ready", "ogate_ready", "fg_ready", "em_ready"))
        mt_ps, mt_ready, m_staged, gb_ps, gb_ready, qk_ps = (sem(n) for n in (
            "mt_ps", "mt_ready", "m_staged", "gb_ps", "gb_ready", "qk_ps"))
        m_e_ready, m_s_ready, num_ps, r_ready, hm_std, hm_ready = (sem(n) for n in (
            "m_e_ready", "m_s_ready", "num_ps", "r_ready", "hm_std", "hm_ready"))
        mix_t, p_t, xn_ready, ot_ps, out_ready = (sem(n) for n in (
            "mix_t", "p_t", "xn_ready", "ot_ps", "out_ready"))
        for kind, a in (("fox", fx), ("dsa", dx)):
            a["rb_in"] = [sem(f"{kind}_rb_in{e}") for e in range(2)]
            for n in ("mb_ready", "staged", "s_ps", "lg_ready", "e_ready", "t_ps", "pt_act", "pt_dve", "o_ps", "o_read"):
                a[n] = sem(f"{kind}_{n}")
        fx.update(q=q_fox, k=k_fox, v=v_fox, pairs=NH // 2, toeplitz=False)
        dx.update(q=aq, k=ak, v=av, pairs=AH // 2, toeplitz=True)

        block = ctx.enter_context(nc.Block())

        def times(eng, n, body, unroll=False):
            if n <= 1 or unroll:
                for i in range(n):
                    body(i)
            else:
                with eng.Fori(0, n) as i:
                    body(i)

        def unit_no(st, i, j, x):
            return st.unit0 + i * st.per_body + (len(st.units[0]) if j else 0) + x

        def slot_of(st, i, j, x):
            n = unit_no(st, i if isinstance(i, int) else 0, j, x)
            return n % RING

        def load_unit(sp, st, src, i, j, x):
            n, s, (k0, nk) = unit_no(st, i, j, x), slot_of(st, i, j, x), st.units[j][x]
            sp.wait_ge(w_used, n + 1)
            for dst, ap in src(i, j, k0, nk, raw[:, s, 0:nk, :]):
                sp.dma_start(dst, ap).then_inc(landed[s], 16)

        def columns(w, c0, step):
            def src(i, j, k0, nk, dst):
                c = c0 + step * 2 * i + step * j
                return [(dst, w[k0 * P:(k0 + nk) * P, ds(c, COLS)].rearrange("(k p) n -> p k n", p=P))]
            return src
        src_of = {}

        def gu_src(w):
            wv = w.rearrange("(k p) (a f) -> p k a f", p=P, a=2)
            def src(i, j, k0, nk, dst):
                f0 = 256 * i + 128 * j
                return [(dst.rearrange("p k (a f) -> p k a f", a=2)[:, :, a, :], wv[:, k0:k0 + nk, a, ds(f0, P)])
                        for a in range(2)]
            return src
        a_w_in, w2 = io["a_w_in"][0], io["w_in_2"][0]
        src_of["mlp_u"], src_of["mlp_v"] = columns(a_w_in, 0, COLS), columns(a_w_in, GW, COLS)
        src_of["mlp_out"] = columns(io["a_w_out"][0], 0, COLS)
        for l in range(2):
            src_of[f"gu{l}"] = gu_src(io["ffn_w_gu"][l])
            src_of[f"down{l}"] = columns(io["ffn_w_down"][l], 0, COLS)
        src_of["k"], src_of["v"] = columns(io["kv_w"], 0, COLS), columns(io["kv_w"], D, COLS)
        src_of["q"], src_of["gate"] = columns(io["b_w_qg"][0], 0, COLS), columns(io["b_w_qg"][0], D, COLS)
        src_of["fox_out"] = columns(io["b_w_o"][0], 0, COLS)
        for name, c0 in (("ixq", O_IXQ), ("mqk", O_MQ), ("mv", O_MV), ("aqk", O_AQ), ("av", O_AV), ("mo", O_MO),
                         ("mz", O_MZ), ("az", O_AZ)):
            src_of[name] = columns(w2, c0, COLS)
        src_of["mix_out"] = columns(io["w_out_2"][0], 0, COLS)

        def ple_src(i, j, k0, nk, dst):
            w = io["w_ple"][0] if j else io["w_ple_gate"][0]
            return [(dst, w[k0 * P:(k0 + nk) * P, ds(256 * i, COLS)].rearrange("(k p) n -> p k n", p=P))]
        src_of["ple"] = ple_src
        for st in STAGES:
            st.dmas = 2 if st.name.startswith("gu") else 1
        total = 0
        for st in STAGES:
            st.landed0 = total
            total += 16 * st.dmas * st.per_body * st.iters // RING

        def landed_value(st, i, j, x):
            at = (len(st.units[0]) if j else 0) + x
            if isinstance(i, int):
                rounds = (i * st.per_body + at) // RING
            else:
                rounds = i * (st.per_body // RING) + at // RING
            return (rounds + 1) * (16 * st.dmas) + st.landed0

        ada_w, kv_ada_w = io["ada_w"], io["kv_ada_w"]

        def ada_load(sp, w, c0, step):
            for half in range(2):
                sp.wait_ge(ada_used, 2 * step + half + 1)
                sp.dma_start(ada_raw[:, half], w[half * 512:half * 512 + 512, ds(c0, COLS)].rearrange("(k p) n -> p k n", p=P)) \
                    .then_inc(ada_landed[half], 16)

        def load_group(sp, name, i, j):
            st = S[name]
            for x in range(len(st.units[j])):
                load_unit(sp, st, src_of[name], i, j, x)

        def load_stage(sp, name, ada=None, unroll=False, skip=0):
            st = S[name]
            def body(i):
                for j in range(2):
                    if skip and 2 * i + j < skip:
                        continue
                    load_group(sp, name, i, j)
                    if ada:
                        ada(i, j)
            times(sp, st.iters, body, unroll or skip > 0 or st.per_body % RING != 0)

        CH = {"h0": 0, "y": 8, "h1": 24, "hkv": 32, "h2": 40, "og": 48, "h3": 56, "h4": 64, "mix": 72, "xg": 84, "pt": 92}

        def done(st, i, j):
            return unit_no(st, i, j, len(st.units[j]) - 1) + 1 + RING

        def bank(b):
            return acc[:, b // 2, b % 2, :]

        WIDTH = [P * (b + 1) for b in range(NB)]
        OFF = [sum(WIDTH[:b]) for b in range(NB)]
        TW = [P * (NB - s) for s in range(NB)]
        TOFF = [sum(TW[:s]) for s in range(NB)]

        def attention_sp(sp, a, source):
            def body(i):
                for e in range(2):
                    sp.wait_ge(a["mb_ready"], 2 * i + e + 1)
                    sp.dma_start(a["rb"][:, e, :], source(2 * i + e)).then_inc(a["rb_in"][e], 16)
            times(sp, a["pairs"], body, unroll=a["toeplitz"])

        def attention_pool(pool, a):
            pool.nop().then_inc(a["mb_ready"], 2)
            def body(i):
                for e in range(2):
                    h = 2 * i + e
                    pool.wait_ge(a["rb_in"][e], 16 * (i + 1))
                    pool.wait_ge(a["lg_ready"], 4 * h + 4)
                    for b in range(NB):
                        lo = (NB - 1 - b) * P if a["toeplitz"] else 0
                        last = pool.tensor_tensor(a["mb"][:, e, OFF[b]:OFF[b] + WIDTH[b]], a["rb"][:, e, lo:lo + WIDTH[b]],
                                                  a["mask"][:, OFF[b]:OFF[b] + WIDTH[b]], ALU.add)
                    last.then_inc(a["mb_ready"], 1)
            times(pool, a["pairs"], body)

        def attention_act(act, a):
            def stage(i):
                act.wait_ge(a["s_ps"], 8 * i + 1)
                act.activation(a["qs"][:], a["q"][:, ds(i, 1), :].rearrange("p a t -> p (a t)"), ACT.Copy).then_inc(a["staged"], 1)
                act.activation(a["ks"][:], a["k"][:, ds(i, 1), :].rearrange("p a t -> p (a t)"), ACT.Copy).then_inc(a["staged"], 1)

            def exps(i, e):
                h = 2 * i + e
                act.wait_ge(a["o_read"], h + 1)
                for b in range(NB):
                    act.wait_ge(a["lg_ready"], 4 * h + b + 9)
                    part = a["p"][:, e, OFF[b]:OFF[b] + WIDTH[b]]
                    act.activation(part, part, ACT.Exp, bias=negmax[:, e, b:b + 1], scale=-1.0,
                                   accum_out=rowsum[:, e, b:b + 1]).then_inc(a["e_ready"], 1)

            def copies(i, e):
                h = 2 * i + e
                act.wait_ge(a["o_ps"], h + 1)
                for s in (1, 3):
                    act.wait_ge(a["t_ps"], 4 * h + s + 9)
                    act.activation(a["pT"][:, TOFF[s]:TOFF[s] + TW[s]], aux[:, 1, 0:TW[s]], ACT.Copy).then_inc(a["pt_act"], 1)
            act.nop().then_inc(a["pt_act"], 1)
            stage(0)
            exps(0, 0)
            def body(i):
                exps(i, 1)
                stage(i + 1)
                copies(i, 0)
                exps(i + 1, 0)
                copies(i, 1)
            times(act, a["pairs"] - 1, body)
            n = a["pairs"] - 1
            exps(n, 1)
            copies(n, 0)
            copies(n, 1)

        def attention_pe(pe, a):
            pe.nop().then_inc(a["t_ps"], 8)
            pe.nop().then_inc(a["s_ps"], 1)
            pe.nop().then_inc(a["o_ps"], 1)
            def scores(i, e):
                h = 2 * i + e
                if e == 0:
                    pe.wait_ge(a["staged"], 2 * i + 2)
                rows64 = slice(64 * e, 64 * e + 64)
                for b in range(NB):
                    pe.wait_ge(a["lg_ready"], 4 * h + b + 5)
                    pe.matmul(bank(b)[:, 0:WIDTH[b]], a["qs"][rows64, b * P:(b + 1) * P], a["ks"][rows64, 0:WIDTH[b]],
                              start=True, stop=True).then_inc(a["s_ps"], 1)

            def tail(i, e):
                h = 2 * i + e
                pe.wait_ge(a["e_ready"], 4 * h + 4)
                for s in range(NB):
                    if s % 2:
                        pe.wait_ge(a["pt_act"], 2 * h + s // 2 + 1)
                    else:
                        pe.wait_ge(a["pt_dve"], 2 * h + s // 2 + 1)
                    for b in range(s, NB):
                        last = pe.transpose(aux[:, s % 2, (b - s) * P:(b - s + 1) * P],
                                            a["p"][:, e, OFF[b] + s * P:OFF[b] + (s + 1) * P], ident[:])
                    last.then_inc(a["t_ps"], 1)
                pe.wait_ge(a["pt_act"], 2 * h + 3)
                pe.wait_ge(a["pt_dve"], 2 * h + 3)
                pe.wait_ge(a["o_read"], h + 1)
                out = (ada_ps if e else ms)
                for b in range(NB):
                    for s in range(b + 1):
                        last = pe.matmul(out[:, b * 64:b * 64 + 64], a["pT"][:, TOFF[s] + (b - s) * P:TOFF[s] + (b - s + 1) * P],
                                         a["v"][:, s, ds(h * 64, 64)], start=s == 0, stop=s == b)
                last.then_inc(a["o_ps"], 1)
            scores(0, 0)
            def body(i):
                scores(i, 1)
                tail(i, 0)
                scores(i + 1, 0)
                tail(i, 1)
            times(pe, a["pairs"] - 1, body)
            n = a["pairs"] - 1
            scores(n, 1)
            tail(n, 0)
            tail(n, 1)

        def attention_dve(dve, a):
            dve.nop().then_inc(a["lg_ready"], 8)
            dve.nop().then_inc(a["pt_dve"], 1)
            dve.nop().then_inc(a["o_read"], 2)
            def soft(i, e):
                h = 2 * i + e
                dve.wait_ge(a["mb_ready"], h + 3)
                dve.wait_ge(a["t_ps"], 4 * h + 4)
                for b in range(NB):
                    dve.wait_ge(a["s_ps"], 4 * h + b + 2)
                    dve.memset(spacer[:, 4 * e + b:4 * e + b + 1], 0.0)
                    part = slice(OFF[b], OFF[b] + WIDTH[b])
                    dve.tensor_tensor_reduce(a["p"][:, e, part], bank(b)[:, 0:WIDTH[b]], a["mb"][:, e, part], -1.0, 3e38,
                                             ALU.add, ALU.min, negmax[:, e, b:b + 1]).then_inc(a["lg_ready"], 1)

            def copies(i, e):
                h = 2 * i + e
                dve.wait_ge(a["o_ps"], h + 1)
                for s in (0, 2):
                    dve.wait_ge(a["t_ps"], 4 * h + s + 9)
                    dve.tensor_copy(a["pT"][:, TOFF[s]:TOFF[s] + TW[s]], aux[:, 0, 0:TW[s]]).then_inc(a["pt_dve"], 1)

            def outputs(i, e):
                h = 2 * i + e
                dve.reciprocal(rowinv[:, e, :], rowsum[:, e, :])
                dve.drain()
                dve.wait_ge(a["o_ps"], h + 2)
                out = (ada_ps if e else ms)
                dve.tensor_tensor(a["o"][:, :, ds(h * 64, 64)], out[:, 0:NB * 64].rearrange("p (b d) -> p b d", b=NB),
                                  rowinv[:, e, :].unsqueeze(2).broadcast_to([P, NB, 64]), ALU.mult).then_inc(a["o_read"], 1)
            soft(0, 0)
            def body(i):
                soft(i, 1)
                copies(i, 0)
                outputs(i, 0)
                soft(i + 1, 0)
                copies(i, 1)
                outputs(i, 1)
            times(dve, a["pairs"] - 1, body)
            n = a["pairs"] - 1
            soft(n, 1)
            for e in range(2):
                copies(n, e)
                outputs(n, e)
        def lead(eng, name, split, epilogue, following, unroll=False):
            st = S[name]
            def body(i):
                split(eng, st, i, 1)
                epilogue(st, i, 0)
                split(eng, st, i + 1, 0)
                epilogue(st, i, 1)
            times(eng, st.iters - 1, body, unroll or st.per_body % RING != 0)
            split(eng, st, st.iters - 1, 1)
            epilogue(st, st.iters - 1, 0)
            if following:
                split(eng, S[following], 0, 0)
            epilogue(st, st.iters - 1, 1)

        def split_hi(act, st, i, j):
            for x, (_, nk) in enumerate(st.units[j]):
                s = slot_of(st, i, j, x)
                act.wait_ge(landed[s], landed_value(st, i, j, x))
                act.activation(w_hi[:, s, 0:nk, :], raw[:, s, 0:nk, :], ACT.Copy).then_inc(w_split_hi, 1)

        def split_lo(pool, st, i, j):
            for x, (_, nk) in enumerate(st.units[j]):
                s = slot_of(st, i, j, x)
                pool.wait_ge(w_split_hi, unit_no(st, i, j, x) + 1)
                pool.tensor_tensor(w_lo[:, s, 0:nk, :], raw[:, s, 0:nk, :], w_hi[:, s, 0:nk, :].bitcast(F32),
                                   ALU.subtract).then_inc(w_split, 1)

        def wait_sums(eng, st, i, j):
            eng.wait_ge(w_used, done(st, i, j))

        def sums(j):
            return acc[:, j]

        def sums_tok(j):
            return acc[:, j].rearrange("p a (b n) -> p (a b) n", b=2)

        @block.sync
        def _(sp):
            def rows128(a):
                return a.rearrange("(j p) -> j p", p=P)

            def par(dst, src, s=par_in):
                sp.dma_start(dst, src).then_inc(s, 16)

            for r, name in ((0, "pre_mix_g"), (16, "post_mix_g"), (32, "pre_ffn_g"), (48, "post_ffn_g")):
                par(rows[r:r + 16, 1, :], io[name].rearrange("l (j p) -> (l j) p", p=P))
            for r, a in ((64, io["kv_norm_g"]), (72, io["norm_in_2"][0]), (80, io["norm_final_2"]),
                         (88, io["a_b_in"][0, 0:GW]), (104, io["c"][0])):
                par(rows[r:r + a.shape[0] // P, 1, :], rows128(a))
            for r, a in ((0, io["ada_b"][0]), (48, io["kv_ada_b"]), (64, io["ada_b"][1])):
                par(rows[r:r + a.shape[0] // P, 0, :], rows128(a))
            par(rows[0:32, 2, :], io["conv_w_2"][0].rearrange("w (j p) -> (w j) p", p=P))
            for half in range(2):
                par(rows[32:33, 2, half * 64:half * 64 + 64], io["k_norm_g"].rearrange("(a d) -> a d", a=1))
                par(rows[33:34, 2, half * 64:half * 64 + 64], io["b_q_norm_g"])
            for r, a in ((34, io["a_ln_g"][0]), (50, io["a_ln_b"][0]), (66, io["m_norm_2"][0])):
                par(rows[r:r + a.shape[0] // P, 2, :], rows128(a))
            sp.dma_start(x_in[:], io["x"][0].rearrange("(b p) d -> p b d", p=P)).then_inc(x_landed, 16)
            for s in range(8):
                ada_load(sp, ada_w[0], COLS * s, s)
            sp.dma_start(ws_raw[:], io["a_w_s"][0].rearrange("g t s -> t g s")).then_inc(ws_in, 16)
            sp.dma_start(b_in[:], io["a_b_in"][0:1, GW:2 * GW].broadcast_to([P, GW])).then_inc(b_in_in, 16)
            par(kvbf[:], io["kv_b_f"].rearrange("(h a) -> h a", a=1), gates_in)
            for a in range(2):
                par(bgate[:, a:a + 1], io["b_gate_2"][0, a * MH:(a + 1) * MH].rearrange("(h a) -> h a", a=1), gates_in)
            par(rel[:], io["rel_bias_2"], gates_in)
            load_stage(sp, "mlp_u", lambda i, j: ada_load(sp, ada_w[0], COLS * (8 + 2 * i + j), 8 + 2 * i + j))
            load_stage(sp, "mlp_v", lambda i, j: ada_load(sp, ada_w[0], COLS * (16 + 2 * i + j), 16 + 2 * i + j))
            sp.wait_ge(v_added, 8)
            sp.dma_start(q_bias[:].rearrange("p g t -> p (g t)"),
                         io["a_b_s"][0].rearrange("g t -> (g t)").rearrange("(a n) -> a n", a=1).broadcast_to([P, GW])) \
                .then_inc(q_bias_in, 16)

            def two_kv(i, j):
                for a in range(2):
                    ada_load(sp, kv_ada_w, COLS * (4 * i + 2 * j + a), 24 + 4 * i + 2 * j + a)
            load_stage(sp, "mlp_out", two_kv)
            load_stage(sp, "gu0", lambda i, j: ada_load(sp, ada_w[1], COLS * (2 * i + j), 32 + 2 * i + j))
            load_stage(sp, "down0", lambda i, j: ada_load(sp, ada_w[1], COLS * (22 + j), 54 + j) if i == 0 else None, unroll=True)
            load_stage(sp, "k")
            sp.wait_ge(wf_zero, 1)
            sp.dma_start(wf_raw[:, :, 0:NH], io["kv_w"][:, 2 * D:2 * D + NH].rearrange("(k p) n -> p k n", p=P)).then_inc(wf_in, 16)
            for name in ("v", "q", "gate"):
                load_stage(sp, name)
            sp.wait_ge(fox_d_ready, 1)
            sp.dma_start(io["fox_nd"], gl_f[:, 4, :]).then_inc(fox_nd_out, 16)
            sp.wait_ge(fox_nd_out, 16)
            load_group(sp, "fox_out", 0, 0)
            attention_sp(sp, fx, lambda h: io["fox_nd"][ds(h, 1), :].broadcast_to([P, T]))
            load_stage(sp, "fox_out", skip=1)
            load_stage(sp, "gu1")
            load_stage(sp, "down1")
            load_group(sp, "ixq", 0, 0)
            sp.wait_ge(xw_zero, 1)
            for c, o, n in ((0, O_IXK, 64), (64, O_IXK, 64), (128, O_IF, MH), (160, O_IF + MH, MH), (256, O_IXW, IH)):
                sp.dma_start(xw_raw[:, :, c:c + n], w2[:, o:o + n].rearrange("(k p) n -> p k n", p=P)).then_inc(xw_in, 16)
            load_stage(sp, "ixq", skip=1)
            sp.dma_start(one_hot[:], io["one_hot"]).then_inc(one_hot_in, 16)
            for name in ("mqk", "mv", "aqk", "av"):
                load_stage(sp, name)
            sp.wait_ge(row_u_ready, 1)
            sp.dma_start(io["rel_u"], row_u[:].unsqueeze(1).broadcast_to([AH, P, UROW])).then_inc(rel_u_out, 16)
            for name in ("mo", "mz", "az"):
                load_stage(sp, name)
            sp.wait_ge(rel_u_out, 16)
            sp.dma_start(p_in[:], io["p_2"][0, 0].rearrange("(b p) d -> p b d", p=P)).then_inc(p_landed, 16)
            load_group(sp, "mix_out", 0, 0)
            sp.wait_ge(hm_ready, MH + 1)
            attention_sp(sp, dx, lambda h: bass.AP(io["rel_u"].tensor, h * P * UROW + P - 1, [[UROW - 1, P], [1, T]]))
            load_stage(sp, "mix_out", skip=1)
            load_stage(sp, "ple")
            sp.wait_ge(out_ready, NB)
            sp.dma_start(io["out"][0].rearrange("(b p) d -> p b d", p=P), x_out[:]).then_inc(stored, 16)
            sp.wait_ge(stored, 16)

        @block.scalar
        def _(act):
            act.nop().then_inc(acc_read["act"], 2)

            def square(ev, k, src):
                if 8 * ev + k >= 2:
                    act.wait_ge(sq_added, 8 * ev + k - 1)
                act.activation(sq[:, k % 2, :], src, ACT.Square).then_inc(sq_ready, 1)

            def squares_of_x(ev, x0):
                for k in range(DC):
                    act.wait_ge(x_ready, x0 + k + 1)
                    square(ev, k, xT[:, k, :])

            def deviation(ev):
                act.wait_ge(ms_ready, ev + 1)
                act.activation(rstd[:], ms[:], ACT.Sqrt, bias=eps[:], scale=1.0 / D).then_inc(std_ready, 1)

            def hi_chunks(name, n, hi, t0=None):
                for k in range(n):
                    c = CH[name] + k
                    act.wait_ge(t_ready, (c if t0 is None else t0 + k) + 1)
                    act.activation(hi[:, k, :], tmp[:, c % 4, :], ACT.Copy).then_inc(h_hi, 1)

            act.wait_ge(par_ok, 3)
            act.activation(c_act[:], par_b[:, 104:112], ACT.Silu).then_inc(c_ok, 1)
            squares_of_x(0, 0)
            deviation(0)
            split_hi(act, S["mlp_u"], 0, 0)
            hi_chunks("h0", DC, hh)

            def epi_u(st, i, j):
                wait_sums(act, st, i, j)
                for m in range(2):
                    col = 4 * i + 2 * j + m
                    ins = act.activation(u[:, ds(col, 1), :], sums(j)[:, m:m + 1, :], ACT.Gelu_apprx_tanh,
                                         bias=par_b[:, ds(88 + col, 1)])
                ins.then_inc(acc_read["act"], 1)
            lead(act, "mlp_u", split_hi, epi_u, "mlp_v")

            def epi_v(st, i, j):
                act.wait_ge(v_added, 2 * i + j + 1)
                part = v[:, :, ds(COLS * (2 * i + j), COLS)]
                act.activation(part, part, ACT.Gelu_apprx_tanh).then_inc(v_gelu, 1)
            lead(act, "mlp_v", split_hi, epi_v, "mlp_out")
            act.wait_ge(ln_moments, 1)
            act.activation(small[:, 0:NB], moments[:, :, 1], ACT.Sqrt, bias=eps[:]).then_inc(ln_std, 1)
            hi_chunks("y", GC, y_hi)

            def output_epilogue(ev, y):
                def epi(st, i, j):
                    wait_sums(act, st, i, j)
                    for m in range(2):
                        square(ev, 4 * i + 2 * j + m, sums(j)[:, m, :])
                    act.activation(y[:, 4 * i + 2 * j:4 * i + 2 * j + 2, :], sums(j), ACT.Copy).then_inc(acc_read["act"], 1)
                return epi
            lead(act, "mlp_out", split_hi, output_epilogue(1, y_mlp), "gu0", unroll=True)
            deviation(1)
            squares_of_x(2, 8)
            deviation(2)
            hi_chunks("h1", DC, hh)

            def gu_epilogue(st, i, j):
                wait_sums(act, st, i, j)
                act.wait_ge(acc_read["dve"], st.read0 + 2 * i + j + 1)
                act.activation(tmp[:, j, :], sums(j)[:, 0, :], ACT.Silu).then_inc(sg_ready, 1)
            lead(act, "gu0", split_hi, gu_epilogue, "down0")
            lead(act, "down0", split_hi, output_epilogue(3, y_h), "k", unroll=True)
            deviation(3)
            squares_of_x(4, 16)
            deviation(4)
            hi_chunks("hkv", DC, hh)

            def head_norm_epilogue(dst, c0):
                def epi(st, i, j):
                    wait_sums(act, st, i, j)
                    c = c0 + 4 * i + 2 * j
                    if c >= 2:
                        act.wait_ge(hs_ps, c)
                    for m in range(2):
                        act.activation(sq[:, m, :], sums(j)[:, m, :], ACT.Square).then_inc(hsq_ready, 1)
                    t = 4 * i + 2 * j
                    act.activation(dst[:, t:t + 2, :], sums(j), ACT.Copy).then_inc(acc_read["act"], 1)
                    if c >= c0 + 2:
                        head_deviation(c - 2)
                    if c == c0 + 6:
                        head_deviation(c)
                return epi

            def head_deviation(c):
                for m in range(2):
                    act.wait_ge(hs_ps, c + m + 1)
                    if c >= 2:
                        act.wait_ge(kq_ready, c + m - 1)
                    act.activation(tmp[:, m, :], aux[:, m, :], ACT.Sqrt, bias=eps[:], scale=1.0 / DH).then_inc(hstd, 1)
            lead(act, "k", split_hi, head_norm_epilogue(k_fox, 0), "v", unroll=True)
            act.wait_ge(wf_in, 16)
            act.activation(wf_hi[:], wf_raw[:], ACT.Copy).then_inc(wf_split_hi, 1)

            def tokens_epilogue(dst):
                def epi(st, i, j):
                    wait_sums(act, st, i, j)
                    c = COLS * (2 * i + j)
                    act.activation(dst[:, :, c:c + COLS], sums_tok(j), ACT.Copy).then_inc(acc_read["act"], 1)
                return epi
            lead(act, "v", split_hi, tokens_epilogue(v_fox), "q", unroll=True)

            def log_sigmoid(parts, ab, n):
                act.wait_ge(ls_abs, n)
                act.activation(ab, ab, ACT.Exp, scale=-1.0)
                act.drain()
                act.activation(ab, ab, ACT.Ln, bias=1.0).then_inc(ls_log, 1)
            log_sigmoid(NH, gl_f[:, 1, :], 1)
            act.wait_ge(w_used, S["q"].unit0 + RING)
            hi_chunks("h2", DC, hh)
            lead(act, "q", split_hi, head_norm_epilogue(q_fox, 8), "gate", unroll=True)

            def func_epilogue(dst, func):
                def epi(st, i, j):
                    wait_sums(act, st, i, j)
                    t = 4 * i + 2 * j
                    act.activation(dst[:, t:t + 2, :], sums(j), func).then_inc(acc_read["act"], 1)
                return epi
            lead(act, "gate", split_hi, func_epilogue(gate, ACT.Sigmoid), "fox_out", unroll=True)
            act.wait_ge(kq_ready, 16)
            attention_act(act, fx)
            hi_chunks("og", DC, og_hi)
            lead(act, "fox_out", split_hi, output_epilogue(5, y_fox), "gu1", unroll=True)
            deviation(5)
            squares_of_x(6, 24)
            deviation(6)
            hi_chunks("h3", DC, hh)
            lead(act, "gu1", split_hi, gu_epilogue, "down1")
            lead(act, "down1", split_hi, output_epilogue(7, y_h), "ixq", unroll=True)
            deviation(7)
            squares_of_x(8, 32)
            deviation(8)
            act.wait_ge(xw_in, 16 * 5)
            act.activation(xw_hi[:], xw_raw[:], ACT.Copy).then_inc(xw_split_hi, 1)
            hi_chunks("h4", DC, hh)

            def scaled_epilogue(dst, scale):
                def epi(st, i, j):
                    wait_sums(act, st, i, j)
                    t = 4 * i + 2 * j
                    act.activation(dst[:, t:t + 2, :], sums(j), ACT.Copy, scale=scale).then_inc(acc_read["act"], 1)
                return epi
            lead(act, "ixq", split_hi, scaled_epilogue(ixq, 64.0 ** -0.5), "mqk", unroll=True)
            for n in range(3 * IH):
                w = WIDTH[1 + n // IH]
                act.wait_ge(ix_ps, n + 1)
                if n >= 4:
                    act.wait_ge(ix_added, n - 3)
                act.activation(tmp[:, n % 4, 0:w], aux[:, n % 2, 0:w], ACT.Relu).then_inc(ix_relu, 1)

            def conv_epilogue(st, i, j):
                wait_sums(act, st, i, j)
                t = 4 * i + 2 * j
                if t >= 2:
                    act.wait_ge(conv_ready, t)
                else:
                    act.wait_ge(xpad_zero, 1)
                act.activation(xpad[:, :, 3:3 + T], sums(j), ACT.Copy).then_inc(acc_read["act"], 1)
                act.drain().then_inc(xpad_ready, 1)
                for m in range(2):
                    dst = mq[:, t + m, :] if t + m < MH else mk[:, t + m - MH, :]
                    act.wait_ge(conv_ready, t + m + 1)
                    act.activation(dst, tmp[:, 2 + m, :], ACT.Silu).then_inc(conv_used, 1)
            lead(act, "mqk", split_hi, conv_epilogue, "mv", unroll=True)
            lead(act, "mv", split_hi, tokens_epilogue(mv), "aqk", unroll=True)

            def aqk_epilogue(st, i, j):
                wait_sums(act, st, i, j)
                t = 4 * i + 2 * j
                dst = aq[:, t:t + 2, :] if t < 4 else ak[:, t - 4:t - 2, :]
                act.activation(dst, sums(j), ACT.Copy, scale=64.0 ** -0.5 if t < 4 else 1.0).then_inc(acc_read["act"], 1)
            lead(act, "aqk", split_hi, aqk_epilogue, "av", unroll=True)
            lead(act, "av", split_hi, tokens_epilogue(av), "mo", unroll=True)
            act.wait_ge(ix_done, 1)
            act.wait_ge(row_u_ready, 1)
            lead(act, "mo", split_hi, func_epilogue(ogate, ACT.Sigmoid), "mz", unroll=True)

            def mz_epilogue(st, i, j):
                wait_sums(act, st, i, j)
                t = 4 * i + 2 * j
                if t >= 2:
                    act.wait_ge(ogate_ready, t)
                act.activation(tmp[:, 2:4, :], sums(j), ACT.Silu).then_inc(acc_read["act"], 1)
                act.drain().then_inc(mz_ready, 1)
            lead(act, "mz", split_hi, mz_epilogue, "az", unroll=True)
            lead(act, "az", split_hi, func_epilogue(az, ACT.Silu), "mix_out", unroll=True)

            log_sigmoid(MH, sq_sum[0:MH, :], 2)
            act.wait_ge(fg_ready, 1)
            act.activation(rstd[0:MH, :], rstd[0:MH, :], ACT.Exp, scale=-1.0).then_inc(em_ready, 1)
            act.wait_ge(w_used, S["mix_out"].unit0 + RING)

            def mlstm_head(h):
                act.wait_ge(num_ps, h + 1)
                act.activation(mks[:].unsqueeze(1), mk[:, ds(h, 1), :], ACT.Copy, scale=MQK ** -0.5).then_inc(m_staged, 1)
                act.activation(sel_h[:].unsqueeze(1), sel[:, ds(h, 1), :], ACT.Copy).then_inc(m_staged, 1)
                act.wait_ge(gb_ready, h + 1)
                for s in range(NB):
                    bias = mt[:, 0, s, ds(h, 1)]
                    ins = act.activation(m_e[:, TOFF[s]:TOFF[s] + P], tmp[:, 1, s * P:(s + 1) * P], ACT.Exp, bias=bias)
                    if s < NB - 1:
                        ins = act.activation(m_e[:, TOFF[s] + P:TOFF[s] + TW[s]], tmp[:, 0, (s + 1) * P:T], ACT.Exp, bias=bias)
                ins.then_inc(m_e_ready, 1)
                act.wait_ge(r_ready, h + 1)
                for b in range(NB):
                    act.activation(tmp[:, 2 + b // 2, (b % 2) * MV:(b % 2 + 1) * MV], aux[:, b // 2, (b % 2) * MV:(b % 2 + 1) * MV], ACT.Square,
                                   scale=small[:, 8 + b:9 + b], accum_out=small[:, 12 + b:13 + b])
                act.drain()
                act.activation(small[:, 16:20], small[:, 12:16], ACT.Sqrt, bias=eps[:], scale=1.0 / MV).then_inc(hm_std, 1)
            times(act, MH, mlstm_head)
            attention_act(act, dx)
            hi_chunks("mix", 12, mix_hi)

            def mix_epilogue(st, i, j):
                for m in range(2):
                    k = 4 * i + 2 * j + m
                    act.wait_ge(acc_read["dve"], st.read0 + 2 * i + j + 1 + 2)
                    act.activation(hh[:, k, :], xT[:, k, :], ACT.Copy).then_inc(h_hi, 1)
            lead(act, "mix_out", split_hi, mix_epilogue, "ple", unroll=True)
            hi_chunks("pt", 2, pt_hi, t0=84)

            def ple_epilogue(st, i, j):
                if j == 0:
                    wait_sums(act, st, i, j)
                    if i == 0:
                        act.wait_ge(h_ready, CH["pt"] + 2)
                    act.wait_ge(acc_read["dve"], st.read0 + 2 * i + 2)
                    act.activation(tmp[:, 0:2, :], sums(0), ACT.Sigmoid).then_inc(sg_ready, 1)
            lead(act, "ple", split_hi, ple_epilogue, None, unroll=True)
            squares_of_x(9, 40)
            deviation(9)
            for b in range(NB):
                act.wait_ge(ot_ps, b + 1)
                act.activation(x_out[:, b, :].rearrange("p (a n) -> p a n", a=2), acc[:, b % 2], ACT.Copy).then_inc(out_ready, 1)

        @block.gpsimd
        def _(pool):
            pool.memset(eps[:], EPS)
            pool.memset(ones[:], 1.0)
            pool.memset(ident[:], 0.0)
            pool.memset(head_ones[:], 0.0)
            pool.memset(tri[:], 0.0)
            pool.memset(tri_t[:], 0.0)
            pool.memset(sel[:], 0.0)
            pool.drain()
            for half in range(2):
                pool.memset(head_ones[64 * half:64 * half + 64, 64 * half:64 * half + 64], 1.0)
            pool.drain()
            pool.affine_select(out=ident[:], in_=ident[:], compare_op=ALU.not_equal, fill=1.0, base=0,
                               pattern=[[-1, P]], channel_multiplier=1)
            pool.affine_select(out=tri[:], in_=tri[:], compare_op=ALU.is_ge, fill=NEG, base=0,
                               pattern=[[-1, P]], channel_multiplier=1)
            pool.affine_select(out=tri_t[:], in_=tri_t[:], compare_op=ALU.is_ge, fill=NEG, base=0,
                               pattern=[[1, P]], channel_multiplier=-1)
            pool.affine_select(out=sel[:], in_=sel[:], compare_op=ALU.not_equal, fill=-1.0, base=0,
                               pattern=[[-1, MH], [0, P]], channel_multiplier=1)
            pool.drain().then_inc(consts, 1)

            def zero_sum(ev):
                if ev:
                    pool.wait_ge(ms_ready, ev)
                pool.memset(sq_sum[:], 0.0)
                pool.drain()

            def add_square(ev, k):
                pool.wait_ge(sq_ready, 8 * ev + k + 1)
                pool.tensor_tensor(sq_sum[:], sq_sum[:], sq[:, k % 2, :], ALU.add)
                pool.drain().then_inc(sq_added, 1)

            def add_squares(ev):
                zero_sum(ev)
                for k in range(DC):
                    add_square(ev, k)

            def lo_chunks(name, n, hi, lo, src=None):
                for k in range(n):
                    c = CH[name] + k
                    pool.wait_ge(h_hi, c + 1)
                    x = tmp[:, c % 4, :] if src is None else src[:, k, :]
                    pool.tensor_tensor(lo[:, k, :], x, hi[:, k, :].bitcast(F32), ALU.subtract).then_inc(h_ready, 1)

            def nothing(st, i, j):
                pass

            add_squares(0)
            pool.wait_ge(ws_in, 16)
            pool.affine_select(out=ws_raw[:], in_=ws_raw[:], compare_op=ALU.is_ge, fill=0.0, base=0,
                               pattern=[[0, 16], [-1, P]], channel_multiplier=1).then_inc(ws_masked, 1)
            split_lo(pool, S["mlp_u"], 0, 0)
            lo_chunks("h0", DC, hh, hl)
            lead(pool, "mlp_u", split_lo, nothing, "mlp_v")
            lead(pool, "mlp_v", split_lo, nothing, "mlp_out")
            lo_chunks("y", GC, y_hi, y_lo)

            def square_epilogue(ev):
                def epi(st, i, j):
                    if i == 0 and j == 0:
                        zero_sum(ev)
                    for m in range(2):
                        add_square(ev, 4 * i + 2 * j + m)
                return epi
            lead(pool, "mlp_out", split_lo, square_epilogue(1), "gu0", unroll=True)
            add_squares(2)
            lo_chunks("h1", DC, hh, hl)
            pool.nop().then_inc(act_ready, 2)

            def gu_epilogue(st, i, j):
                f = 2 * i + j
                pool.wait_ge(a_hi, (FC if st.name == "gu1" else 0) + f + 1)
                pool.tensor_tensor(act_lo[:, ds(f, 1), :], tmp[:, 2 + j:3 + j, :], act_hi[:, ds(f, 1), :].bitcast(F32),
                                   ALU.subtract).then_inc(act_ready, 1)
            lead(pool, "gu0", split_lo, gu_epilogue, "down0")
            lead(pool, "down0", split_lo, square_epilogue(3), "k", unroll=True)
            add_squares(4)
            lo_chunks("hkv", DC, hh, hl)
            pool.memset(wf_raw[:], 0.0).then_inc(wf_zero, 1)
            pool.memset(fx["mask"][:], 0.0)
            pool.drain()
            for b in range(NB):
                pool.tensor_copy(fx["mask"][:, OFF[b] + b * P:OFF[b] + (b + 1) * P], tri[:])
            pool.drain()
            lead(pool, "k", split_lo, nothing, "v", unroll=True)
            pool.wait_ge(wf_split_hi, 1)
            pool.tensor_tensor(wf_lo[:], wf_raw[:], wf_hi[:].bitcast(F32), ALU.subtract).then_inc(wf_split, 1)
            lead(pool, "v", split_lo, nothing, "q", unroll=True)
            lo_chunks("h2", DC, hh, hl)
            lead(pool, "q", split_lo, nothing, "gate", unroll=True)
            lead(pool, "gate", split_lo, nothing, "fox_out", unroll=True)
            attention_pool(pool, fx)
            lo_chunks("og", DC, og_hi, og_lo)
            lead(pool, "fox_out", split_lo, square_epilogue(5), "gu1", unroll=True)
            add_squares(6)
            lo_chunks("h3", DC, hh, hl)
            lead(pool, "gu1", split_lo, gu_epilogue, "down1")
            lead(pool, "down1", split_lo, square_epilogue(7), "ixq", unroll=True)
            pool.memset(xw_raw[:], 0.0).then_inc(xw_zero, 1)
            add_squares(8)
            pool.wait_ge(xw_split_hi, 1)
            pool.tensor_tensor(xw_lo[:], xw_raw[:], xw_hi[:].bitcast(F32), ALU.subtract).then_inc(xw_split, 1)
            lo_chunks("h4", DC, hh, hl)
            for name, following in (("ixq", "mqk"), ("mqk", "mv"), ("mv", "aqk"), ("aqk", "av"), ("av", "mo"), ("mo", "mz")):
                lead(pool, name, split_lo, nothing, following, unroll=True)

            def mz_epilogue(st, i, j):
                t = 4 * i + 2 * j
                pool.wait_ge(mz_ready, t // 2 + 1)
                for m in range(2):
                    pool.tensor_tensor(ogate[:, t + m, :], ogate[:, t + m, :], tmp[:, 2 + m, :], ALU.mult).then_inc(ogate_ready, 1)
            lead(pool, "mz", split_lo, mz_epilogue, "az", unroll=True)
            lead(pool, "az", split_lo, nothing, "mix_out", unroll=True)
            pool.wait_ge(dmask_ready, 1)
            attention_pool(pool, dx)
            lo_chunks("mix", 12, mix_hi, mix_lo)

            def mix_epilogue(st, i, j):
                for m in range(2):
                    k = 4 * i + 2 * j + m
                    pool.wait_ge(h_hi, CH["xg"] + k + 1)
                    pool.tensor_tensor(hl[:, k, :], xT[:, k, :], hh[:, k, :].bitcast(F32), ALU.subtract).then_inc(h_ready, 1)
            lead(pool, "mix_out", split_lo, mix_epilogue, "ple", unroll=True)
            lo_chunks("pt", 2, pt_hi, pt_lo)
            lead(pool, "ple", split_lo, nothing, None, unroll=True)
            add_squares(9)
        @block.tensor
        def _(pe):
            pe.nop().then_inc(w_used, RING)

            def products(out, pairs, first, last, check=False):
                for n, (w, x) in enumerate(pairs):
                    ins = pe.matmul(out, w, x, start=first and n == 0, stop=last and n == len(pairs) - 1, skip_group_check=check)
                return ins

            def gemm(name, hi, lo, ready, ready0, after=None, unroll=False, second=None):
                st = S[name]
                before = STAGES[STAGES.index(st) - 1] if st.group0 else None
                def body(i):
                    for j in range(2):
                        pe.wait_ge(acc_read[st.reader], st.read0 + 2 * i + j + 1)
                        if before and before.reader != st.reader:
                            pe.wait_ge(acc_read[before.reader], before.read0 + before.groups + j + 1)
                        a_hi, a_lo, a_ready, a_ready0 = second if second and j else (hi, lo, ready, ready0)
                        kc = st.kchunks[j]
                        for x, (k0, nk) in enumerate(st.units[j]):
                            s = slot_of(st, i, j, x)
                            pe.wait_ge(w_split, unit_no(st, i, j, x) + 1)
                            pe.wait_ge(a_ready, a_ready0 + k0 + nk)
                            for kk in range(nk):
                                k = k0 + kk
                                if st.token_major:
                                    for b in range(NB):
                                        blk = slice(b * P, (b + 1) * P)
                                        wh, wl = w_hi[:, s, kk, :], w_lo[:, s, kk, :]
                                        ins = products(sums_tok(j)[:, b, :], ((a_hi[:, k, blk], wh), (a_hi[:, k, blk], wl), (a_lo[:, k, blk], wh)),
                                                       k == 0 and b % 2 == 0, k == kc - 1, True)
                                else:
                                    for m in range(2):
                                        col = slice(m * P, (m + 1) * P)
                                        wh, wl = w_hi[:, s, kk, col], w_lo[:, s, kk, col]
                                        ins = products(sums(j)[:, m, :], ((wh, a_hi[:, k, :]), (wh, a_lo[:, k, :]), (wl, a_hi[:, k, :])),
                                                       k == 0, k == kc - 1)
                            ins.then_inc(w_used, 1)
                        if after:
                            after(i, j)
                times(pe, st.iters, body, unroll or st.per_body % RING != 0)

            def ada_column(step, par, setup=False):
                pe.wait_ge(ada_ready, step + 1)
                if not setup:
                    pe.wait_ge(ada_col, step + 1)
                elif step >= 2:
                    pe.wait_ge(ada_col, step - 1)
                for m in range(2):
                    ins = pe.matmul(ada_ps[:, 2 * par + m:2 * par + m + 1], ada_acc[:, par, m * P:(m + 1) * P], ones[:, 0:1],
                                    start=True, stop=True)
                ins.then_inc(ada_sum, 1)

            def mean_square(ev):
                pe.wait_ge(sq_added, 8 * ev + 8)
                pe.matmul(ms[:], ones[:], sq_sum[:], start=True, stop=True).then_inc(ms_ready, 1)

            pe.wait_ge(consts, 1)
            pe.wait_ge(par_in, 16 * 20)
            for n, r in enumerate((112, 112, 74)):
                pe.transpose(bank(n)[:, 0:r], rows[0:r, n, :], ident[0:r, 0:r]).then_inc(par_t, 1)
            pe.wait_ge(x_landed, 16)
            pe.wait_ge(par_ok, 3)
            banks = [bank(0), bank(1), bank(2), bank(3), ms, ada_ps, aux[:, 0, :], aux[:, 1, :]]
            for k in range(DC):
                for b in range(NB):
                    ins = pe.transpose(banks[k][:, b * P:(b + 1) * P], x_in[:, b, k * P:(k + 1) * P], ident[:])
                ins.then_inc(xt_ps, 1)
            pe.wait_ge(x_ready, DC)
            mean_square(0)
            for s in range(8):
                ada_column(s, s % 2, True)
            pe.wait_ge(ws_masked, 1)
            for q in range(4):
                if q >= 2:
                    pe.wait_ge(wst_ready, q - 1)
                for n in range(4):
                    ins = pe.transpose(aux[:, q % 2, n * P:(n + 1) * P], ws_raw[:, 4 * q + n, :], ident[:])
                ins.then_inc(wst_ps, 1)
            gemm("mlp_u", hh, hl, h_ready, CH["h0"], lambda i, j: ada_column(8 + 2 * i + j, j))
            gemm("mlp_v", hh, hl, h_ready, CH["h0"], lambda i, j: ada_column(16 + 2 * i + j, j))
            pe.wait_ge(wst_ready, 4)
            for q in range(4):
                if q >= 2:
                    pe.wait_ge(r_read, q - 1)
                pe.matmul(aux[:, q % 2, :], ones[:], ws_t[:, 4 * q:4 * q + 4, :].rearrange("p g t -> p (g t)"),
                          start=True, stop=True).then_inc(r_ps, 1)
            pe.wait_ge(v_norm, NB)
            pe.wait_ge(r_read, 4)
            for g in range(16):
                if g >= 2:
                    pe.wait_ge(mix_read, g - 1)
                for b in range(NB):
                    ins = pe.matmul(aux[:, g % 2, b * P:(b + 1) * P], v[:, b, g * P:(g + 1) * P], ws_t[:, g, :], start=True, stop=True)
                ins.then_inc(mix_ps, 1)

            def kv_columns(i, j):
                for a in range(2):
                    ada_column(24 + 4 * i + 2 * j + a, a)
            gemm("mlp_out", y_hi, y_lo, h_ready, CH["y"], kv_columns, unroll=True)
            mean_square(1)
            mean_square(2)
            gemm("gu0", hh, hl, h_ready, CH["h1"], lambda i, j: ada_column(32 + 2 * i + j, j))
            gemm("down0", act_hi, act_lo, act_ready, 2, lambda i, j: ada_column(54 + j, j) if i == 0 else None, unroll=True)
            mean_square(3)
            mean_square(4)

            def head_squares(c0):
                def after(i, j):
                    c = c0 + 4 * i + 2 * j
                    for t in ([] if c == c0 else [c - 2, c - 1]) + ([c, c + 1] if c == c0 + 6 else []):
                        pe.wait_ge(hsq_ready, t + 1)
                        if t >= 2:
                            pe.wait_ge(hstd, t - 1)
                        pe.matmul(aux[:, t % 2, :], head_ones[:], sq[:, t % 2, :], start=True, stop=True).then_inc(hs_ps, 1)
                return after
            gemm("k", hh, hl, h_ready, CH["hkv"], head_squares(0), unroll=True)
            pe.wait_ge(wf_split, 1)
            pe.wait_ge(hstd, 8)
            for k in range(DC):
                ins = products(aux[:, 0, :], ((wf_hi[:, k, :], hh[:, k, :]), (wf_hi[:, k, :], hl[:, k, :]), (wf_lo[:, k, :], hh[:, k, :])),
                               k == 0, k == DC - 1)
            ins.then_inc(f_ps, 1)
            gemm("v", hh, hl, h_ready, CH["hkv"], unroll=True)
            pe.wait_ge(f_read, 1)
            gemm("q", hh, hl, h_ready, CH["h2"], head_squares(8), unroll=True)
            gemm("gate", hh, hl, h_ready, CH["h2"], unroll=True)
            attention_pe(pe, fx)

            def to_features(src, n, done_sem, read_sem, c0, r0):
                for k in range(n):
                    if c0 + k >= 2:
                        pe.wait_ge(read_sem, r0 + k - 1)
                    for b in range(NB):
                        ins = pe.transpose(aux[:, k % 2, b * P:(b + 1) * P], src[:, b, k * P:(k + 1) * P], ident[:])
                    ins.then_inc(done_sem, 1)
            pe.wait_ge(fx["o_read"], NH + 2)
            to_features(fx["o"], DC, og_ps, t_ready, 0, CH["og"])
            gemm("fox_out", og_hi, og_lo, h_ready, CH["og"], unroll=True)
            mean_square(5)
            mean_square(6)
            gemm("gu1", hh, hl, h_ready, CH["h3"])
            gemm("down1", act_hi, act_lo, act_ready, FC + 2, unroll=True)
            mean_square(7)
            mean_square(8)
            pe.wait_ge(xw_split, 1)
            pe.wait_ge(h_ready, CH["h4"] + DC)
            for n in range(2):
                for k in range(DC):
                    wh, wl = xw_hi[:, k, n * P:(n + 1) * P], xw_lo[:, k, n * P:(n + 1) * P]
                    ins = products(aux[:, n, :], ((wh, hh[:, k, :]), (wh, hl[:, k, :]), (wl, hh[:, k, :])), k == 0, k == DC - 1)
            for b in range(NB):
                blk = slice(b * P, (b + 1) * P)
                for k in range(DC):
                    wh, wl = xw_hi[:, k, 256:264], xw_lo[:, k, 256:264]
                    ins = products(ms[:, b * IH:(b + 1) * IH], ((hh[:, k, blk], wh), (hh[:, k, blk], wl), (hl[:, k, blk], wh)),
                                   k == 0, k == DC - 1)
            ins.then_inc(xw_ps, 1)
            gemm("ixq", hh, hl, h_ready, CH["h4"], unroll=True)
            pe.wait_ge(xw_read, 1)
            pe.wait_ge(acc_read["act"], S["mqk"].read0 + 2)
            for n in range(3 * IH):
                b, h = 1 + n // IH, n % IH
                half = slice(64 * (h % 2), 64 * (h % 2) + 64)
                if n >= 2:
                    pe.wait_ge(ix_relu, n - 1)
                pe.matmul(aux[:, n % 2, 0:WIDTH[b]], ixq[half, h // 2, b * P:(b + 1) * P], ixk[half, 0:WIDTH[b]],
                          start=True, stop=True).then_inc(ix_ps, 1)
            gemm("mqk", hh, hl, h_ready, CH["h4"], unroll=True)
            pe.wait_ge(one_hot_in, 16)
            pe.wait_ge(gates_in, 64)
            pe.wait_ge(ix_relu, 3 * IH)
            pe.matmul(aux[0:AH, 0, :], rel[:], one_hot[:, 0:T], start=True, stop=True)
            pe.matmul(aux[0:AH, 1, 0:UROW - T], rel[:], one_hot[:, T:UROW], start=True, stop=True).then_inc(u_ps, 1)
            gemm("mv", hh, hl, h_ready, CH["h4"], unroll=True)
            gemm("aqk", hh, hl, h_ready, CH["h4"], unroll=True)
            gemm("av", hh, hl, h_ready, CH["h4"], unroll=True)
            gemm("mo", hh, hl, h_ready, CH["h4"], unroll=True)
            gemm("mz", hh, hl, h_ready, CH["h4"], unroll=True)
            gemm("az", hh, hl, h_ready, CH["h4"], unroll=True)

            pe.wait_ge(em_ready, 1)
            pe.wait_ge(row_u_ready, 1)
            for n, src in enumerate((sq[0:MH, 0, :], rstd[0:MH, :])):
                for b in range(NB):
                    c = (n * NB + b) * MH
                    ins = pe.matmul(ada_ps[:, c:c + MH], src[:, b * P:(b + 1) * P], ident[0:MH, 0:MH], start=True, stop=True)
            ins.then_inc(mt_ps, 1)
            pe.wait_ge(mt_ready, 1)
            pe.wait_ge(acc_read["act"], S["az"].read0 + S["az"].groups + 2)

            def mlstm_head(h):
                pe.wait_ge(m_staged, 2 * h + 2)
                pe.matmul(ms[:], sel_h[:], sq_sum[0:MH, :], start=True, stop=True).then_inc(gb_ps, 1)
                for s in range(NB):
                    ins = pe.matmul(bank(s)[:, 0:TW[s]], mks[:, s * P:(s + 1) * P], mq[:, ds(h, 1), s * P:T].rearrange("p a t -> p (a t)"),
                                    start=True, stop=True)
                ins.then_inc(qk_ps, 1)
                pe.wait_ge(m_s_ready, h + 1)
                pe.wait_ge(hm_ready, h + 1)
                for b in range(NB):
                    for s in range(b + 1):
                        w = m_s[:, TOFF[s] + (b - s) * P:TOFF[s] + (b - s + 1) * P]
                        pe.matmul(aux[:, b // 2, (b % 2) * MV:(b % 2 + 1) * MV], w, mv[:, s, ds(h * MV, MV)], start=s == 0, stop=s == b)
                        ins = pe.matmul(ada_ps[:, b:b + 1], w, ones[:, 0:1], start=s == 0, stop=s == b)
                ins.then_inc(num_ps, 1)
            pe.nop().then_inc(num_ps, 1)
            times(pe, MH, mlstm_head)
            pe.wait_ge(hm_ready, MH + 1)
            attention_pe(pe, dx)
            pe.wait_ge(dx["o_read"], AH + 2)
            to_features(hm, 8, mix_t, t_ready, 0, CH["mix"])
            to_features(dx["o"], 4, mix_t, t_ready, 8, CH["mix"] + 8)
            gemm("mix_out", mix_hi, mix_lo, h_ready, CH["mix"])
            pe.wait_ge(p_landed, 16)
            for k in range(2):
                for b in range(NB):
                    ins = pe.transpose(aux[:, k, b * P:(b + 1) * P], p_in[:, b, k * P:(k + 1) * P], ident[:])
                ins.then_inc(p_t, 1)
            gemm("ple", hh, hl, h_ready, CH["xg"], second=(pt_hi, pt_lo, h_ready, CH["pt"]))
            mean_square(9)
            pe.wait_ge(xn_ready, DC)
            for b in range(NB):
                if b >= 2:
                    pe.wait_ge(out_ready, b - 1)
                for k in range(DC):
                    ins = pe.transpose(acc[:, b % 2, k // 4, (k % 4) * P:(k % 4 + 1) * P], x_norm[:, k, b * P:(b + 1) * P], ident[:])
                ins.then_inc(ot_ps, 1)

        @block.vector
        def _(dve):
            dve.nop().then_inc(acc_read["dve"], 2)
            dve.nop().then_inc(ada_used, 2)

            def ada_step(w_col, step, par, finish=True):
                if finish:
                    ada_finish(step - 2, par, step)
                for half in range(2):
                    dve.drain()
                    dve.wait_ge(ada_landed[half], 16 * step + 16)
                    for kk in range(KU):
                        k = half * KU + kk
                        if k == 0:
                            ins = dve.tensor_scalar(ada_acc[:, par, :], ada_raw[:, half, kk, :], c_act[:, k:k + 1], None, ALU.mult)
                        else:
                            if kk:
                                dve.drain()
                            ins = dve.scalar_tensor_tensor(ada_acc[:, par, :], ada_raw[:, half, kk, :], c_act[:, k:k + 1],
                                                           ada_acc[:, par, :], ALU.mult, ALU.add)
                    ins.then_inc(ada_used, 1)
                dve.drain().then_inc(ada_ready, 1)

            def ada_finish(step, par, summed):
                dve.wait_ge(ada_sum, summed)
                dve.tensor_tensor(mod[:, ds(2 * step, 2)], ada_ps[:, 2 * par:2 * par + 2], par_a[:, ds(2 * step, 2)], ALU.add) \
                    .then_inc(ada_col, 1)

            def inverse_deviation(ev):
                dve.wait_ge(std_ready, ev + 1)
                dve.reciprocal(rstd[:], rstd[:])
                dve.drain()

            def free_tmp(c):
                if c >= 4:
                    dve.wait_ge(h_ready, c - 3)

            def normed(name, gain, scale=None, shift=None):
                if scale is None:
                    col = gain
                else:
                    dve.scalar_tensor_tensor(scol[:], scale, 1.0, gain, ALU.add, ALU.mult)
                    col = scol[:]
                for k in range(0, DC, 2):
                    for m in range(2):
                        c = CH[name] + k + m
                        free_tmp(c)
                        dve.tensor_tensor(tmp[:, c % 4, :], xT[:, k + m, :], rstd[:], ALU.mult)
                    dve.drain()
                    for m in range(2):
                        c = CH[name] + k + m
                        dve.tensor_scalar(tmp[:, c % 4, :], tmp[:, c % 4, :], col[:, k + m:k + m + 1],
                                          shift[:, k + m:k + m + 1] if shift is not None else None,
                                          ALU.mult, ALU.add if shift is not None else ALU.bypass).then_inc(t_ready, 1)

            def add_normed(y, gain, gate_col):
                dve.tensor_tensor(bcol[:], gate_col, gain, ALU.mult)
                for k in range(0, DC, 2):
                    for m in range(2):
                        dve.tensor_tensor(tmp[:, (k + m) % 4, :], y[:, k + m, :], rstd[:], ALU.mult)
                    dve.drain()
                    for m in range(2):
                        dve.scalar_tensor_tensor(xT[:, k + m, :], tmp[:, (k + m) % 4, :], bcol[:, k + m:k + m + 1], xT[:, k + m, :],
                                                 ALU.mult, ALU.add).then_inc(x_ready, 1)
                dve.drain()

            for n, (dst, r) in enumerate(((par_a, 112), (par_b, 112), (par_c, 74))):
                dve.wait_ge(par_t, n + 1)
                dve.tensor_copy(dst[:, 0:r], bank(n)[:, 0:r]).then_inc(par_ok, 1)
            banks = [bank(0), bank(1), bank(2), bank(3), ms, ada_ps, aux[:, 0, :], aux[:, 1, :]]
            for k in range(DC):
                dve.wait_ge(xt_ps, k + 1)
                dve.tensor_copy(xT[:, k, :], banks[k][:]).then_inc(x_ready, 1)
            dve.wait_ge(c_ok, 1)
            for s in range(8):
                ada_step(None, s, s % 2, s >= 2)
            for s in (6, 7):
                ada_finish(s, s % 2, 8)
            dve.drain()
            inverse_deviation(0)
            normed("h0", par_b[:, 0:8], mod[:, 8:16], mod[:, 0:8])
            for q in range(4):
                dve.wait_ge(wst_ps, q + 1)
                dve.tensor_copy(ws_t[:, 4 * q:4 * q + 4, :].rearrange("p g t -> p (g t)"), aux[:, q % 2, :]).then_inc(wst_ready, 1)

            def u_body(i):
                for j in range(2):
                    ada_step(None, 8 + 2 * i + j, j)
            times(dve, S["mlp_u"].iters, u_body)
            dve.wait_ge(b_in_in, 16)
            st = S["mlp_v"]

            def v_body(i):
                for j in range(2):
                    ada_step(None, 16 + 2 * i + j, j)
                    wait_sums(dve, st, i, j)
                    c = COLS * (2 * i + j)
                    dve.tensor_tensor(v[:, :, ds(c, COLS)], sums_tok(j), b_in[:, ds(c, COLS)].unsqueeze(1).broadcast_to([P, NB, COLS]),
                                      ALU.add).then_inc(acc_read["dve"], 1)
                    dve.drain().then_inc(v_added, 1)
                    dve.wait_ge(v_gelu, 2 * i + j + 1)
                    for b in range(NB):
                        dve.bn_stats(stats[:, b, ds(2 * i + j, 1), :].rearrange("p a s -> p (a s)"),
                                     v[:, b, ds(c, COLS)])
            times(dve, st.iters, v_body)
            dve.drain()
            for b in range(NB):
                ins = dve.bn_aggr(moments[:, b, :], stats[:, b, :, :].rearrange("p a s -> p (a s)"))
            ins.then_inc(ln_moments, 1)
            dve.wait_ge(ln_std, 1)
            dve.reciprocal(small[:, 4:8], small[:, 0:NB])
            dve.drain()
            for b in range(NB):
                dve.tensor_scalar(v[:, b, :], v[:, b, :], moments[:, b, 0:1], small[:, 4 + b:5 + b], ALU.subtract, ALU.mult) \
                    .then_inc(v_norm, 1)
            dve.wait_ge(q_bias_in, 16)
            for q in range(4):
                dve.wait_ge(r_ps, q + 1)
                for n in range(4):
                    g = 4 * q + n
                    ins = dve.scalar_tensor_tensor(q_bias[:, g, :], aux[:, q % 2, n * P:(n + 1) * P], par_c[:, 50 + g:51 + g],
                                                   q_bias[:, g, :], ALU.mult, ALU.add)
                ins.then_inc(r_read, 1)
            dve.drain()
            for g in range(16):
                c = CH["y"] + g
                free_tmp(c)
                dve.wait_ge(mix_ps, g + 1)
                dve.scalar_tensor_tensor(tmp[:, c % 4, :].rearrange("p (b t) -> p b t", b=NB), aux[:, g % 2, :].rearrange("p (b t) -> p b t", b=NB),
                                         par_c[:, 34 + g:35 + g], q_bias[:, g:g + 1, :].broadcast_to([P, NB, P]),
                                         ALU.mult, ALU.add).then_inc(mix_read, 1)
                dve.drain()
                dve.tensor_tensor(tmp[:, c % 4, :], tmp[:, c % 4, :], u[:, g, :], ALU.mult).then_inc(t_ready, 1)
            for s in range(8):
                ada_step(None, 24 + s, s % 2)
            inverse_deviation(1)
            add_normed(y_mlp, par_b[:, 16:24], mod[:, 16:24])
            inverse_deviation(2)
            normed("h1", par_b[:, 32:40], mod[:, 32:40], mod[:, 24:32])

            def feed_forward(name, l, ada=None):
                st = S[name]
                def body(i):
                    for j in range(2):
                        if ada is not None:
                            ada_step(None, ada + 2 * i + j, j)
                        wait_sums(dve, st, i, j)
                        f = 2 * i + j
                        dve.wait_ge(sg_ready, l * FC + f + 1)
                        dve.wait_ge(act_ready, l * FC + f + 1)
                        dve.tensor_tensor(tmp[:, 2 + j, :], sums(j)[:, 1, :], tmp[:, j, :], ALU.mult).then_inc(acc_read["dve"], 1)
                        dve.drain()
                        dve.tensor_copy(act_hi[:, ds(f, 1), :], tmp[:, 2 + j:3 + j, :]).then_inc(a_hi, 1)
                times(dve, st.iters, body)
            feed_forward("gu0", 0, 32)
            for s in (54, 55):
                ada_step(None, s, s % 2)
            for s in (54, 55):
                ada_finish(s, s % 2, 56)
            dve.drain()
            inverse_deviation(3)
            add_normed(y_h, par_b[:, 48:56], mod[:, 40:48])
            inverse_deviation(4)
            normed("hkv", par_b[:, 64:72], mod[:, 56:64], mod[:, 48:56])

            def head_norm(dst, gain, c0):
                for k in range(DC):
                    c = c0 + k
                    dve.wait_ge(hstd, c + 1)
                    dve.reciprocal(tmp[:, c % 2, :], tmp[:, c % 2, :])
                    dve.drain()
                    dve.scalar_tensor_tensor(dst[:, k, :], dst[:, k, :], gain, tmp[:, c % 2, :], ALU.mult, ALU.mult).then_inc(kq_ready, 1)
            dve.tensor_scalar(qgain[:], par_c[:, 33:34], DH ** -0.5, None, ALU.mult)
            head_norm(k_fox, par_c[:, 32:33], 0)

            def log_forget(f, ab, low, total, n):
                dve.scalar_tensor_tensor(ab, f, -1.0, f, ALU.mult, ALU.max).then_inc(ls_abs, 1)
                dve.tensor_scalar(low, f, 0.0, None, ALU.min)
                dve.drain()
                dve.wait_ge(ls_log, n)
                dve.tensor_tensor(low, low, ab, ALU.subtract)
                dve.drain()
                rows_n = low.shape[0]
                dve.tensor_tensor_scan(total, ones[0:rows_n, 0:1].broadcast_to([rows_n, T]), low, 0.0, ALU.mult, ALU.add)
                dve.drain()
            dve.wait_ge(f_ps, 1)
            dve.wait_ge(gates_in, 64)
            dve.tensor_scalar(gl_f[:, 0, :], aux[0:NH, 0, :], kvbf[:], None, ALU.add).then_inc(f_read, 1)
            dve.drain()
            log_forget(gl_f[:, 0, :], gl_f[:, 1, :], gl_f[:, 2, :], gl_f[:, 3, :], 1)
            dve.tensor_scalar(gl_f[:, 4, :], gl_f[:, 3, :], -1.0, None, ALU.mult).then_inc(fox_d_ready, 1)
            normed("h2", par_b[:, 8:16], mod[:, 72:80], mod[:, 64:72])
            head_norm(q_fox, qgain[:], 8)
            attention_dve(dve, fx)
            for k in range(DC):
                c = CH["og"] + k
                free_tmp(c)
                dve.wait_ge(og_ps, k + 1)
                dve.tensor_tensor(tmp[:, c % 4, :], aux[:, k % 2, :], gate[:, k, :], ALU.mult).then_inc(t_ready, 1)
            inverse_deviation(5)
            add_normed(y_fox, par_b[:, 24:32], mod[:, 80:88])
            inverse_deviation(6)
            normed("h3", par_b[:, 40:48], mod[:, 96:104], mod[:, 88:96])
            feed_forward("gu1", 1)
            inverse_deviation(7)
            add_normed(y_h, par_b[:, 56:64], mod[:, 104:112])
            inverse_deviation(8)
            normed("h4", par_b[:, 72:80])

            dve.wait_ge(xw_ps, 1)
            dve.tensor_copy(ixk[:], aux[:, 0, :])
            dve.tensor_scalar(iw[:].rearrange("p b h -> p (b h)"), ms[:, 0:NB * IH], IH ** -0.5, None, ALU.mult)
            dve.tensor_copy(sq[0:MH, 0, :], aux[0:MH, 1, :])
            dve.tensor_copy(sq[0:MH, 1, :], aux[32:32 + MH, 1, :])
            dve.memset(xpad[:, :, 0:3], 0.0).then_inc(xpad_zero, 1)
            dve.drain().then_inc(xw_read, 1)
            for n in range(3 * IH):
                b, h = 1 + n // IH, n % IH
                part = score[:, OFF[b] - P:OFF[b] - P + WIDTH[b]]
                dve.wait_ge(ix_relu, n + 1)
                if h == 0:
                    dve.tensor_scalar(part, tmp[:, n % 4, 0:WIDTH[b]], iw[:, b, h:h + 1], None, ALU.mult).then_inc(ix_added, 1)
                else:
                    dve.drain()
                    dve.scalar_tensor_tensor(part, tmp[:, n % 4, 0:WIDTH[b]], iw[:, b, h:h + 1], part, ALU.mult, ALU.add).then_inc(ix_added, 1)
            dve.drain()
            for b in range(1, NB):
                diag = score[:, OFF[b] - P + b * P:OFF[b] - P + (b + 1) * P]
                dve.tensor_tensor(diag, diag, tri[:], ALU.add)
            for t in range(2 * MH):
                m = t % 2
                dve.wait_ge(xpad_ready, t // 2 + 1)
                if t >= 2:
                    dve.wait_ge(conv_used, t - 1)
                out = tmp[:, 2 + m, :]
                dve.tensor_scalar(out, xpad[:, m, 0:T], par_c[:, t:t + 1], None, ALU.mult)
                for w in range(1, 4):
                    dve.drain()
                    ins = dve.scalar_tensor_tensor(out, xpad[:, m, w:w + T], par_c[:, 8 * w + t:8 * w + t + 1], out, ALU.mult, ALU.add)
                ins.then_inc(conv_ready, 1)
            for b in range(1, NB):
                part = score[:, OFF[b] - P:OFF[b] - P + WIDTH[b]]
                work = tmp[:, 0, 0:WIDTH[b]]
                dve.tensor_copy(work, part)
                dve.drain()
                def round8(i):
                    dve.max(best[:], work)
                    dve.drain()
                    dve.match_replace(work, best[:], work, TAKEN)
                    dve.drain()
                times(dve, TOPK // 8, round8)
                sel_part = dmask[:, OFF[b]:OFF[b] + WIDTH[b]]
                dve.tensor_tensor(sel_part, part, work, ALU.not_equal)
                dve.drain()
                dve.tensor_scalar(sel_part, sel_part, -NEG, NEG, ALU.mult, ALU.add)
                if b == 1:
                    dve.tensor_copy(dmask[:, 0:P], tri[:])
            dve.drain().then_inc(dmask_ready, 1)
            dve.nop().then_inc(ix_done, 1)
            dve.wait_ge(u_ps, 1)
            dve.tensor_copy(row_u[:, 0:T], aux[0:AH, 0, :])
            dve.tensor_copy(row_u[:, T:UROW], aux[0:AH, 1, 0:UROW - T])
            dve.drain().then_inc(row_u_ready, 1)

            dve.tensor_scalar(sq[0:MH, 0, :], sq[0:MH, 0, :], bgate[:, 0:1], None, ALU.add)
            dve.tensor_scalar(sq[0:MH, 1, :], sq[0:MH, 1, :], bgate[:, 1:2], None, ALU.add)
            dve.drain()
            log_forget(sq[0:MH, 1, :], sq_sum[0:MH, :], rstd[0:MH, :], sq[0:MH, 1, :], 2)
            dve.tensor_tensor(sq[0:MH, 0, :], sq[0:MH, 0, :], sq[0:MH, 1, :], ALU.subtract)
            dve.drain()
            dve.tensor_tensor_scan(sq_sum[0:MH, :], sq[0:MH, 0, :], sq[0:MH, 0, :], 0.0, ALU.max, ALU.max)
            dve.drain()
            dve.tensor_tensor(rstd[0:MH, :], sq_sum[0:MH, :], sq[0:MH, 1, :], ALU.add).then_inc(fg_ready, 1)
            dve.wait_ge(mt_ps, 1)
            dve.tensor_copy(mt[:].rearrange("p n b h -> p (n b h)"), ada_ps[:, 0:2 * NB * MH]).then_inc(mt_ready, 1)
            dve.drain()

            def mlstm_head(h):
                dve.wait_ge(gb_ps, h + 1)
                dve.tensor_copy(tmp[:, 0, :], ms[:])
                dve.drain()
                dve.tensor_tensor(tmp[:, 1, :].rearrange("p (b t) -> p b t", b=NB), tmp[:, 0, :].rearrange("p (b t) -> p b t", b=NB),
                                  tri_t[:].unsqueeze(1).broadcast_to([P, NB, P]), ALU.add).then_inc(gb_ready, 1)
                dve.wait_ge(m_e_ready, h + 1)
                dve.wait_ge(qk_ps, h + 1)
                for s in range(NB):
                    ins = dve.tensor_tensor(m_s[:, TOFF[s]:TOFF[s] + TW[s]], bank(s)[:, 0:TW[s]], m_e[:, TOFF[s]:TOFF[s] + TW[s]], ALU.mult)
                ins.then_inc(m_s_ready, 1)
                dve.wait_ge(num_ps, h + 2)
                dve.scalar_tensor_tensor(small[:, 20:24], ada_ps[:, 0:NB], -1.0, mt[:, 1, :, ds(h, 1)].rearrange("p b a -> p (b a)"),
                                         ALU.mult, ALU.max)
                dve.drain()
                dve.tensor_tensor(small[:, 20:24], small[:, 20:24], ada_ps[:, 0:NB], ALU.max)
                dve.drain()
                dve.reciprocal(small[:, 8:12], small[:, 20:24]).then_inc(r_ready, 1)
                dve.wait_ge(hm_std, h + 1)
                dve.reciprocal(small[:, 24:28], small[:, 16:20])
                dve.drain()
                dve.tensor_tensor(small[:, 28:32], small[:, 24:28], small[:, 8:12], ALU.mult)
                dve.drain()
                for b in range(NB):
                    ins = dve.tensor_scalar(hm[:, b, ds(h * MV, MV)], aux[:, b // 2, (b % 2) * MV:(b % 2 + 1) * MV],
                                            small[:, 28 + b:29 + b], None, ALU.mult)
                ins.then_inc(hm_ready, 1)
            dve.nop().then_inc(hm_ready, 1)
            times(dve, MH, mlstm_head)
            attention_dve(dve, dx)
            for k in range(12):
                c = CH["mix"] + k
                free_tmp(c)
                dve.wait_ge(mix_t, k + 1)
                if k < 8:
                    dve.scalar_tensor_tensor(tmp[:, c % 4, :], aux[:, k % 2, :], par_c[:, 66 + k:67 + k], ogate[:, k, :],
                                             ALU.mult, ALU.mult).then_inc(t_ready, 1)
                else:
                    dve.tensor_tensor(tmp[:, c % 4, :], aux[:, k % 2, :], az[:, k - 8, :], ALU.mult).then_inc(t_ready, 1)
            st = S["mix_out"]
            for i in range(st.iters):
                for j in range(2):
                    wait_sums(dve, st, i, j)
                    t = 4 * i + 2 * j
                    dve.tensor_tensor(xT[:, t:t + 2, :], xT[:, t:t + 2, :], sums(j), ALU.add).then_inc(acc_read["dve"], 1)
            for k in range(2):
                dve.wait_ge(p_t, k + 1)
                c = CH["pt"] + k
                free_tmp(c)
                dve.tensor_copy(tmp[:, c % 4, :], aux[:, k, :]).then_inc(t_ready, 1)
            st = S["ple"]
            for i in range(st.iters):
                dve.wait_ge(sg_ready, 2 * FC + i + 1)
                dve.nop().then_inc(acc_read["dve"], 1)
                dve.drain()
                wait_sums(dve, st, i, 1)
                dve.tensor_tensor(tmp[:, 2:4, :], sums(1), tmp[:, 0:2, :], ALU.mult).then_inc(acc_read["dve"], 1)
                dve.drain()
                for m in range(2):
                    dve.tensor_tensor(xT[:, 2 * i + m, :], xT[:, 2 * i + m, :], tmp[:, 2 + m, :], ALU.add).then_inc(x_ready, 1)
            inverse_deviation(9)
            for k in range(0, DC, 2):
                for m in range(2):
                    dve.tensor_tensor(x_norm[:, k + m, :], xT[:, k + m, :], rstd[:], ALU.mult)
                dve.drain()
                for m in range(2):
                    dve.tensor_scalar(x_norm[:, k + m, :], x_norm[:, k + m, :], par_b[:, 80 + k + m:81 + k + m], None, ALU.mult).then_inc(xn_ready, 1)


INPUTS = ["x", "c", "ada_w", "ada_b", "pre_mix_g", "post_mix_g", "pre_ffn_g", "post_ffn_g", "ffn_w_gu", "ffn_w_down", "a_w_in",
          "a_b_in", "a_ln_g", "a_ln_b", "a_w_s", "a_b_s", "a_w_out", "kv_ada_w", "kv_ada_b", "kv_norm_g", "kv_w", "kv_b_f",
          "k_norm_g", "b_w_qg", "b_q_norm_g", "b_w_o", "p_2", "w_in_2", "b_gate_2", "conv_w_2", "w_out_2", "norm_in_2",
          "m_norm_2", "rel_bias_2", "w_ple_2", "w_ple_gate_2", "norm_final_2"]


def kernel(**inputs):
    import concourse.bacc as bacc
    from concourse.bass_utils import run_bass_kernel_spmd

    nc = bacc.Bacc("TRN2", target_bir_lowering=False, num_devices=1)
    arrays = {name: np.ascontiguousarray(inputs[name]) for name in INPUTS}
    arrays["one_hot"] = distance_buckets()
    io = {}
    for name, a in arrays.items():
        io[name.removesuffix("_2") if name in ("w_ple_2", "w_ple_gate_2") else name] = \
            nc.dram_tensor(f"in_{name}", a.shape, F32, kind="ExternalInput").ap()
    io["out"] = nc.dram_tensor("out", (1, T, D), F32, kind="ExternalOutput").ap()
    io["fox_nd"] = nc.dram_tensor("fox_nd", (NH, T), F32, kind="Internal").ap()
    io["rel_u"] = nc.dram_tensor("rel_u", (AH, P, UROW), F32, kind="Internal").ap()
    build_program(nc, io)
    result = run_bass_kernel_spmd(nc, [{f"in_{name}": a for name, a in arrays.items()}], core_ids=[0])
    return result.results[0]["out"]
```

```python
from contextlib import ExitStack

import numpy as np

import concourse.bass as bass
from concourse import mybir
from concourse.alu_op_type import AluOpType as ALU

F32 = mybir.dt.float32
F32R = mybir.dt.float32r
ACT = mybir.ActivationFunctionType
ds = bass.ds

P = 128
T = 512
NB = T // P
D = 1024
DC = D // P
GW = 2 * D
GC = GW // P
F = 2816
FC = F // P
NH, DH = 16, 64
MH, MQK, MV = 4, 128, 256
AH = 8
IH = 8
TOPK = 128
DPLE = 256
EPS = 1e-6
NEG = -1e30
TAKEN = -3e38
COLS = 256
KU = 4
RING = 4
REL_BUCKETS, REL_MAX_DIST = 32, 128
ADA_PE = 2
ADA_SETUP = 8
ADA_PAIRS = ADA_SETUP - 2
ADA_STEPS = 56
DOWN_STEP, DOWN_FROM, DOWN_EVERY = 46, 24, 6
IX_STEP = 6
IX_CHUNKS = 2
V_PART = 4
UROW = 640

O_MQ, O_MV, O_MO, O_MZ = 0, 1024, 2048, 3072
O_IF, O_AQ, O_AV, O_AZ, O_IXQ, O_IXK, O_IXW = 4096, 4104, 5128, 5640, 6152, 6664, 6728


def distance_buckets():
    dist = np.maximum(T - 1 - np.arange(UROW), 0)
    exact = REL_BUCKETS // 2
    ratio = np.maximum(dist, 1).astype(np.float32) / np.float32(exact)
    scale = np.float32(np.log(REL_MAX_DIST / exact))
    large = exact + (np.log(ratio) / scale * np.float32(REL_BUCKETS - exact)).astype(np.int32)
    bucket = np.where(dist < exact, dist, np.minimum(large, REL_BUCKETS - 1))
    return (bucket[None, :] == np.arange(REL_BUCKETS)[:, None]).astype(np.float32)


class Stage:

    def __init__(self, name, iters, kchunks, reader, token_major=False, second=None):
        self.name, self.iters, self.reader, self.token_major = name, iters, reader, token_major
        def units(k):
            return [(a, min(KU, k - a)) for a in range(0, k, KU)]
        self.units = [units(kchunks), units(second or kchunks)]
        self.kchunks = [kchunks, second or kchunks]
        self.per_body = len(self.units[0]) + len(self.units[1])
        self.groups = 2 * iters


STAGES = [
    Stage("mlp_u", 4, DC, "act"), Stage("mlp_v", 4, DC, "dve", True), Stage("mlp_out", 2, GC, "dve", True),
    Stage("gu0", 11, DC, "dve"), Stage("down0", 2, FC, "dve", True),
    Stage("k", 2, DC, "act"), Stage("v", 2, DC, "act", True), Stage("q", 2, DC, "act"),
    Stage("gate", 2, DC, "act"), Stage("fox_out", 2, DC, "dve", True),
    Stage("gu1", 11, DC, "dve"), Stage("down1", 2, FC, "dve", True),
    Stage("ixq", 1, DC, "act"), Stage("mqk", 2, DC, "act"), Stage("mv", 2, DC, "act", True),
    Stage("aqk", 2, DC, "act"), Stage("av", 1, DC, "act", True),
    Stage("mo", 2, DC, "act"), Stage("mz", 2, DC, "act"), Stage("az", 1, DC, "act"),
    Stage("mix_out", 2, 12, "dve", True), Stage("ple", 4, DC, "dve", True, second=DPLE // P),
]


def number_stages():
    unit = group = 0
    count = {"act": 0, "dve": 0}
    for s in STAGES:
        s.unit0, s.group0, s.read0 = unit, group, count[s.reader]
        unit += s.per_body * s.iters
        group += s.groups
        count[s.reader] += s.groups
        assert unit % RING == 0 and group % 2 == 0
    return {s.name: s for s in STAGES}


def build_program(nc, io):
    S = number_stages()
    ctx = ExitStack()
    with ctx:
        def sem(name):
            return ctx.enter_context(nc.semaphore(name))

        base = 16512
        cursor = [base]

        def place(name, shape, dt=F32, at=None):
            size = int(np.prod(shape[1:])) * 4
            if at is None:
                at = cursor[0]
                cursor[0] += (size + 31) // 32 * 32
            return nc.alloc_sbuf_tensor_at(name, shape, dt, offset=at)

        K = 1024
        ring_at = cursor[0]
        raw = place("raw", [P, RING, KU, COLS])
        w_lo = place("w_lo", [P, RING, KU, COLS], F32R, at=ring_at)
        w_hi = place("w_hi", [P, RING, KU, COLS], F32R)
        x_tok = place("x_tok", [P, NB, D])
        h_at = cursor[0]
        hh = place("hh", [P, DC, T], F32R)
        hl = place("hl", [P, DC, T], F32R)
        y_h = place("y_h", [P, NB, D], at=h_at)
        ident = place("ident", [P, P])
        tri = place("tri", [P, P])
        tri_t = place("tri_t", [P, P])
        ones = place("ones", [P, P])
        head_ones = place("head_ones", [P, P])
        par_a = place("par_a", [P, 112])
        par_b = place("par_b", [P, 112])
        par_c = place("par_c", [P, 80])
        mod = place("mod", [P, 112])
        gain_at = cursor[0]
        gain_row = place("gain_row", [P, D])
        square_sum = place("square_sum", [P, 5, NB])
        scol = place("scol", [P, 8])
        bcol = place("bcol", [P, 8])
        c_act = place("c_act", [P, 8])
        eps = place("eps", [P, 1])
        qgain = place("qgain", [P, 1])
        small = place("small", [P, 8])
        warm = place("warm", [P, 1])
        ln_shift = place("ln_shift", [P, NB])
        stat_at = cursor[0]
        stats = place("stats", [P, NB, 8, 6])
        m_stat = place("m_stat", [P, 5, MH, NB], at=stat_at)
        moments = place("moments", [P, NB, 2])
        sq_at = cursor[0]
        sq = place("sq", [P, 2, T])
        inv_diag = place("inv_diag", [P, NB, P])
        gate_row = place("gate_row", [P, T])
        tmp = place("tmp", [P, 4, T])
        ada_acc = place("ada_acc", [P, 2, COLS])
        iw = place("iw", [P, NB, IH])
        mt = place("mt", [P, 2, NB, MH])
        kvbf = place("kvbf", [16, 1])
        bgate = place("bgate", [MH, 2])
        rel = place("rel", [REL_BUCKETS, AH])
        best = place("best", [P, 8])
        spacer = place("spacer", [P, 8])
        negmax = place("negmax", [P, 2, NB])
        rowsum = place("rowsum", [P, 2, NB])
        rowinv = place("rowinv", [P, 2, NB])
        sel = place("sel", [MH, MH, P])
        ph = cursor[0]
        room = 229344 - ph
        assert room >= 98 * K, room

        ada_raw = place("ada_raw", [P, 2, KU, COLS], at=ph + 88 * K)
        u = place("u", [P, GC, T], at=ph)
        y_hi = place("y_hi", [P, GC, T], F32R, at=ph)
        y_lo = place("y_lo", [P, GC, T], F32R, at=h_at)
        v = place("v", [P, NB, GW], at=ph + 32 * K)
        ada_first = place("ada_first", [P, ADA_PE, DC, COLS], at=ph)
        ada_next = place("ada_next", [P, ADA_SETUP - ADA_PE, DC, COLS], at=ph + 32 * K)
        ada_setup = place("ada_setup", [P, ADA_PAIRS - ADA_PE, COLS], at=ph + 82 * K)
        x_first = place("x_first", [P, DC, T], at=ph + 16 * K)
        ws_raw = place("ws_raw", [P, 16, P], at=ph + 48 * K)
        y_mlp = place("y_mlp", [P, NB, D], at=ph + 32 * K)
        ws_t = place("ws_t", [P, 16, P], at=ph + 64 * K)
        b_in = place("b_in", [P, GW], at=ph + 72 * K)
        q_bias = place("q_bias", [P, 16, P], at=ph + 80 * K)
        rows = place("rows", [P, 3, P], at=ph + 80 * K)
        c_row = place("c_row", [DC, P], at=ph + 81 * K + K // 2)
        act_hi = place("act_hi", [P, FC, T], F32R, at=ph)
        act_lo = place("act_lo", [P, FC, T], F32R, at=ph + 44 * K)
        x_scaled = place("x_scaled", [P, NB, D], at=ph + 64 * K)
        k_fox = place("k_fox", [P, DC, T], at=ph)
        q_fox = place("q_fox", [P, DC, T], at=ph + 16 * K)
        v_fox = place("v_fox", [P, NB, D], at=ph + 32 * K)
        gate = place("gate", [P, DC, T], at=ph + 48 * K)
        fx = {
            "rb": place("fox_rb", [P, 2, T], at=ph + 64 * K), "mb": place("fox_mb", [P, 2, 1280], at=ph + 68 * K),
            "mask": place("fox_mask", [P, 1280], at=ph + 78 * K),
            "qz": place("fox_qz", [P, 2, T], at=ph + 94 * K),
            "o": place("fox_o", [P, NB, D], at=h_at),
            "p": place("fox_p", [P, 2, 1280], at=h_at + 16 * K), "pT": place("fox_pT", [P, 1280], at=h_at + 26 * K),
        }
        gl_f = place("gl_f", [16, 5, T], at=ph + 83 * K)
        wf_raw = place("wf_raw", [P, DC, P], at=ph + 68 * K)
        wf_lo = place("wf_lo", [P, DC, P], F32R, at=ph + 68 * K)
        wf_hi = place("wf_hi", [P, DC, P], F32R, at=ph + 72 * K)
        og_hi = place("og_hi", [P, DC, T], F32R, at=ph)
        og_lo = place("og_lo", [P, DC, T], F32R, at=ph + 16 * K)
        y_fox = place("y_fox", [P, NB, D], at=ph + 32 * K)
        x_kept = place("x_kept", [P, DC, T], at=ph + 48 * K)
        mq = place("mq", [P, MH, T], at=ph)
        mk = place("mk", [P, MH, T], at=ph + 8 * K)
        mv = place("mv", [P, NB, MH, MV + 1], at=ph + 16 * K)
        ogate = place("ogate", [P, DC, T], at=ph + 34 * K)
        ixq = place("ixq", [P, 4, T], at=ph + 34 * K)
        ixk = place("ixk", [P, T], at=ph + 42 * K)
        aq = place("aq", [P, 4, T], at=ph + 50 * K)
        ak = place("ak", [P, 4, T], at=ph + 58 * K)
        av = place("av", [P, NB, AH * 64], at=ph + 66 * K)
        az = place("az", [P, 4, T], at=ph + 74 * K)
        dmask = place("dmask", [P, 1280], at=ph + 82 * K)
        score = place("score", [P, 1152], at=ph + 87 * K)
        p_in = place("p_in", [P, NB, DPLE], at=ph + 82 * K)
        XW, X_IF, X_FG, X_IW = 2 * P, P, P + 32, P + 64
        xw_raw = place("xw_raw", [P, DC, XW], at=ph)
        xw_lo = place("xw_lo", [P, DC, XW], F32R, at=ph)
        xw_hi = place("xw_hi", [P, DC, XW], F32R, at=ph + 87 * K)
        xpad = place("xpad", [P, 2, 516], at=ph + 87 * K + 4608)
        m_e = place("m_e", [P, 1280], at=ph + 92 * K)
        m_s = place("m_s", [P, 2, 1280], at=h_at + 5 * K + K // 2)
        hm = place("hm", [P, NB, MH * MV], at=h_at + 16 * K)
        dx = {
            "rb": place("dsa_rb", [P, 2, T], at=gain_at), "mb": place("dsa_mb", [P, 2, 1280], at=ph + 87 * K),
            "p": place("dsa_p", [P, 2, 1280], at=ph + 16 * K), "pT": place("dsa_pT", [P, 1280], at=ph + 26 * K),
            "qz": place("dsa_qz", [P, 2, T], at=sq_at),
            "o": place("dsa_o", [P, NB, AH * 64], at=h_at + 8 * K), "mask": dmask,
        }
        mix_hi = place("mix_hi", [P, 12, T], F32R, at=ph)
        mix_lo = place("mix_lo", [P, 12, T], F32R, at=ph + 50 * K)
        pt_hi = place("pt_hi", [P, 2, T], F32R, at=ph + 24 * K)
        pt_lo = place("pt_lo", [P, 2, T], F32R, at=ph + 28 * K)
        row_u = place("row_u", [AH, UROW], at=ph + 92 * K)
        one_hot = place("one_hot", [REL_BUCKETS, UROW], at=ph + 44 * K)

        acc = ctx.enter_context(nc.psum_tensor("acc", [P, 2, 2, T], F32))
        ms = ctx.enter_context(nc.psum_tensor("ms", [P, T], F32))
        ada_ps = ctx.enter_context(nc.psum_tensor("ada_ps", [P, T], F32))
        aux = ctx.enter_context(nc.psum_tensor("aux", [P, 2, T], F32))

        landed = [sem(f"w_landed{s}") for s in range(RING)]
        w_split_hi = sem("w_split_hi")
        w_split = sem("w_split")
        w_used = sem("w_used")
        acc_read = {"act": sem("acc_read_act"), "dve": sem("acc_read_dve")}
        ada_first_in = [sem(f"ada_first_in{s}") for s in range(ADA_PE)]
        ada_next_in = [sem(f"ada_next_in{s}") for s in range(ADA_SETUP - ADA_PE)]
        ada_landed = [sem("ada_landed0"), sem("ada_landed1")]
        c_in, c_ps, ada_setup_ready, kept_ready = sem("c_in"), sem("c_ps"), sem("ada_setup_ready"), sem("kept_ready")
        xstd_ready, xinv_ready, xn_dve, xn_act = (sem(n) for n in ("xstd_ready", "xinv_ready", "xn_dve", "xn_act"))
        par_in, x_landed, ws_in, b_in_in, q_bias_in, gates_in = (sem(n) for n in (
            "par_in", "x_landed", "ws_in", "b_in_in", "q_bias_in", "gates_in"))
        wf_in, fox_nd_out, xw_in, one_hot_in, rel_u_out, p_landed = (sem(n) for n in (
            "wf_in", "fox_nd_out", "xw_in", "one_hot_in", "rel_u_out", "p_landed"))
        stored, consts, par_t, par_ok, c_ok, xt_ps = (sem(n) for n in (
            "stored", "consts", "par_t", "par_ok", "c_ok", "xt_ps"))
        x_ready, ada_used, ada_ready, ada_sum, ada_col, sq_ready = (sem(n) for n in (
            "x_ready", "ada_used", "ada_ready", "ada_sum", "ada_col", "sq_ready"))
        sum_ready, std_ready, t_ready, h_hi, h_ready = (sem(n) for n in (
            "sum_ready", "std_ready", "t_ready", "h_hi", "h_ready"))
        sg_ready, a_hi, act_ready, ws_masked, wst_ps, wst_ready = (sem(n) for n in (
            "sg_ready", "a_hi", "act_ready", "ws_masked", "wst_ps", "wst_ready"))
        v_added, v_gelu, ln_moments, ln_std, v_norm, r_ps = (sem(n) for n in (
            "v_added", "v_gelu", "ln_moments", "ln_std", "v_norm", "r_ps"))
        r_read, mix_ps, mix_read, hsq_ready, hs_ps, hstd = (sem(n) for n in (
            "r_read", "mix_ps", "mix_read", "hsq_ready", "hs_ps", "hstd"))
        kq_ready, sw_zero, sw_split_hi, sw_split, f_ps, f_read = (sem(n) for n in (
            "kq_ready", "sw_zero", "sw_split_hi", "sw_split", "f_ps", "f_read"))
        ls_abs, ls_log, fox_d_ready, og_ps = (sem(n) for n in (
            "ls_abs", "ls_log", "fox_d_ready", "og_ps"))
        xw_ps, xw_read, iw_ps, ix_ps, ix_relu, ix_added = (sem(n) for n in (
            "xw_ps", "xw_read", "iw_ps", "ix_ps", "ix_relu", "ix_added"))
        xpad_zero, xpad_ready, conv_ready, conv_used, u_ps = (sem(n) for n in (
            "xpad_zero", "xpad_ready", "conv_ready", "conv_used", "u_ps"))
        row_u_ready, dmask_ready, mz_ready, ogate_ready, fg_ready, em_ready = (sem(n) for n in (
            "row_u_ready", "dmask_ready", "mz_ready", "ogate_ready", "fg_ready", "em_ready"))
        mt_ps, mt_ready, mk_scaled, gb_ps, gb_ready, qk_ps = (sem(n) for n in (
            "mt_ps", "mt_ready", "mk_scaled", "gb_ps", "gb_ready", "qk_ps"))
        m_e_ready, m_s_ready, num_ps, r_ready, hm_sq, hm_ready = (sem(n) for n in (
            "m_e_ready", "m_s_ready", "num_ps", "r_ready", "hm_sq", "hm_ready"))
        mix_t, p_t, bdiag_ready, gain_ps, out_ready, hm_std, hm_scaled, diag_ready, ada_first_ps, v_norm_act, ln_ready, gain_ready = (sem(n) for n in (
            "mix_t", "p_t", "bdiag_ready", "gain_ps", "out_ready", "hm_std", "hm_scaled", "diag_ready", "ada_first_ps", "v_norm_act", "ln_ready", "gain_ready"))
        for kind, a in (("fox", fx), ("dsa", dx)):
            a["rb_in"] = [sem(f"{kind}_rb_in{e}") for e in range(2)]
            for n in ("mb_ready", "staged", "s_ps", "lg_ready", "e_ready", "t_ps", "pt_act", "pt_dve", "o_ps", "o_read", "sum_read", "zeroed"):
                a[n] = sem(f"{kind}_{n}")
        fx.update(q=q_fox, k=k_fox, v=v_fox, pairs=NH // 2, toeplitz=False, qz_free=(f_ps, 1), mb_free=None)
        dx.update(q=aq, k=ak, v=av, pairs=AH // 2, toeplitz=True, qz_free=(mt_ps, 1), mb_free=(m_s_ready, MH + 1))

        block = ctx.enter_context(nc.Block())

        def times(eng, n, body, unroll=False):
            if n <= 1 or unroll:
                for i in range(n):
                    body(i)
            else:
                with eng.Fori(0, n) as i:
                    body(i)

        def unit_no(st, i, j, x):
            return st.unit0 + i * st.per_body + (len(st.units[0]) if j else 0) + x

        def slot_of(st, i, j, x):
            n = unit_no(st, i if isinstance(i, int) else 0, j, x)
            return n % RING

        def load_unit(sp, st, src, i, j, x):
            n, s, (k0, nk) = unit_no(st, i, j, x), slot_of(st, i, j, x), st.units[j][x]
            sp.wait_ge(w_used, n + 1)
            for dst, ap in src(i, j, k0, nk, raw[:, s, 0:nk, :]):
                sp.dma_start(dst, ap).then_inc(landed[s], 16)

        def columns(w, c0, step):
            def src(i, j, k0, nk, dst):
                c = c0 + step * 2 * i + step * j
                return [(dst, w[k0 * P:(k0 + nk) * P, ds(c, COLS)].rearrange("(k p) n -> p k n", p=P))]
            return src
        src_of = {}

        def gu_src(w):
            wv = w.rearrange("(k p) (a f) -> p k a f", p=P, a=2)
            def src(i, j, k0, nk, dst):
                f0 = 256 * i + 128 * j
                return [(dst.rearrange("p k (a f) -> p k a f", a=2)[:, :, a, :], wv[:, k0:k0 + nk, a, ds(f0, P)])
                        for a in range(2)]
            return src
        a_w_in, w2 = io["a_w_in"][0], io["w_in_2"][0]
        src_of["mlp_u"], src_of["mlp_v"] = columns(a_w_in, 0, COLS), columns(a_w_in, GW, COLS)
        src_of["mlp_out"] = columns(io["a_w_out"][0], 0, COLS)
        for l in range(2):
            src_of[f"gu{l}"] = gu_src(io["ffn_w_gu"][l])
            src_of[f"down{l}"] = columns(io["ffn_w_down"][l], 0, COLS)
        src_of["k"], src_of["v"] = columns(io["kv_w"], 0, COLS), columns(io["kv_w"], D, COLS)
        src_of["q"], src_of["gate"] = columns(io["b_w_qg"][0], 0, COLS), columns(io["b_w_qg"][0], D, COLS)
        src_of["fox_out"] = columns(io["b_w_o"][0], 0, COLS)
        for name, c0 in (("ixq", O_IXQ), ("mqk", O_MQ), ("mv", O_MV), ("aqk", O_AQ), ("av", O_AV), ("mo", O_MO),
                         ("mz", O_MZ), ("az", O_AZ)):
            src_of[name] = columns(w2, c0, COLS)
        src_of["mix_out"] = columns(io["w_out_2"][0], 0, COLS)

        def ple_src(i, j, k0, nk, dst):
            w = io["w_ple"][0] if j else io["w_ple_gate"][0]
            return [(dst, w[k0 * P:(k0 + nk) * P, ds(256 * i, COLS)].rearrange("(k p) n -> p k n", p=P))]
        src_of["ple"] = ple_src
        for st in STAGES:
            st.dmas = 2 if st.name.startswith("gu") else 1
        total = 0
        for st in STAGES:
            st.landed0 = total
            total += 16 * st.dmas * st.per_body * st.iters // RING

        def landed_value(st, i, j, x):
            at = (len(st.units[0]) if j else 0) + x
            if isinstance(i, int):
                rounds = (i * st.per_body + at) // RING
            else:
                rounds = i * (st.per_body // RING) + at // RING
            return (rounds + 1) * (16 * st.dmas) + st.landed0

        ada_w, kv_ada_w = io["ada_w"], io["kv_ada_w"]

        def ada_round(step):
            return step - ADA_SETUP

        def ada_load(sp, w, c0, step):
            n = ada_round(step)
            for half in range(2):
                sp.wait_ge(ada_used, 2 * n + half + 1)
                sp.dma_start(ada_raw[:, half], w[half * 512:half * 512 + 512, ds(c0, COLS)].rearrange("(k p) n -> p k n", p=P)) \
                    .then_inc(ada_landed[half], 16)

        def load_group(sp, name, i, j):
            st = S[name]
            for x in range(len(st.units[j])):
                load_unit(sp, st, src_of[name], i, j, x)

        def load_stage(sp, name, ada=None, unroll=False, skip=0):
            st = S[name]
            def group(i, j):
                load_group(sp, name, i, j)
                if ada:
                    ada(i, j)
            def body(i):
                group(i, 0)
                group(i, 1)
            if skip % 2:
                group(skip // 2, 1)
            first = (skip + 1) // 2
            if unroll or st.iters - first <= 1 or st.per_body % RING:
                for i in range(first, st.iters):
                    body(i)
            else:
                with sp.Fori(first, st.iters) as i:
                    body(i)

        CH = {"h0": 0, "y": 8, "h1": 24, "hkv": 32, "h2": 40, "og": 48, "h3": 56, "h4": 64, "mix": 72, "xg": 84, "pt": 92}

        XT = {"h0": 0, "h1": 8, "hkv": 16, "h3": 24, "h4": 32, "xg": 40}

        def done(st, i, j):
            return unit_no(st, i, j, len(st.units[j]) - 1) + 1 + RING

        def bank(b):
            return acc[:, b // 2, b % 2, :]
        XT_BANKS = [ms[:], aux[:, 0, :], aux[:, 1, :], bank(2), bank(3)]
        M_BANKS = [aux[:, 0, :], aux[:, 1, :], ada_ps[:], bank(3)]

        def qk_part(s):
            at, width = (0, 1, 2, 1)[s], P * (NB - s)
            return bank(at)[:, T - width:T] if s == NB - 1 else bank(at)[:, 0:width]
        XG_BANKS = [ms[:], ada_ps[:]]

        WIDTH = [P * (b + 1) for b in range(NB)]
        OFF = [sum(WIDTH[:b]) for b in range(NB)]
        TW = [P * (NB - s) for s in range(NB)]
        TOFF = [sum(TW[:s]) for s in range(NB)]
        T_BANKS = [(aux[:, 0, :], (0,)), (aux[:, 1, :], (1, 3)), (ada_ps, (2,))]
        PT_OFF = {0: 0, 1: T, 3: T + TW[1], 2: 2 * T}

        def attention_loop(eng, a, first, step, last):
            first()
            with eng.Fori(1, a["pairs"]) as i:
                step(i, 0)
                step(i, 1)
            last(2 * a["pairs"])

        def attention_sp(sp, a, source):
            def body(i):
                for e in range(2):
                    sp.wait_ge(a["mb_ready"], 2 * i + e + 1)
                    sp.dma_start(a["rb"][:, e, :], source(2 * i + e)).then_inc(a["rb_in"][e], 16)
            times(sp, a["pairs"], body, unroll=a["toeplitz"])

        def attention_pool(pool, a):
            pool.nop().then_inc(a["mb_ready"], 2)
            def body(i):
                for e in range(2):
                    h = 2 * i + e
                    pool.wait_ge(a["rb_in"][e], 16 * (i + 1))
                    pool.wait_ge(a["lg_ready"], 4 * h + 4)
                    if isinstance(h, int) and h == 1 and a["mb_free"]:
                        pool.wait_ge(*a["mb_free"])
                    for b in range(NB):
                        lo = (NB - 1 - b) * P if a["toeplitz"] else 0
                        last = pool.tensor_tensor(a["mb"][:, e, OFF[b]:OFF[b] + WIDTH[b]], a["rb"][:, e, lo:lo + WIDTH[b]],
                                                  a["mask"][:, OFF[b]:OFF[b] + WIDTH[b]], ALU.add)
                    last.then_inc(a["mb_ready"], 1)
            pool.wait_ge(*a["qz_free"])
            pool.drain()
            pool.memset(a["qz"][64:P, 0, :], 0.0)
            pool.memset(a["qz"][0:64, 1, :], 0.0).then_inc(a["zeroed"], 1)
            pool.drain()
            body(0)
            with pool.Fori(1, a["pairs"]) as i:
                body(i)

        def attention_act(act, a):
            act.nop().then_inc(a["pt_act"], 1)
            def stage(i):
                act.wait_ge(a["s_ps"], 8 * i + 1)
                for e in range(2):
                    half = slice(64 * e, 64 * e + 64)
                    act.activation(a["qz"][half, e, :].unsqueeze(1), a["q"][half, ds(i, 1), :], ACT.Copy).then_inc(a["staged"], 1)

            def exps(h, e):
                act.wait_ge(a["sum_read"], h + 1)
                for b in range(NB):
                    act.wait_ge(a["lg_ready"], 4 * h + b + 9)
                    part = a["p"][:, e, OFF[b]:OFF[b] + WIDTH[b]]
                    act.activation(part, part, ACT.Exp, bias=negmax[:, e, b:b + 1], scale=-1.0,
                                   accum_out=rowsum[:, e, b:b + 1]).then_inc(a["e_ready"], 1)

            def copy(h):
                act.wait_ge(a["o_ps"], h + 1)
                act.wait_ge(a["t_ps"], 3 * h + 8)
                act.activation(a["pT"][:, T:2 * T], T_BANKS[1][0], ACT.Copy).then_inc(a["pt_act"], 1)

            def first():
                stage(0)
                exps(0, 0)
                stage(1)
                exps(1, 1)
                copy(0)

            def step(i, e):
                h = 2 * i + e
                if e:
                    stage(i + 1)
                exps(h, e)
                copy(h - 1)

            first()
            with act.Fori(1, a["pairs"] - 1) as i:
                step(i, 0)
                step(i, 1)
            n = 2 * a["pairs"]
            exps(n - 2, 0)
            copy(n - 3)
            exps(n - 1, 1)
            copy(n - 2)
            copy(n - 1)

        def attention_pe(pe, a):
            pe.nop().then_inc(a["t_ps"], 6)
            pe.nop().then_inc(a["s_ps"], 1)
            pe.nop().then_inc(a["o_ps"], 1)
            def scores(i, e):
                h = 2 * i + e
                pe.wait_ge(a["staged"], 2 * i + e + 1)
                for b in range(NB):
                    pe.wait_ge(a["lg_ready"], 4 * h + b + 5)
                    pe.matmul(bank(b)[:, 0:WIDTH[b]], a["qz"][:, e, b * P:(b + 1) * P],
                              a["k"][:, ds(i, 1), 0:WIDTH[b]].rearrange("p a t -> p (a t)"),
                              start=True, stop=True).then_inc(a["s_ps"], 1)

            def transposes(h, e):
                pe.wait_ge(a["e_ready"], 4 * h + 4)
                for n, (out, blocks) in enumerate(T_BANKS):
                    if n == 1:
                        pe.wait_ge(a["pt_act"], h + 1)
                    else:
                        pe.wait_ge(a["pt_dve"], 2 * h + 1 + n // 2)
                    c = 0
                    for s in blocks:
                        for b in range(s, NB):
                            last = pe.transpose(out[:, c:c + P], a["p"][:, e, OFF[b] + s * P:OFF[b] + (s + 1) * P], ident[:])
                            c += P
                    last.then_inc(a["t_ps"], 1)

            def values(h):
                pe.wait_ge(a["pt_act"], h + 2)
                pe.wait_ge(a["pt_dve"], 2 * h + 4)
                pe.wait_ge(a["o_read"], h + 2)
                for b in range(NB):
                    for s in range(b + 1):
                        c = PT_OFF[s] + (b - s) * P
                        last = pe.matmul(ms[:, b * 64:b * 64 + 64], a["pT"][:, c:c + P], a["v"][:, s, ds(h * 64, 64)],
                                         start=s == 0, stop=s == b)
                last.then_inc(a["o_ps"], 1)

            def first():
                pe.wait_ge(a["zeroed"], 1)
                scores(0, 0)
                scores(0, 1)
                transposes(0, 0)

            def step(i, e):
                scores(i, e)
                values(2 * i + e - 2)
                transposes(2 * i + e - 1, 1 - e)

            def last(n):
                values(n - 2)
                transposes(n - 1, 1)
                values(n - 1)
            attention_loop(pe, a, first, step, last)

        def attention_dve(dve, a):
            dve.nop().then_inc(a["lg_ready"], 8)
            dve.nop().then_inc(a["pt_dve"], 2)
            dve.nop().then_inc(a["o_read"], 2)
            dve.nop().then_inc(a["sum_read"], 2)
            def soft(h, e):
                dve.wait_ge(a["mb_ready"], h + 3)
                dve.wait_ge(a["t_ps"], 3 * h + 3)
                for b in range(NB):
                    dve.wait_ge(a["s_ps"], 4 * h + b + 2)
                    dve.memset(spacer[:, 4 * e + b:4 * e + b + 1], 0.0)
                    part = slice(OFF[b], OFF[b] + WIDTH[b])
                    dve.tensor_tensor_reduce(a["p"][:, e, part], bank(b)[:, 0:WIDTH[b]], a["mb"][:, e, part], -1.0, 3e38,
                                             ALU.add, ALU.min, negmax[:, e, b:b + 1]).then_inc(a["lg_ready"], 1)

            def copies(h, e):
                dve.wait_ge(a["o_ps"], h + 1)
                for n, s in ((0, 0), (2, 2)):
                    dve.wait_ge(a["t_ps"], 3 * h + 7 + n)
                    dve.tensor_copy(a["pT"][:, PT_OFF[s]:PT_OFF[s] + TW[s]], T_BANKS[n][0][:, 0:TW[s]]).then_inc(a["pt_dve"], 1)
                dve.reciprocal(rowinv[:, e, :], rowsum[:, e, :]).then_inc(a["sum_read"], 1)
                dve.drain()

            def outputs(h, e):
                dve.wait_ge(a["o_ps"], h + 2)
                dve.tensor_tensor(a["o"][:, :, ds(h * 64, 64)], ms[:, 0:NB * 64].rearrange("p (b d) -> p b d", b=NB),
                                  rowinv[:, e, :].unsqueeze(2).broadcast_to([P, NB, 64]), ALU.mult).then_inc(a["o_read"], 1)

            def first():
                soft(0, 0)
                soft(1, 1)
                copies(0, 0)

            def step(i, e):
                h = 2 * i + e
                soft(h, e)
                outputs(h - 2, e)
                copies(h - 1, 1 - e)

            def last(n):
                outputs(n - 2, 0)
                copies(n - 1, 1)
                outputs(n - 1, 1)
            attention_loop(dve, a, first, step, last)
        def lead(eng, name, split, epilogue, following, unroll=False):
            st = S[name]
            def body(i):
                split(eng, st, i, 1)
                epilogue(st, i, 0)
                split(eng, st, i + 1, 0)
                epilogue(st, i, 1)
            times(eng, st.iters - 1, body, unroll or st.per_body % RING != 0)
            split(eng, st, st.iters - 1, 1)
            epilogue(st, st.iters - 1, 0)
            if following:
                split(eng, S[following], 0, 0)
            epilogue(st, st.iters - 1, 1)

        def lead_ple(eng, split, epilogue):
            st = S["ple"]
            for i in range(st.iters):
                split(eng, st, i, 1)
                if i + 1 < st.iters:
                    split(eng, st, i + 1, 0)
                epilogue(st, i, 0)
                epilogue(st, i, 1)

        def split_hi(act, st, i, j, units=slice(None)):
            for x, (_, nk) in list(enumerate(st.units[j]))[units]:
                s = slot_of(st, i, j, x)
                act.wait_ge(landed[s], landed_value(st, i, j, x))
                act.activation(w_hi[:, s, 0:nk, :], raw[:, s, 0:nk, :], ACT.Copy).then_inc(w_split_hi, 1)

        def split_lo(pool, st, i, j, units=slice(None)):
            for x, (_, nk) in list(enumerate(st.units[j]))[units]:
                s = slot_of(st, i, j, x)
                pool.wait_ge(w_split_hi, unit_no(st, i, j, x) + 1)
                pool.tensor_tensor(w_lo[:, s, 0:nk, :], raw[:, s, 0:nk, :], w_hi[:, s, 0:nk, :].bitcast(F32),
                                   ALU.subtract).then_inc(w_split, 1)

        def wait_sums(eng, st, i, j):
            eng.wait_ge(w_used, done(st, i, j))

        def sums(j):
            return acc[:, j]

        def sums_tok(j):
            return acc[:, j].rearrange("p a (b n) -> p (a b) n", b=2)

        @block.sync
        def _(sp):
            sp.dma_start(c_row[:], io["c"][0].rearrange("(k p) -> k p", p=P)).then_inc(c_in, 16)
            def whole_step(dst, s, landed_sem):
                sp.dma_start(dst, ada_w[0][:, COLS * s:COLS * (s + 1)].rearrange("(k p) n -> p k n", p=P)).then_inc(landed_sem, 16)
            def next_step(s):
                whole_step(ada_next[:, s], ADA_PE + s, ada_next_in[s])
            next_step(0)
            whole_step(ada_first[:, 0], 0, ada_first_in[0])
            next_step(1)
            sp.dma_start(x_tok[:], io["x"][0].rearrange("(b p) d -> p b d", p=P)).then_inc(x_landed, 16)
            for s in range(1, ADA_PE):
                whole_step(ada_first[:, s], s, ada_first_in[s])
            sp.wait_ge(x_landed, 16)
            for s in range(2, ADA_SETUP - ADA_PE):
                next_step(s)
            load_group(sp, "mlp_u", 0, 0)
            load_group(sp, "mlp_u", 0, 1)
            sp.wait_ge(ada_ready, ADA_SETUP - ADA_PAIRS)
            sp.dma_start(ws_raw[:], io["a_w_s"][0].rearrange("g t s -> t g s")).then_inc(ws_in, 16)
            sp.dma_start(b_in[:], io["a_b_in"][0:1, GW:2 * GW].broadcast_to([P, GW])).then_inc(b_in_in, 16)
            sp.wait_ge(par_t, 3)
            sp.wait_ge(ada_first_ps, 1)
            sp.dma_start(q_bias[:].rearrange("p g t -> p (g t)"),
                         io["a_b_s"][0].rearrange("g t -> (g t)").rearrange("(a n) -> a n", a=1).broadcast_to([P, GW])) \
                .then_inc(q_bias_in, 16)
            def par(dst, src, s):
                sp.dma_start(dst, src).then_inc(s, 16)
            par(kvbf[:], io["kv_b_f"].rearrange("(h a) -> h a", a=1), gates_in)
            for a in range(2):
                par(bgate[:, a:a + 1], io["b_gate_2"][0, a * MH:(a + 1) * MH].rearrange("(h a) -> h a", a=1), gates_in)
            par(rel[:], io["rel_bias_2"], gates_in)
            for j in range(2):
                ada_load(sp, ada_w[0], COLS * (8 + j), 8 + j)
            load_stage(sp, "mlp_u", lambda i, j: ada_load(sp, ada_w[0], COLS * (8 + 2 * i + j), 8 + 2 * i + j), skip=2)
            load_stage(sp, "mlp_v", lambda i, j: ada_load(sp, ada_w[0], COLS * (16 + 2 * i + j), 16 + 2 * i + j))
            load_stage(sp, "mlp_out")
            KV0, KV1 = 24, 32
            for i in range((KV1 - KV0) // 2):
                for j in range(2):
                    load_group(sp, "gu0", i, j)
                    ada_load(sp, kv_ada_w, COLS * (2 * i + j), KV0 + 2 * i + j)
            def layer1(i, j):
                ada_load(sp, ada_w[1], COLS * (KV0 - KV1 + 2 * i + j), KV0 + 2 * i + j)
            load_stage(sp, "gu0", layer1, skip=KV1 - KV0)
            st, step = S["down0"], DOWN_STEP
            for g in range(st.groups):
                for x, (k0, nk) in enumerate(st.units[g % 2]):
                    load_unit(sp, st, src_of["down0"], g // 2, g % 2, x)
                    if step < ADA_STEPS and g * FC + k0 + nk >= DOWN_FROM + KU + DOWN_EVERY * (step - DOWN_STEP):
                        ada_load(sp, ada_w[1], COLS * (step - KV1), step)
                        step += 1
            load_stage(sp, "k")
            sp.wait_ge(sw_zero, 1)
            sp.dma_start(wf_raw[:, :, 0:NH], io["kv_w"][:, 2 * D:2 * D + NH].rearrange("(k p) n -> p k n", p=P)).then_inc(wf_in, 16)
            for name in ("v", "q", "gate"):
                load_stage(sp, name)
            sp.wait_ge(fox_d_ready, 1)
            sp.dma_start(io["fox_nd"], gl_f[:, 4, :]).then_inc(fox_nd_out, 16)
            sp.wait_ge(fox_nd_out, 16)
            load_group(sp, "fox_out", 0, 0)
            attention_sp(sp, fx, lambda h: io["fox_nd"][ds(h, 1), :].broadcast_to([P, T]))
            load_stage(sp, "fox_out", skip=1)
            load_stage(sp, "gu1")
            load_stage(sp, "down1")
            load_group(sp, "ixq", 0, 0)
            sp.wait_ge(sw_zero, 2)
            for c, o, n in ((0, O_IXK, 64), (64, O_IXK, 64), (X_IF, O_IF, MH), (X_FG, O_IF + MH, MH), (X_IW, O_IXW, IH)):
                sp.dma_start(xw_raw[:, :, c:c + n], w2[:, o:o + n].rearrange("(k p) n -> p k n", p=P)).then_inc(xw_in, 16)
            load_stage(sp, "ixq", skip=1)
            sp.dma_start(one_hot[:], io["one_hot"]).then_inc(one_hot_in, 16)
            for name in ("mqk", "mv", "aqk", "av", "mo"):
                load_stage(sp, name)
            sp.wait_ge(row_u_ready, 1)
            sp.dma_start(io["rel_u"], row_u[:].unsqueeze(1).broadcast_to([AH, P, UROW])).then_inc(rel_u_out, 16)
            for name in ("mz", "az"):
                load_stage(sp, name)
            load_group(sp, "mix_out", 0, 0)
            sp.wait_ge(rel_u_out, 16)
            sp.wait_ge(dmask_ready, 1)
            attention_sp(sp, dx, lambda h: bass.AP(io["rel_u"].tensor, h * P * UROW + P - 1, [[UROW - 1, P], [1, T]]))
            load_stage(sp, "mix_out", skip=1)
            sp.wait_ge(dx["lg_ready"], 4 * AH + 8)
            sp.dma_start(p_in[:], io["p_2"][0, 0].rearrange("(b p) d -> p b d", p=P)).then_inc(p_landed, 16)
            sp.wait_ge(x_ready, 16)
            sp.dma_start(gain_row[:], io["norm_final_2"].rearrange("(a d) -> a d", a=1).broadcast_to([P, D])).then_inc(p_landed, 16)
            load_stage(sp, "ple")
            for b in range(NB):
                sp.wait_ge(out_ready, b + 1)
                sp.dma_start(io["out"][0, b * P:(b + 1) * P, :], x_tok[:, b, :]).then_inc(stored, 16)
            sp.wait_ge(stored, 16 * NB)

        @block.scalar
        def _(act):
            act.nop().then_inc(acc_read["act"], 2)
            def rows128(a):
                return a.rearrange("(j p) -> j p", p=P)

            def par(dst, src):
                act.dma_start(dst, src).then_inc(par_in, 16)

            for r, name in ((0, "pre_mix_g"), (16, "post_mix_g"), (32, "pre_ffn_g"), (48, "post_ffn_g")):
                par(rows[r:r + 16, 1, :], io[name].rearrange("l (j p) -> (l j) p", p=P))
            act.wait_ge(c_ps, 1)
            act.activation(c_act[:], aux[:, 0, 0:DC], ACT.Silu).then_inc(c_ok, 1)
            for r, a in ((64, io["kv_norm_g"]), (72, io["norm_in_2"][0]), (80, io["norm_final_2"]),
                         (88, io["a_b_in"][0, 0:GW])):
                par(rows[r:r + a.shape[0] // P, 1, :], rows128(a))
            for r, a in ((0, io["ada_b"][0]), (48, io["kv_ada_b"]), (64, io["ada_b"][1])):
                par(rows[r:r + a.shape[0] // P, 0, :], rows128(a))
            par(rows[0:32, 2, :], io["conv_w_2"][0].rearrange("w (j p) -> (w j) p", p=P))
            for half in range(2):
                par(rows[32:33, 2, half * 64:half * 64 + 64], io["k_norm_g"].rearrange("(a d) -> a d", a=1))
                par(rows[33:34, 2, half * 64:half * 64 + 64], io["b_q_norm_g"])
            for r, a in ((34, io["a_ln_g"][0]), (50, io["a_ln_b"][0]), (66, io["m_norm_2"][0])):
                par(rows[r:r + a.shape[0] // P, 2, :], rows128(a))

            junk = sq[:].rearrange("p a t -> p (a t)")

            def block_squares(b):
                act.activation(junk, x_tok[:, b, :], ACT.Square, accum_out=square_sum[:, 4, b:b + 1])
                act.drain()

            def norm_x(n):
                for half in range(2):
                    blocks = slice(2 * half, 2 * half + 2)
                    for b in range(2 * half, 2 * half + 2):
                        act.wait_ge(x_ready, NB * n + b + 1)
                        block_squares(b)
                    act.activation(small[:, blocks], square_sum[:, 4, blocks], ACT.Sqrt, bias=eps[:], scale=1.0 / D).then_inc(xstd_ready, 1)
                act.wait_ge(xinv_ready, n + 1)
                for b in range(NB // 2, NB):
                    act.activation(x_scaled[:, b, :], x_tok[:, b, :], ACT.Copy, scale=small[:, 4 + b:5 + b]).then_inc(xn_act, 1)

            def squares_of_group(src, g):
                for b in range(NB):
                    act.activation(junk[:, b * COLS:(b + 1) * COLS], src[:, b, :], ACT.Square, accum_out=square_sum[:, g, b:b + 1])
                    if b % 2:
                        act.drain()
                        act.nop().then_inc(sq_ready, 1)

            def deviation(n):
                act.wait_ge(sum_ready, n + 1)
                act.activation(small[:, 0:NB], square_sum[:, 4, :], ACT.Sqrt, bias=eps[:], scale=1.0 / D).then_inc(std_ready, 1)

            def hi_chunks(name, n, hi, k0=0, free=None):
                for k in range(k0, k0 + n):
                    if free:
                        act.wait_ge(w_used, free(k))
                    c = CH[name] + k
                    act.wait_ge(t_ready, c + 1)
                    act.activation(hi[:, k, :], tmp[:, c % 4, :], ACT.Copy).then_inc(h_hi, 1)

            act.wait_ge(x_landed, 16)
            for b in range(NB):
                block_squares(b)
            act.activation(small[:, 0:NB], square_sum[:, 4, :], ACT.Sqrt, bias=eps[:], scale=1.0 / D).then_inc(std_ready, 1)
            for k in range(DC):
                act.wait_ge(xt_ps, k + 1)
                act.activation(x_first[:, k, :], XT_BANKS[k % len(XT_BANKS)], ACT.Copy).then_inc(kept_ready, 1)
            split_hi(act, S["mlp_u"], 0, 0)
            hi_chunks("h0", DC, hh)

            def epi_u(st, i, j):
                wait_sums(act, st, i, j)
                for m in range(2):
                    col = 4 * i + 2 * j + m
                    ins = act.activation(u[:, ds(col, 1), :], sums(j)[:, m:m + 1, :], ACT.Gelu_apprx_tanh,
                                         bias=par_b[:, ds(88 + col, 1)])
                ins.then_inc(acc_read["act"], 1)
            lead(act, "mlp_u", split_hi, epi_u, "mlp_v")

            def epi_v(st, i, j):
                act.wait_ge(v_added, 2 * i + j + 1)
                part = v[:, :, ds(COLS * (2 * i + j), COLS)]
                act.activation(part, part, ACT.Gelu_apprx_tanh).then_inc(v_gelu, 1)
            lead(act, "mlp_v", split_hi, epi_v, None)
            split_hi(act, S["mlp_out"], 0, 0, slice(0, 1))
            act.wait_ge(ln_moments, 1)
            act.activation(small[:, 0:NB], moments[:, :, 1], ACT.Sqrt, bias=eps[:]).then_inc(ln_std, 1)
            act.wait_ge(ln_ready, 1)
            for g in range(0, GC, V_PART):
                for b in range(NB // 2, NB):
                    part = v[:, b, g * P:(g + V_PART) * P]
                    act.activation(part, part, ACT.Identity, bias=ln_shift[:, b:b + 1], scale=small[:, 4 + b:5 + b]).then_inc(v_norm_act, 1)
            for x in range(GC // KU):
                hi_chunks("y", KU, y_hi, KU * x)
                split_hi(act, S["mlp_out"], 0, 0, slice(x + 1, x + 2))

            def output_epilogue():
                def epi(st, i, j):
                    if 2 * i + j == st.groups - 1:
                        act.activation(warm[:], eps[:], ACT.Sqrt)
                    wait_sums(act, st, i, j)
                    squares_of_group(sums_tok(j), 2 * i + j)
                return epi
            lead(act, "mlp_out", split_hi, output_epilogue(), None, unroll=True)
            deviation(0)
            split_hi(act, S["gu0"], 0, 0)
            norm_x(0)
            hi_chunks("h1", DC, hh)

            def gu_epilogue(st, i, j):
                wait_sums(act, st, i, j)
                act.wait_ge(acc_read["dve"], st.read0 + 2 * i + j + 1)
                act.activation(tmp[:, j, :], sums(j)[:, 0, :], ACT.Silu).then_inc(sg_ready, 1)
            lead(act, "gu0", split_hi, gu_epilogue, "down0")
            lead(act, "down0", split_hi, output_epilogue(), None, unroll=True)
            deviation(1)
            split_hi(act, S["k"], 0, 0)
            norm_x(1)
            hi_chunks("hkv", DC, hh)

            def head_norm_epilogue(dst, c0):
                def epi(st, i, j):
                    wait_sums(act, st, i, j)
                    c = c0 + 4 * i + 2 * j
                    if c >= 2:
                        act.wait_ge(hs_ps, c)
                    for m in range(2):
                        act.activation(sq[:, m, :], sums(j)[:, m, :], ACT.Square).then_inc(hsq_ready, 1)
                    t = 4 * i + 2 * j
                    act.activation(dst[:, t:t + 2, :], sums(j), ACT.Copy).then_inc(acc_read["act"], 1)
                    if c >= c0 + 2:
                        head_deviation(c - 2)
                return epi

            def head_deviation(c):
                for m in range(2):
                    act.wait_ge(hs_ps, c + m + 1)
                    if c >= 2:
                        act.wait_ge(kq_ready, c + m - 1)
                    act.activation(tmp[:, m, :], aux[:, m, :], ACT.Sqrt, bias=eps[:], scale=1.0 / DH).then_inc(hstd, 1)
            lead(act, "k", split_hi, head_norm_epilogue(k_fox, 0), "v", unroll=True)
            act.wait_ge(wf_in, 16)
            act.activation(wf_hi[:], wf_raw[:], ACT.Copy).then_inc(sw_split_hi, 1)

            def tokens_epilogue(dst):
                def epi(st, i, j):
                    wait_sums(act, st, i, j)
                    c = COLS * (2 * i + j)
                    act.activation(dst[:, :, c:c + COLS], sums_tok(j), ACT.Copy).then_inc(acc_read["act"], 1)
                return epi
            def log_sigmoid(ab, n):
                act.wait_ge(ls_abs, n)
                act.activation(ab, ab, ACT.Exp, scale=-1.0)
                act.drain()
                act.activation(ab, ab, ACT.Ln, bias=1.0).then_inc(ls_log, 1)
            def v_epilogue(st, i, j):
                if (i, j) == (1, 1):
                    log_sigmoid(gl_f[:, 1, :], 1)
                tokens_epilogue(v_fox)(st, i, j)
                if (i, j) == (0, 0):
                    head_deviation(6)
            lead(act, "v", split_hi, v_epilogue, "q", unroll=True)

            hi_chunks("h2", DC, hh, free=lambda k: S["q"].unit0 - (k < KU) + RING)
            lead(act, "q", split_hi, head_norm_epilogue(q_fox, 8), "gate", unroll=True)

            def func_epilogue(dst, func):
                def epi(st, i, j):
                    wait_sums(act, st, i, j)
                    t = 4 * i + 2 * j
                    act.activation(dst[:, t:t + 2, :], sums(j), func).then_inc(acc_read["act"], 1)
                return epi

            def gate_epilogue(st, i, j):
                func_epilogue(gate, ACT.Sigmoid)(st, i, j)
                if (i, j) == (0, 0):
                    head_deviation(14)
            lead(act, "gate", split_hi, gate_epilogue, "fox_out", unroll=True)
            act.wait_ge(kq_ready, 16)
            attention_act(act, fx)
            hi_chunks("og", DC, og_hi)
            lead(act, "fox_out", split_hi, output_epilogue(), None, unroll=True)
            deviation(2)
            split_hi(act, S["gu1"], 0, 0)
            norm_x(2)
            hi_chunks("h3", DC, hh)
            lead(act, "gu1", split_hi, gu_epilogue, "down1")
            lead(act, "down1", split_hi, output_epilogue(), None, unroll=True)
            deviation(3)
            split_hi(act, S["ixq"], 0, 0)
            norm_x(3)
            hi_chunks("h4", DC, hh)
            act.wait_ge(xw_in, 16 * 5)
            act.activation(xw_hi[:], xw_raw[:], ACT.Copy).then_inc(sw_split_hi, 1)

            def scaled_epilogue(dst, scale):
                def epi(st, i, j):
                    wait_sums(act, st, i, j)
                    t = 4 * i + 2 * j
                    act.activation(dst[:, t:t + 2, :], sums(j), ACT.Copy, scale=scale).then_inc(acc_read["act"], 1)
                return epi
            lead(act, "ixq", split_hi, scaled_epilogue(ixq, 64.0 ** -0.5), "mqk", unroll=True)

            def conv_epilogue(st, i, j):
                for n in range(IX_STEP * (2 * i + j), IX_STEP * (2 * i + j + 1)):
                    w = WIDTH[1 + n // IH]
                    act.wait_ge(ix_ps, n + 1)
                    if n >= 2:
                        act.wait_ge(ix_added, n - 1)
                    act.activation(tmp[:, n % 2, 0:w], aux[:, n % 2, 0:w], ACT.Relu).then_inc(ix_relu, 1)
                wait_sums(act, st, i, j)
                t = 4 * i + 2 * j
                if t >= 2:
                    act.wait_ge(conv_ready, t)
                else:
                    act.wait_ge(xpad_zero, 1)
                act.activation(xpad[:, :, 3:3 + T], sums(j), ACT.Copy).then_inc(acc_read["act"], 1)
                act.drain().then_inc(xpad_ready, 1)
                for m in range(2):
                    dst = mq[:, t + m, :] if t + m < MH else mk[:, t + m - MH, :]
                    act.wait_ge(conv_ready, t + m + 1)
                    act.activation(dst, tmp[:, 2 + m, :], ACT.Silu).then_inc(conv_used, 1)
            lead(act, "mqk", split_hi, conv_epilogue, "mv", unroll=True)
            
            def mv_epilogue(st, i, j):
                wait_sums(act, st, i, j)
                act.activation(mv[:, :, 2 * i + j, 0:MV], sums_tok(j), ACT.Copy).then_inc(acc_read["act"], 1)
            lead(act, "mv", split_hi, mv_epilogue, "aqk", unroll=True)
            act.activation(mk[:], mk[:], ACT.Copy, scale=MQK ** -0.5).then_inc(mk_scaled, 1)

            def aqk_epilogue(st, i, j):
                wait_sums(act, st, i, j)
                t = 4 * i + 2 * j
                dst = aq[:, t:t + 2, :] if t < 4 else ak[:, t - 4:t - 2, :]
                act.activation(dst, sums(j), ACT.Copy, scale=64.0 ** -0.5 if t < 4 else 1.0).then_inc(acc_read["act"], 1)
            lead(act, "aqk", split_hi, aqk_epilogue, "av", unroll=True)
            lead(act, "av", split_hi, tokens_epilogue(av), "mo", unroll=True)
            act.wait_ge(row_u_ready, 1)
            lead(act, "mo", split_hi, func_epilogue(ogate, ACT.Sigmoid), "mz", unroll=True)
            run_max = inv_diag[0:MH].rearrange("p b t -> p (b t)")
            log_sigmoid(run_max, 2)
            act.wait_ge(fg_ready, 1)
            act.activation(gate_row[0:MH, :], gate_row[0:MH, :], ACT.Exp, scale=-1.0).then_inc(em_ready, 1)

            def mz_epilogue(st, i, j):
                wait_sums(act, st, i, j)
                t = 4 * i + 2 * j
                if t >= 2:
                    act.wait_ge(ogate_ready, t)
                act.activation(tmp[:, 2:4, :], sums(j), ACT.Silu).then_inc(acc_read["act"], 1)
                act.drain().then_inc(mz_ready, 1)
            lead(act, "mz", split_hi, mz_epilogue, "az", unroll=True)
            act.nop().then_inc(m_e_ready, 1)
            act.nop().then_inc(hm_sq, 1)
            def decays(h):
                act.wait_ge(gb_ready, h + 2)
                act.wait_ge(m_s_ready, h + 1)
                for s in range(NB):
                    bias = mt[:, 0, s, ds(h, 1)]
                    ins = act.activation(m_e[:, TOFF[s]:TOFF[s] + P], tmp[:, 1, s * P:(s + 1) * P], ACT.Exp, bias=bias)
                    if s < NB - 1:
                        ins = act.activation(m_e[:, TOFF[s] + P:TOFF[s] + TW[s]], tmp[:, 0, (s + 1) * P:T], ACT.Exp, bias=bias)
                ins.then_inc(m_e_ready, 1)

            decays(0)
            lead(act, "az", split_hi, func_epilogue(az, ACT.Silu), "mix_out", unroll=True)

            def head_squares(h):
                act.wait_ge(r_ready, h + 1)
                for b in range(NB):
                    ins = act.activation(tmp[:, 2 + b // 2, (b % 2) * MV:(b % 2 + 1) * MV], M_BANKS[b][:, 0:MV],
                                         ACT.Square, scale=m_stat[:, 1, ds(h, 1), b:b + 1].rearrange("p a b -> p (a b)"),
                                         accum_out=m_stat[:, 2, ds(h, 1), b:b + 1].rearrange("p a b -> p (a b)"))
                act.drain()
                act.nop().then_inc(hm_sq, 1)

            for h in range(1, MH - 1):
                decays(h)
            for h in range(MH):
                head_squares(h)
                if h + 3 < MH:
                    decays(h + 3)
            act.activation(m_stat[:, 3], m_stat[:, 2], ACT.Sqrt, bias=eps[:], scale=1.0 / MV).then_inc(hm_std, 1)
            attention_act(act, dx)
            hi_chunks("mix", 12, mix_hi)

            def mix_epilogue(st, i, j):
                g = 2 * i + j
                if g:
                    hi_chunks("xg", 2, hh, 2 * g - 2)
                if g == st.groups - 1:
                    hi_chunks("xg", 2, hh, 2 * g)
            lead(act, "mix_out", split_hi, mix_epilogue, "ple", unroll=True)
            hi_chunks("pt", 2, pt_hi)

            def ple_epilogue(st, i, j):
                if j == 0:
                    wait_sums(act, st, i, j)
                    if i == 0:
                        act.wait_ge(h_ready, CH["pt"] + 2)
                    act.wait_ge(acc_read["dve"], st.read0 + 2 * i + 2)
                    act.activation(tmp[:, 0:2, :], sums(0), ACT.Sigmoid).then_inc(sg_ready, 1)
                else:
                    if i == st.iters - 1:
                        act.activation(warm[:], eps[:], ACT.Sqrt)
                    act.wait_ge(x_ready, 16 + i + 1)
                    squares_of_group(x_tok[:, :, i * COLS:(i + 1) * COLS], i)
            lead_ple(act, split_hi, ple_epilogue)
            deviation(4)

        @block.gpsimd
        def _(pool):
            pool.memset(eps[:], EPS)
            pool.memset(ones[:], 1.0)
            pool.memset(ident[:], 0.0)
            pool.memset(head_ones[:], 0.0)
            pool.memset(tri[:], 0.0)
            pool.memset(tri_t[:], 0.0)
            pool.memset(sel[:], 0.0)
            pool.drain()
            for half in range(2):
                pool.memset(head_ones[64 * half:64 * half + 64, 64 * half:64 * half + 64], 1.0)
            pool.drain()
            pool.affine_select(out=ident[:], in_=ident[:], compare_op=ALU.not_equal, fill=1.0, base=0,
                               pattern=[[-1, P]], channel_multiplier=1)
            pool.affine_select(out=tri[:], in_=tri[:], compare_op=ALU.is_ge, fill=NEG, base=0,
                               pattern=[[-1, P]], channel_multiplier=1)
            pool.affine_select(out=tri_t[:], in_=tri_t[:], compare_op=ALU.is_ge, fill=NEG, base=0,
                               pattern=[[1, P]], channel_multiplier=-1)
            pool.affine_select(out=sel[:], in_=sel[:], compare_op=ALU.not_equal, fill=-1.0, base=0,
                               pattern=[[-1, MH], [0, P]], channel_multiplier=1)
            pool.drain().then_inc(consts, 1)

            def lo_chunks(name, n, hi, lo, k0=0):
                for k in range(k0, k0 + n):
                    c = CH[name] + k
                    pool.wait_ge(h_hi, c + 1)
                    pool.tensor_tensor(lo[:, k, :], tmp[:, c % 4, :], hi[:, k, :].bitcast(F32), ALU.subtract).then_inc(h_ready, 1)

            def nothing(st, i, j):
                pass

            split_lo(pool, S["mlp_u"], 0, 0)
            lo_chunks("h0", DC, hh, hl)
            lead(pool, "mlp_u", split_lo, nothing, "mlp_v")
            pool.wait_ge(ws_in, 16)
            pool.affine_select(out=ws_raw[:], in_=ws_raw[:], compare_op=ALU.is_ge, fill=0.0, base=0,
                               pattern=[[0, 16], [-1, P]], channel_multiplier=1).then_inc(ws_masked, 1)
            lead(pool, "mlp_v", split_lo, nothing, None)
            split_lo(pool, S["mlp_out"], 0, 0, slice(0, 1))
            for x in range(GC // KU):
                lo_chunks("y", KU, y_hi, y_lo, KU * x)
                split_lo(pool, S["mlp_out"], 0, 0, slice(x + 1, x + 2))

            lead(pool, "mlp_out", split_lo, nothing, "gu0", unroll=True)
            lo_chunks("h1", DC, hh, hl)
            pool.nop().then_inc(act_ready, 2)

            def gu_epilogue(st, i, j):
                f = 2 * i + j
                pool.wait_ge(a_hi, (FC if st.name == "gu1" else 0) + f + 1)
                pool.tensor_tensor(act_lo[:, ds(f, 1), :], tmp[:, 2 + j:3 + j, :], act_hi[:, ds(f, 1), :].bitcast(F32),
                                   ALU.subtract).then_inc(act_ready, 1)
            lead(pool, "gu0", split_lo, gu_epilogue, "down0")
            lead(pool, "down0", split_lo, nothing, "k", unroll=True)
            lo_chunks("hkv", DC, hh, hl)
            pool.memset(wf_raw[:], 0.0).then_inc(sw_zero, 1)
            pool.memset(fx["mask"][:], 0.0)
            pool.drain()
            for b in range(NB):
                pool.tensor_copy(fx["mask"][:, OFF[b] + b * P:OFF[b] + (b + 1) * P], tri[:])
            pool.drain()
            lead(pool, "k", split_lo, nothing, "v", unroll=True)
            pool.wait_ge(sw_split_hi, 1)
            pool.tensor_tensor(wf_lo[:], wf_raw[:], wf_hi[:].bitcast(F32), ALU.subtract).then_inc(sw_split, 1)
            lead(pool, "v", split_lo, nothing, "q", unroll=True)
            lo_chunks("h2", DC, hh, hl)
            lead(pool, "q", split_lo, nothing, "gate", unroll=True)
            lead(pool, "gate", split_lo, nothing, "fox_out", unroll=True)
            attention_pool(pool, fx)
            lo_chunks("og", DC, og_hi, og_lo)
            lead(pool, "fox_out", split_lo, nothing, "gu1", unroll=True)
            lo_chunks("h3", DC, hh, hl)
            lead(pool, "gu1", split_lo, gu_epilogue, "down1")
            lead(pool, "down1", split_lo, nothing, "ixq", unroll=True)
            pool.wait_ge(w_used, S["ixq"].unit0 + RING)
            pool.memset(xw_raw[:], 0.0).then_inc(sw_zero, 1)
            lo_chunks("h4", DC, hh, hl)

            def split_xw(st, i, j):
                if j == 0:
                    pool.wait_ge(sw_split_hi, 2)
                    pool.tensor_tensor(xw_lo[:], xw_raw[:], xw_hi[:].bitcast(F32), ALU.subtract).then_inc(sw_split, 1)
            lead(pool, "ixq", split_lo, split_xw, "mqk", unroll=True)
            for name, following in (("mqk", "mv"), ("mv", "aqk"), ("aqk", "av"), ("av", "mo"), ("mo", "mz")):
                lead(pool, name, split_lo, nothing, following, unroll=True)

            def mz_epilogue(st, i, j):
                t = 4 * i + 2 * j
                pool.wait_ge(mz_ready, t // 2 + 1)
                for m in range(2):
                    pool.tensor_tensor(ogate[:, t + m, :], ogate[:, t + m, :], tmp[:, 2 + m, :], ALU.mult).then_inc(ogate_ready, 1)
            lead(pool, "mz", split_lo, mz_epilogue, "az", unroll=True)
            lead(pool, "az", split_lo, nothing, "mix_out", unroll=True)
            pool.wait_ge(dmask_ready, 1)
            attention_pool(pool, dx)
            lo_chunks("mix", 12, mix_hi, mix_lo)

            def mix_epilogue(st, i, j):
                g = 2 * i + j
                if g:
                    lo_chunks("xg", 2, hh, hl, 2 * g - 2)
                if g == st.groups - 1:
                    lo_chunks("xg", 2, hh, hl, 2 * g)
            lead(pool, "mix_out", split_lo, mix_epilogue, "ple", unroll=True)
            lo_chunks("pt", 2, pt_hi, pt_lo)
            lead_ple(pool, split_lo, nothing)
        @block.tensor
        def _(pe):
            pe.nop().then_inc(w_used, RING)

            def products(out, pairs, first, last, check=False):
                for n, (w, x) in enumerate(pairs):
                    ins = pe.matmul(out, w, x, start=first and n == 0, stop=last and n == len(pairs) - 1, skip_group_check=check)
                return ins

            def gemm(name, hi, lo, ready, ready0, after=None, unroll=False, second=None, before_chunk=None):
                st = S[name]
                before = STAGES[STAGES.index(st) - 1] if st.group0 else None
                def body(i):
                    for j in range(2):
                        pe.wait_ge(acc_read[st.reader], st.read0 + 2 * i + j + 1)
                        if before and before.reader != st.reader:
                            pe.wait_ge(acc_read[before.reader], before.read0 + before.groups + j + 1)
                        a_hi, a_lo, a_ready, a_ready0 = second if second and j else (hi, lo, ready, ready0)
                        kc = st.kchunks[j]
                        for x, (k0, nk) in enumerate(st.units[j]):
                            s = slot_of(st, i, j, x)
                            pe.wait_ge(w_split, unit_no(st, i, j, x) + 1)
                            for kk in range(nk):
                                k = k0 + kk
                                if before_chunk:
                                    before_chunk(i, j, k)
                                pe.wait_ge(a_ready, a_ready0 + k + 1)
                                if st.token_major:
                                    for b in range(NB):
                                        blk = slice(b * P, (b + 1) * P)
                                        wh, wl = w_hi[:, s, kk, :], w_lo[:, s, kk, :]
                                        ins = products(sums_tok(j)[:, b, :], ((a_hi[:, k, blk], wh), (a_hi[:, k, blk], wl), (a_lo[:, k, blk], wh)),
                                                       k == 0 and b % 2 == 0, k == kc - 1, True)
                                else:
                                    for m in range(2):
                                        col = slice(m * P, (m + 1) * P)
                                        wh, wl = w_hi[:, s, kk, col], w_lo[:, s, kk, col]
                                        ins = products(sums(j)[:, m, :], ((wh, a_hi[:, k, :]), (wh, a_lo[:, k, :]), (wl, a_hi[:, k, :])),
                                                       k == 0, k == kc - 1)
                            ins.then_inc(w_used, 1)
                        if after:
                            after(i, j)
                times(pe, st.iters, body, unroll or st.per_body % RING != 0)

            def ada_column(step, par, setup=False):
                n = step - ADA_PAIRS
                pe.wait_ge(ada_ready, n + 1)
                if not setup:
                    pe.wait_ge(ada_col, n + 1)
                column_sums(ada_ps[:, 2 * par:2 * par + 2], ada_acc[:, par, :]).then_inc(ada_sum, 1)

            def column_sums(dst, src):
                for m in range(2):
                    ins = pe.matmul(dst[:, m:m + 1], src[:, m * P:(m + 1) * P], ones[:, 0:1], start=True, stop=True)
                return ins

            def spread_gain(n):
                pe.wait_ge(bdiag_ready, n + 1)
                for half in range(2):
                    ins = pe.matmul(bank(2 + half), ones[:], gain_row[:, half * T:(half + 1) * T], start=True, stop=True)
                ins.then_inc(gain_ps, 1)

            def first_to_features():
                pe.wait_ge(diag_ready, 1)
                for k in range(DC):
                    if k >= len(XT_BANKS):
                        pe.wait_ge(kept_ready, k - len(XT_BANKS) + 1)
                    for b in range(NB):
                        ins = pe.matmul(XT_BANKS[k % len(XT_BANKS)][:, b * P:(b + 1) * P], x_tok[:, b, k * P:(k + 1) * P], inv_diag[:, b, :],
                                        start=True, stop=True)
                    ins.then_inc(xt_ps, 1)

            def x_to_features(n, name):
                banks = len(XT_BANKS)
                def chunk_part(k, b):
                    return pe.transpose(XT_BANKS[k % banks][:, b * P:(b + 1) * P], x_scaled[:, b, k * P:(k + 1) * P], ident[:])
                for b in range(NB):
                    if b < NB // 2:
                        pe.wait_ge(xn_dve, NB // 2 * n + b + 1)
                    else:
                        pe.wait_ge(xn_act, NB // 2 * (n - 1) + b + 1)
                    for k in range(banks):
                        ins = chunk_part(k, b)
                        if b == NB - 1:
                            ins.then_inc(xt_ps, 1)
                for k in range(banks, DC):
                    pe.wait_ge(t_ready, CH[name] + k - banks + 1)
                    for b in range(NB):
                        ins = chunk_part(k, b)
                    ins.then_inc(xt_ps, 1)

            pe.wait_ge(consts, 1)
            pe.wait_ge(c_in, 16)
            pe.transpose(aux[:, 0, 0:DC], c_row[:], ident[0:DC, 0:DC]).then_inc(c_ps, 1)
            pe.wait_ge(c_ok, 1)
            for s in range(ADA_PE):
                pe.wait_ge(ada_first_in[s], 16)
                for m in range(2):
                    for k in range(DC):
                        pe.matmul(bank(0)[:, 2 * s + m:2 * s + m + 1], ada_first[:, s, k, m * P:(m + 1) * P], c_act[:, k:k + 1],
                                  start=k == 0, stop=k == DC - 1)
            pe.wait_ge(par_in, 16 * 19)
            for n, r in enumerate((112, 104, 74)):
                pe.transpose(bank(1 + n)[:, 0:r], rows[0:r, n, :], ident[0:r, 0:r]).then_inc(par_t, 1)
            pe.wait_ge(par_ok, 3)
            first_to_features()
            for s in range(ADA_PE, ADA_PAIRS):
                pe.wait_ge(ada_setup_ready, s - ADA_PE + 1)
                ins = column_sums(bank(0)[:, 2 * s:2 * s + 2], ada_setup[:, s - ADA_PE, :])
            ins.then_inc(ada_first_ps, 1)
            for s in range(ADA_PAIRS, ADA_SETUP):
                ada_column(s, s % 2, True)
            gemm("mlp_u", hh, hl, h_ready, CH["h0"], lambda i, j: ada_column(8 + 2 * i + j, j))
            pe.wait_ge(ws_masked, 1)
            for q in range(4):
                if q >= 2:
                    pe.wait_ge(wst_ready, q - 1)
                for n in range(4):
                    ins = pe.transpose(aux[:, q % 2, n * P:(n + 1) * P], ws_raw[:, 4 * q + n, :], ident[:])
                ins.then_inc(wst_ps, 1)
            for q in range(4):
                pe.wait_ge(wst_ready, 3 + q % 2 if q < 2 else 4)
                if q >= 2:
                    pe.wait_ge(r_read, q - 1)
                pe.matmul(aux[:, q % 2, :], ones[:], ws_t[:, 4 * q:4 * q + 4, :].rearrange("p g t -> p (g t)"),
                          start=True, stop=True).then_inc(r_ps, 1)
            gemm("mlp_v", hh, hl, h_ready, CH["h0"], lambda i, j: ada_column(16 + 2 * i + j, j))
            pe.wait_ge(r_read, 4)
            pe.wait_ge(acc_read["dve"], S["mlp_v"].read0 + S["mlp_v"].groups + 2)
            spread_gain(0)
            AHEAD = 4

            def mix_tokens(g):
                if g % V_PART == 0:
                    pe.wait_ge(v_norm, NB // 2 * (g // V_PART + 1))
                    pe.wait_ge(v_norm_act, NB // 2 * (g // V_PART + 1))
                if g >= 2:
                    pe.wait_ge(mix_read, g - 1)
                for b in range(NB):
                    ins = pe.matmul(aux[:, g % 2, b * P:(b + 1) * P], v[:, b, g * P:(g + 1) * P], ws_t[:, g, :], start=True, stop=True)
                ins.then_inc(mix_ps, 1)

            def mixing_beside(i, j, k):
                if (i, j) == (0, 0) and k + AHEAD < GC:
                    mix_tokens(k + AHEAD)
                if (i, j, k) == (0, 1, 0):
                    pe.wait_ge(gain_ready, 1)
            for g in range(AHEAD):
                mix_tokens(g)

            gemm("mlp_out", y_hi, y_lo, h_ready, CH["y"], unroll=True, before_chunk=mixing_beside)
            x_to_features(0, "h1")
            gemm("gu0", hh, hl, h_ready, CH["h1"], lambda i, j: ada_column(24 + 2 * i + j, j))
            def gain_beside(n, k_at):
                def before_chunk(i, j, k):
                    if (i, j, k) == (0, 0, k_at):
                        spread_gain(n)
                    if (i, j, k) == (0, 1, 0):
                        pe.wait_ge(gain_ready, n + 1)
                return before_chunk

            def last_columns(i, j, k):
                gain_beside(1, 4 * KU)(i, j, k)
                n, off = divmod((2 * i + j) * FC + k - DOWN_FROM, DOWN_EVERY)
                if off == 0 and 0 <= n < ADA_STEPS - DOWN_STEP:
                    ada_column(DOWN_STEP + n, n % 2)
            gemm("down0", act_hi, act_lo, act_ready, 2, unroll=True, before_chunk=last_columns)
            x_to_features(1, "hkv")

            def head_squares(c):
                for t in (c, c + 1):
                    pe.wait_ge(hsq_ready, t + 1)
                    if t >= 2:
                        pe.wait_ge(hstd, t - 1)
                    pe.matmul(aux[:, t % 2, :], head_ones[:], sq[:, t % 2, :], start=True, stop=True).then_inc(hs_ps, 1)

            def squares_behind(c0):
                def after(i, j):
                    if (i, j) != (0, 0):
                        head_squares(c0 + 4 * i + 2 * j - 2)
                return after
            gemm("k", hh, hl, h_ready, CH["hkv"], squares_behind(0), unroll=True, before_chunk=gain_beside(2, KU))
            def forget_gates(i, j):
                if (i, j) == (0, 0):
                    head_squares(6)
                if (i, j) == (1, 0):
                    pe.wait_ge(sw_split, 1)
                    pe.wait_ge(hstd, 8)
                    for k in range(DC):
                        ins = products(aux[:, 0, :], ((wf_hi[:, k, :], hh[:, k, :]), (wf_hi[:, k, :], hl[:, k, :]), (wf_lo[:, k, :], hh[:, k, :])),
                                       k == 0, k == DC - 1)
                    ins.then_inc(f_ps, 1)
            gemm("v", hh, hl, h_ready, CH["hkv"], forget_gates, unroll=True)
            pe.wait_ge(f_read, 1)
            gemm("q", hh, hl, h_ready, CH["h2"], squares_behind(8), unroll=True)
            def last_queries(i, j):
                if (i, j) == (0, 0):
                    head_squares(14)
            gemm("gate", hh, hl, h_ready, CH["h2"], last_queries, unroll=True)
            attention_pe(pe, fx)

            def to_features(src, k, done_sem, chunk, first):
                if chunk - first >= 2:
                    pe.wait_ge(t_ready, chunk - 1)
                for b in range(NB):
                    ins = pe.transpose(aux[:, (chunk - first) % 2, b * P:(b + 1) * P], src[:, b, k * P:(k + 1) * P], ident[:])
                ins.then_inc(done_sem, 1)

            pe.wait_ge(fx["o_read"], NH + 2)
            for k in range(DC):
                to_features(fx["o"], k, og_ps, CH["og"] + k, CH["og"])
            gemm("fox_out", og_hi, og_lo, h_ready, CH["og"], unroll=True)
            x_to_features(2, "h3")
            gemm("gu1", hh, hl, h_ready, CH["h3"])
            gemm("down1", act_hi, act_lo, act_ready, FC + 2, unroll=True, before_chunk=gain_beside(3, 4 * KU))
            x_to_features(3, "h4")
            gemm("ixq", hh, hl, h_ready, CH["h4"], unroll=True)
            pe.wait_ge(sw_split, 2)
            for n in range(2):
                for k in range(DC):
                    wh, wl = xw_hi[:, k, n * P:(n + 1) * P], xw_lo[:, k, n * P:(n + 1) * P]
                    ins = products(aux[:, n, :], ((wh, hh[:, k, :]), (wh, hl[:, k, :]), (wl, hh[:, k, :])), k == 0, k == DC - 1)
            ins.then_inc(xw_ps, 1)

            def indexer_beside(i, j, k):
                if (i, j, k) == (0, 0, 1):
                    pe.wait_ge(xw_read, 1)
                    rows_iw = slice(X_IW - P, X_IW - P + IH)
                    for b in range(NB):
                        ins = pe.transpose(ms[:, b * IH:(b + 1) * IH], sq[rows_iw, 0, b * P:(b + 1) * P], ident[rows_iw, rows_iw])
                    ins.then_inc(iw_ps, 1)
                if (i, j, k) == (0, 0, DC - IX_CHUNKS):
                    pe.wait_ge(acc_read["act"], S["mqk"].read0 + 2)
                per_chunk = IX_STEP // IX_CHUNKS
                n0 = IX_STEP * (2 * i + j) + per_chunk * (k - (DC - IX_CHUNKS))
                for n in range(n0, n0 + per_chunk if k >= DC - IX_CHUNKS else n0):
                    b, h = 1 + n // IH, n % IH
                    half = slice(64 * (h % 2), 64 * (h % 2) + 64)
                    if n >= 2:
                        pe.wait_ge(ix_relu, n - 1)
                    pe.matmul(aux[:, n % 2, 0:WIDTH[b]], ixq[half, h // 2, b * P:(b + 1) * P], ixk[half, 0:WIDTH[b]],
                              start=True, stop=True).then_inc(ix_ps, 1)
            gemm("mqk", hh, hl, h_ready, CH["h4"], unroll=True, before_chunk=indexer_beside)
            pe.wait_ge(one_hot_in, 16)
            pe.wait_ge(gates_in, 64)
            pe.wait_ge(ix_relu, 3 * IH)
            pe.matmul(aux[0:AH, 0, :], rel[:], one_hot[:, 0:T], start=True, stop=True)
            pe.matmul(aux[0:AH, 1, 0:UROW - T], rel[:], one_hot[:, T:UROW], start=True, stop=True).then_inc(u_ps, 1)
            gemm("mv", hh, hl, h_ready, CH["h4"], unroll=True)
            gemm("aqk", hh, hl, h_ready, CH["h4"], unroll=True)
            gemm("av", hh, hl, h_ready, CH["h4"], unroll=True)
            gemm("mo", hh, hl, h_ready, CH["h4"], unroll=True)
            gemm("mz", hh, hl, h_ready, CH["h4"], unroll=True)
            pe.nop().then_inc(qk_ps, 1)
            pe.nop().then_inc(num_ps, 1)
            pe.wait_ge(em_ready, 1)
            pe.wait_ge(row_u_ready, 1)
            for n, src in enumerate((sq[0:MH, 0, :], gate_row[0:MH, :])):
                for b in range(NB):
                    c = (n * NB + b) * MH
                    ins = pe.matmul(ada_ps[:, c:c + MH], src[:, b * P:(b + 1) * P], ident[0:MH, 0:MH], start=True, stop=True)
            ins.then_inc(mt_ps, 1)
            pe.wait_ge(mt_ready, 1)

            def head_gates(h):
                pe.wait_ge(gb_ready, h + 1)
                pe.matmul(ms[:], sel[:, h, :], inv_diag[0:MH].rearrange("p b t -> p (b t)"), start=True, stop=True).then_inc(gb_ps, 1)
            head_gates(0)
            gemm("az", hh, hl, h_ready, CH["h4"], unroll=True)

            pe.wait_ge(acc_read["act"], S["az"].read0 + S["az"].groups + 2)

            def head_products(h):
                pe.wait_ge(m_s_ready, h + 1)
                for s in range(NB):
                    ins = pe.matmul(qk_part(s), mk[:, h, s * P:(s + 1) * P], mq[:, h, s * P:T],
                                    start=True, stop=True)
                ins.then_inc(qk_ps, 1)

            def head_values(h, e):
                pe.wait_ge(m_s_ready, h + 2)
                pe.wait_ge(hm_ready, h + 1)
                pe.wait_ge(hm_sq, h + 1)
                for b in range(NB):
                    for s in range(b + 1):
                        w = m_s[:, e, TOFF[s] + (b - s) * P:TOFF[s] + (b - s + 1) * P]
                        ins = pe.matmul(M_BANKS[b][:, 0:MV + 1], w, mv[:, s, h, :], start=s == 0, stop=s == b)
                ins.then_inc(num_ps, 1)
            pe.wait_ge(mk_scaled, 1)
            head_products(0)
            head_gates(1)
            for h in range(MH):
                if h + 1 < MH:
                    head_products(h + 1)
                if h + 2 < MH:
                    head_gates(h + 2)
                head_values(h, h % 2)
            pe.wait_ge(hm_ready, MH + 1)
            pe.wait_ge(hm_sq, MH + 1)
            attention_pe(pe, dx)
            pe.wait_ge(dx["o_read"], AH + 2)
            pe.wait_ge(hm_scaled, 1)
            def mix_chunk(k):
                if k < DC:
                    to_features(hm, k, mix_t, CH["mix"] + k, CH["mix"])
                else:
                    to_features(dx["o"], k - DC, mix_t, CH["mix"] + k, CH["mix"])
            mix_chunk(0)
            mix_chunk(1)

            def mix_beside(i, j, k):
                if (i, j) == (0, 0) and k + 2 < S["mix_out"].kchunks[0]:
                    mix_chunk(k + 2)

            def x_chunks(i, j):
                g = 2 * i + j
                for k in range(max(2 * g - 2, 0), 2 * g + (2 if g == S["mix_out"].groups - 1 else 0)):
                    pe.wait_ge(acc_read["dve"], S["mix_out"].read0 + k // 2 + 3)
                    if k >= 2:
                        pe.wait_ge(t_ready, CH["xg"] + k - 1)
                    for b in range(NB):
                        ins = pe.transpose(XG_BANKS[k % 2][:, b * P:(b + 1) * P], x_tok[:, b, k * P:(k + 1) * P], ident[:])
                    ins.then_inc(xt_ps, 1)
            gemm("mix_out", mix_hi, mix_lo, h_ready, CH["mix"], x_chunks, unroll=True,
                 before_chunk=mix_beside)
            pe.wait_ge(p_landed, 32)
            for k in range(2):
                for b in range(NB):
                    ins = pe.transpose(aux[:, k, b * P:(b + 1) * P], p_in[:, b, k * P:(k + 1) * P], ident[:])
                ins.then_inc(p_t, 1)
            gemm("ple", hh, hl, h_ready, CH["xg"], second=(pt_hi, pt_lo, h_ready, CH["pt"]))

        @block.vector
        def _(dve):
            dve.nop().then_inc(acc_read["dve"], 2)
            dve.nop().then_inc(ada_used, 2)

            def ada_step(step, par):
                ada_finish(step - 2, par, step - ADA_PAIRS)
                for half in range(2):
                    dve.drain()
                    dve.wait_ge(ada_landed[half], 16 * ada_round(step) + 16)
                    ada_chunks(ada_acc[:, par, :], ada_raw[:, half], half * KU).then_inc(ada_used, 1)
                dve.drain().then_inc(ada_ready, 1)

            def ada_chunks(total, w, k0):
                for kk in range(w.shape[1]):
                    if k0 + kk == 0:
                        ins = dve.tensor_scalar(total, w[:, kk, :], c_act[:, 0:1], None, ALU.mult)
                    else:
                        if kk:
                            dve.drain()
                        ins = dve.scalar_tensor_tensor(total, w[:, kk, :], c_act[:, k0 + kk:k0 + kk + 1], total, ALU.mult, ALU.add)
                return ins

            def ada_finish(step, par, summed):
                dve.wait_ge(ada_sum, summed)
                dve.tensor_tensor(mod[:, ds(2 * step, 2)], ada_ps[:, 2 * par:2 * par + 2], par_a[:, ds(2 * step, 2)], ALU.add) \
                    .then_inc(ada_col, 1)

            def inverse_deviation(n):
                dve.wait_ge(std_ready, n + 1)
                dve.reciprocal(small[:, 4:8], small[:, 0:NB])
                dve.drain()

            def free_tmp(c):
                if c >= 4:
                    dve.wait_ge(h_ready, c - 3)

            def modulation(gain, scale):
                dve.scalar_tensor_tensor(scol[:], scale, 1.0, gain, ALU.add, ALU.mult)
                dve.drain()

            def normed(name, col, shift=None, keep=False, kept=None, kept_sem=None):
                for k in range(DC):
                    c = CH[name] + k
                    free_tmp(c)
                    if kept is not None:
                        src = kept[:, k, :]
                        if kept_sem is not None:
                            dve.wait_ge(kept_sem, k + 1)
                    else:
                        src = XT_BANKS[k % len(XT_BANKS)]
                        dve.wait_ge(xt_ps, XT[name] + k + 1)
                    if keep:
                        dve.tensor_copy(x_kept[:, k, :], src)
                    dve.tensor_scalar(tmp[:, c % 4, :], src, col[:, k:k + 1], shift[:, k:k + 1] if shift is not None else None,
                                      ALU.mult, ALU.add if shift is not None else ALU.bypass).then_inc(t_ready, 1)

            def gain_diagonal(gain, gate_col):
                dve.tensor_tensor(bcol[:], gate_col, gain, ALU.mult)
                dve.drain()
                dve.tensor_tensor(gain_row[:].rearrange("p (k n) -> p k n", k=DC), ident[:].unsqueeze(1).broadcast_to([P, DC, P]),
                                  bcol[:].unsqueeze(2).broadcast_to([P, DC, P]), ALU.mult).then_inc(bdiag_ready, 1)

            def gain_copy(n):
                dve.wait_ge(gain_ps, n + 1)
                dve.tensor_copy(gain_row[:].rearrange("p (a t) -> p a t", a=2), sums(1)).then_inc(gain_ready, 1)
                dve.drain()

            def add_square_sums(n, g):
                dve.wait_ge(sq_ready, 8 * n + 2 * g + 2)
                if g:
                    ins = dve.tensor_tensor(square_sum[:, 4, :], square_sum[:, 0 if g == 1 else 4, :], square_sum[:, g, :], ALU.add)
                    if g == 3:
                        ins.then_inc(sum_ready, 1)
                    else:
                        dve.drain()

            def product_group(n, g, y):
                cols = slice(g * COLS, (g + 1) * COLS)
                for half in range(2):
                    blocks = slice(2 * half, 2 * half + 2)
                    if half:
                        add_square_sums(n, g)
                    else:
                        dve.wait_ge(sq_ready, 8 * n + 2 * g + 1)
                    ins = dve.tensor_tensor(y[:, blocks, cols], sums_tok(g % 2)[:, blocks, :],
                                            gain_row[:, cols].unsqueeze(1).broadcast_to([P, 2, COLS]), ALU.mult)
                ins.then_inc(acc_read["dve"], 1)

            def add_normed(n, y):
                inverse_deviation(n + 1)
                for b in range(NB):
                    dve.scalar_tensor_tensor(x_tok[:, b, :], y[:, b, :], small[:, 4 + b:5 + b], x_tok[:, b, :], ALU.mult, ALU.add).then_inc(x_ready, 1)
                for half in range(2):
                    dve.drain()
                    dve.wait_ge(xstd_ready, 2 * n + half + 1)
                    ins = dve.reciprocal(small[:, 4 + 2 * half:6 + 2 * half], small[:, 2 * half:2 * half + 2])
                    if half:
                        ins.then_inc(xinv_ready, 1)
                    dve.drain()
                    dve.tensor_scalar(x_scaled[:, half, :], x_tok[:, half, :], small[:, 4 + half:5 + half], None, ALU.mult).then_inc(xn_dve, 1)

            dve.wait_ge(c_ok, 1)
            for s in range(ADA_PE, ADA_SETUP):
                if s == ADA_PE + 2:
                    inverse_deviation(0)
                    dve.tensor_tensor(inv_diag[:], ident[:].unsqueeze(1).broadcast_to([P, NB, P]),
                                      small[:, 4:8].unsqueeze(2).broadcast_to([P, NB, P]), ALU.mult).then_inc(diag_ready, 1)
                if s == ADA_PE + 3:
                    for n, (dst, r) in enumerate(((par_a, 112), (par_b, 104), (par_c, 74))):
                        dve.wait_ge(par_t, n + 1)
                        dve.tensor_copy(dst[:, 0:r], bank(1 + n)[:, 0:r]).then_inc(par_ok, 1)
                dve.wait_ge(ada_next_in[s - ADA_PE], 16)
                ada_chunks(ada_setup[:, s - ADA_PE, :] if s < ADA_PAIRS else ada_acc[:, s % 2, :], ada_next[:, s - ADA_PE], 0)
                dve.drain().then_inc(ada_setup_ready if s < ADA_PAIRS else ada_ready, 1)
            dve.wait_ge(ada_first_ps, 1)
            dve.tensor_tensor(mod[:, 0:2 * ADA_PAIRS], bank(0)[:, 0:2 * ADA_PAIRS], par_a[:, 0:2 * ADA_PAIRS], ALU.add)
            for s in range(ADA_PAIRS, ADA_SETUP):
                ada_finish(s, s % 2, ADA_SETUP - ADA_PAIRS)
            dve.drain()
            modulation(par_b[:, 0:8], mod[:, 8:16])
            normed("h0", scol[:], mod[:, 0:8], kept=x_first, kept_sem=kept_ready)
            def u_body(i):
                for j in range(2):
                    ada_step(8 + 2 * i + j, j)
            times(dve, S["mlp_u"].iters, u_body)
            for q in range(4):
                dve.wait_ge(wst_ps, q + 1)
                dve.tensor_copy(ws_t[:, 4 * q:4 * q + 4, :].rearrange("p g t -> p (g t)"), aux[:, q % 2, :]).then_inc(wst_ready, 1)
            dve.drain()
            dve.wait_ge(q_bias_in, 16)
            for q in range(4):
                dve.wait_ge(r_ps, q + 1)
                for n in range(4):
                    g = 4 * q + n
                    ins = dve.scalar_tensor_tensor(q_bias[:, g, :], aux[:, q % 2, n * P:(n + 1) * P], par_c[:, 50 + g:51 + g],
                                                   q_bias[:, g, :], ALU.mult, ALU.add)
                ins.then_inc(r_read, 1)
            dve.drain()
            gain_diagonal(par_b[:, 16:24], mod[:, 16:24])
            dve.wait_ge(b_in_in, 16)
            st = S["mlp_v"]

            def v_body(i):
                for j in range(2):
                    ada_step(16 + 2 * i + j, j)
                    wait_sums(dve, st, i, j)
                    c = COLS * (2 * i + j)
                    dve.tensor_tensor(v[:, :, ds(c, COLS)], sums_tok(j), b_in[:, ds(c, COLS)].unsqueeze(1).broadcast_to([P, NB, COLS]),
                                      ALU.add).then_inc(acc_read["dve"], 1)
                    dve.drain().then_inc(v_added, 1)
                    dve.wait_ge(v_gelu, 2 * i + j + 1)
                    for b in range(NB):
                        dve.bn_stats(stats[:, b, ds(2 * i + j, 1), :].rearrange("p a s -> p (a s)"),
                                     v[:, b, ds(c, COLS)])
            times(dve, st.iters, v_body)
            dve.drain()
            for b in range(NB):
                ins = dve.bn_aggr(moments[:, b, :], stats[:, b, :, :].rearrange("p a s -> p (a s)"))
            ins.then_inc(ln_moments, 1)
            dve.wait_ge(ln_std, 1)
            dve.reciprocal(small[:, 4:8], small[:, 0:NB])
            dve.drain()
            dve.scalar_tensor_tensor(ln_shift[:], moments[:, :, 0], -1.0, small[:, 4:8], ALU.mult, ALU.mult)
            dve.drain().then_inc(ln_ready, 1)
            for g in range(0, GC, V_PART):
                for b in range(NB // 2):
                    part = v[:, b, g * P:(g + V_PART) * P]
                    dve.tensor_scalar(part, part, moments[:, b, 0:1], small[:, 4 + b:5 + b], ALU.subtract, ALU.mult).then_inc(v_norm, 1)
            for g0 in range(0, GC, 2):
                for g in (g0, g0 + 1):
                    c = CH["y"] + g
                    free_tmp(c)
                    dve.wait_ge(mix_ps, g + 1)
                    dve.scalar_tensor_tensor(tmp[:, c % 4, :].rearrange("p (b t) -> p b t", b=NB), aux[:, g % 2, :].rearrange("p (b t) -> p b t", b=NB),
                                             par_c[:, 34 + g:35 + g], q_bias[:, g:g + 1, :].broadcast_to([P, NB, P]),
                                             ALU.mult, ALU.add).then_inc(mix_read, 1)
                dve.drain()
                for g in (g0, g0 + 1):
                    c = CH["y"] + g
                    dve.tensor_tensor(tmp[:, c % 4, :], tmp[:, c % 4, :], u[:, g, :], ALU.mult).then_inc(t_ready, 1)
            gain_copy(0)
            for g in range(4):
                product_group(0, g, y_mlp)
            modulation(par_b[:, 32:40], mod[:, 32:40])
            add_normed(0, y_mlp)
            normed("h1", scol[:], mod[:, 24:32])

            def feed_forward(name, l, ada=None):
                st = S[name]
                def body(i):
                    for j in range(2):
                        if ada is not None:
                            ada_step(ada + 2 * i + j, j)
                        wait_sums(dve, st, i, j)
                        f = 2 * i + j
                        dve.wait_ge(sg_ready, l * FC + f + 1)
                        dve.wait_ge(act_ready, l * FC + f + 1)
                        dve.tensor_tensor(tmp[:, 2 + j, :], sums(j)[:, 1, :], tmp[:, j, :], ALU.mult).then_inc(acc_read["dve"], 1)
                        dve.drain()
                        dve.tensor_copy(act_hi[:, ds(f, 1), :], tmp[:, 2 + j:3 + j, :]).then_inc(a_hi, 1)
                times(dve, st.iters, body)
            feed_forward("gu0", 0, 24)
            gain_diagonal(par_b[:, 48:56], mod[:, 40:48])
            gain_copy(1)
            for s in range(DOWN_STEP, ADA_STEPS):
                ada_step(s, s % 2)
                if s in (49, 53, 55):
                    product_group(1, (49, 53, 55).index(s), y_h)
            product_group(1, 3, y_h)
            for s in (54, 55):
                ada_finish(s, s % 2, ADA_STEPS - ADA_PAIRS)
            dve.drain()
            modulation(par_b[:, 64:72], mod[:, 56:64])
            add_normed(1, y_h)
            normed("hkv", scol[:], mod[:, 48:56], keep=True)
            gain_diagonal(par_b[:, 24:32], mod[:, 80:88])
            gain_copy(2)

            def head_norm(dst, gain, c0):
                for k in range(DC):
                    c = c0 + k
                    dve.wait_ge(hstd, c + 1)
                    dve.reciprocal(tmp[:, c % 2, :], tmp[:, c % 2, :])
                    dve.drain()
                    dve.scalar_tensor_tensor(dst[:, k, :], dst[:, k, :], gain, tmp[:, c % 2, :], ALU.mult, ALU.mult).then_inc(kq_ready, 1)
            dve.tensor_scalar(qgain[:], par_c[:, 33:34], DH ** -0.5, None, ALU.mult)
            head_norm(k_fox, par_c[:, 32:33], 0)

            def log_forget(f, ab, low, total, n):
                dve.scalar_tensor_tensor(ab, f, -1.0, f, ALU.mult, ALU.max).then_inc(ls_abs, 1)
                dve.tensor_scalar(low, f, 0.0, None, ALU.min)
                dve.drain()
                dve.wait_ge(ls_log, n)
                dve.tensor_tensor(low, low, ab, ALU.subtract)
                dve.drain()
                rows_n = low.shape[0]
                dve.tensor_tensor_scan(total, ones[0:rows_n, 0:1].broadcast_to([rows_n, T]), low, 0.0, ALU.mult, ALU.add)
                dve.drain()
            dve.wait_ge(f_ps, 1)
            dve.wait_ge(gates_in, 64)
            dve.tensor_scalar(gl_f[:, 0, :], aux[0:NH, 0, :], kvbf[:], None, ALU.add).then_inc(f_read, 1)
            dve.drain()
            log_forget(gl_f[:, 0, :], gl_f[:, 1, :], gl_f[:, 2, :], gl_f[:, 3, :], 1)
            dve.tensor_scalar(gl_f[:, 4, :], gl_f[:, 3, :], -1.0, None, ALU.mult).then_inc(fox_d_ready, 1)
            modulation(par_b[:, 8:16], mod[:, 72:80])
            normed("h2", scol[:], mod[:, 64:72], kept=x_kept)
            head_norm(q_fox, qgain[:], 8)
            attention_dve(dve, fx)
            for k in range(DC):
                c = CH["og"] + k
                free_tmp(c)
                dve.wait_ge(og_ps, k + 1)
                dve.tensor_tensor(tmp[:, c % 4, :], aux[:, k % 2, :], gate[:, k, :], ALU.mult).then_inc(t_ready, 1)
            for g in range(4):
                product_group(2, g, y_fox)
            modulation(par_b[:, 40:48], mod[:, 96:104])
            add_normed(2, y_fox)
            normed("h3", scol[:], mod[:, 88:96])
            feed_forward("gu1", 1)
            gain_diagonal(par_b[:, 56:64], mod[:, 104:112])
            gain_copy(3)
            for g in range(4):
                product_group(3, g, y_h)
            add_normed(3, y_h)
            normed("h4", par_b[:, 72:80])

            dve.wait_ge(xw_ps, 1)
            dve.tensor_copy(ixk[:], aux[:, 0, :])
            rows_iw = slice(X_IW - P, X_IW - P + IH)
            dve.tensor_scalar(sq[rows_iw, 0, :], aux[rows_iw, 1, :], IH ** -0.5, None, ALU.mult)
            for m, c in enumerate((X_IF, X_FG)):
                dve.tensor_copy(sq[0:MH, m, :], aux[c - P:c - P + MH, 1, :])
            dve.memset(mv[:, :, :, MV:MV + 1], 1.0)
            dve.memset(xpad[:, :, 0:3], 0.0).then_inc(xpad_zero, 1)
            dve.drain().then_inc(xw_read, 1)
            dve.wait_ge(iw_ps, 1)
            dve.tensor_copy(iw[:].rearrange("p b h -> p (b h)"), ms[:, 0:NB * IH])
            dve.drain()

            def add_head(n):
                b, h = 1 + n // IH, n % IH
                part = score[:, OFF[b] - P:OFF[b] - P + WIDTH[b]]
                dve.wait_ge(ix_relu, n + 1)
                if h == 0:
                    dve.tensor_scalar(part, tmp[:, n % 2, 0:WIDTH[b]], iw[:, b, h:h + 1], None, ALU.mult).then_inc(ix_added, 1)
                else:
                    dve.drain()
                    dve.scalar_tensor_tensor(part, tmp[:, n % 2, 0:WIDTH[b]], iw[:, b, h:h + 1], part, ALU.mult, ALU.add).then_inc(ix_added, 1)

            def convolve(t):
                m = t % 2
                dve.wait_ge(xpad_ready, t // 2 + 1)
                if t >= 2:
                    dve.wait_ge(conv_used, t - 1)
                out = tmp[:, 2 + m, :]
                dve.tensor_scalar(out, xpad[:, m, 0:T], par_c[:, t:t + 1], None, ALU.mult)
                for w in range(1, 4):
                    dve.drain()
                    ins = dve.scalar_tensor_tensor(out, xpad[:, m, w:w + T], par_c[:, 8 * w + t:8 * w + t + 1], out, ALU.mult, ALU.add)
                ins.then_inc(conv_ready, 1)
            for g in range(S["mqk"].groups):
                for n in range(IX_STEP * g, IX_STEP * (g + 1)):
                    add_head(n)
                convolve(2 * g)
                convolve(2 * g + 1)
            dve.drain()
            for b in range(1, NB):
                diag = score[:, OFF[b] - P + b * P:OFF[b] - P + (b + 1) * P]
                dve.tensor_tensor(diag, diag, tri[:], ALU.add)
            dve.drain()
            for b in range(1, NB):
                part = score[:, OFF[b] - P:OFF[b] - P + WIDTH[b]]
                work = tmp[:, 0, 0:WIDTH[b]]
                dve.tensor_copy(work, part)
                dve.drain()
                def round8(i):
                    dve.max(best[:], work)
                    dve.drain()
                    dve.match_replace(work, best[:], work, TAKEN)
                    dve.drain()
                times(dve, TOPK // 8, round8)
                sel_part = dmask[:, OFF[b]:OFF[b] + WIDTH[b]]
                dve.tensor_tensor(sel_part, part, work, ALU.not_equal)
                dve.drain()
                dve.tensor_scalar(sel_part, sel_part, -NEG, NEG, ALU.mult, ALU.add)
                if b == 1:
                    dve.tensor_copy(dmask[:, 0:P], tri[:])
            dve.drain().then_inc(dmask_ready, 1)
            dve.wait_ge(u_ps, 1)
            dve.tensor_copy(row_u[:, 0:T], aux[0:AH, 0, :])
            dve.tensor_copy(row_u[:, T:UROW], aux[0:AH, 1, 0:UROW - T])
            dve.drain().then_inc(row_u_ready, 1)

            run_max = inv_diag[0:MH].rearrange("p b t -> p (b t)")
            dve.tensor_scalar(sq[0:MH, 0, :], sq[0:MH, 0, :], bgate[:, 0:1], None, ALU.add)
            dve.tensor_scalar(sq[0:MH, 1, :], sq[0:MH, 1, :], bgate[:, 1:2], None, ALU.add)
            dve.drain()
            log_forget(sq[0:MH, 1, :], run_max, gate_row[0:MH, :], sq[0:MH, 1, :], 2)
            dve.tensor_tensor(sq[0:MH, 0, :], sq[0:MH, 0, :], sq[0:MH, 1, :], ALU.subtract)
            dve.drain()
            dve.tensor_tensor_scan(run_max, sq[0:MH, 0, :], sq[0:MH, 0, :], 0.0, ALU.max, ALU.max)
            dve.drain()
            dve.tensor_tensor(gate_row[0:MH, :], run_max, sq[0:MH, 1, :], ALU.add).then_inc(fg_ready, 1)
            dve.nop().then_inc(gb_ready, 1)
            dve.wait_ge(mt_ps, 1)
            dve.tensor_copy(mt[:].rearrange("p n b h -> p (n b h)"), ada_ps[:, 0:2 * NB * MH]).then_inc(mt_ready, 1)
            dve.drain()

            def head_decays(h):
                dve.wait_ge(gb_ps, h + 1)
                dve.wait_ge(m_e_ready, h + 1)
                dve.tensor_copy(tmp[:, 0, :], ms[:])
                dve.drain()
                dve.tensor_tensor(tmp[:, 1, :].rearrange("p (b t) -> p b t", b=NB), tmp[:, 0, :].rearrange("p (b t) -> p b t", b=NB),
                                  tri_t[:].unsqueeze(1).broadcast_to([P, NB, P]), ALU.add).then_inc(gb_ready, 1)

            def head_weights(h, e):
                dve.wait_ge(m_e_ready, h + 2)
                dve.wait_ge(qk_ps, h + 2)
                for s in range(NB):
                    ins = dve.tensor_tensor(m_s[:, e, TOFF[s]:TOFF[s] + TW[s]], qk_part(s), m_e[:, TOFF[s]:TOFF[s] + TW[s]], ALU.mult)
                ins.then_inc(m_s_ready, 1)

            def head_outputs(h):
                dve.wait_ge(num_ps, h + 2)
                den = m_stat[:, 0, ds(h, 1), :].rearrange("p a b -> p (a b)")
                for b in range(NB):
                    dve.scalar_tensor_tensor(den[:, b:b + 1], M_BANKS[b][:, MV:MV + 1], -1.0, mt[:, 1, b, h:h + 1], ALU.mult, ALU.max)
                dve.drain()
                for b in range(NB):
                    dve.tensor_tensor(den[:, b:b + 1], den[:, b:b + 1], M_BANKS[b][:, MV:MV + 1], ALU.max)
                dve.drain()
                dve.reciprocal(m_stat[:, 1, ds(h, 1), :].rearrange("p a b -> p (a b)"), den).then_inc(r_ready, 1)
                dve.wait_ge(hm_sq, h + 2)
                for b in range(NB):
                    ins = dve.tensor_copy(hm[:, b, h * MV:(h + 1) * MV], M_BANKS[b][:, 0:MV])
                ins.then_inc(hm_ready, 1)
            dve.nop().then_inc(hm_ready, 1)
            dve.nop().then_inc(m_s_ready, 1)
            head_decays(0)
            head_weights(0, 0)
            head_decays(1)
            head_weights(1, 1)
            for h in range(MH):
                if h + 2 < MH:
                    head_decays(h + 2)
                head_outputs(h)
                if h + 2 < MH:
                    head_weights(h + 2, h % 2)

            def head_scales():
                dve.wait_ge(hm_std, 1)
                dve.reciprocal(m_stat[:, 4], m_stat[:, 3])
                dve.drain()
                dve.tensor_tensor(m_stat[:, 4], m_stat[:, 4], m_stat[:, 1], ALU.mult)
                dve.drain()
                for b in range(NB):
                    part = hm[:, b, :].rearrange("p (h d) -> p h d", h=MH)
                    ins = dve.tensor_tensor(part, part, m_stat[:, 4, :, b].unsqueeze(2).broadcast_to([P, MH, MV]), ALU.mult)
                ins.then_inc(hm_scaled, 1)
            head_scales()
            attention_dve(dve, dx)
            for k in range(12):
                c = CH["mix"] + k
                free_tmp(c)
                dve.wait_ge(mix_t, k + 1)
                if k < 8:
                    dve.scalar_tensor_tensor(tmp[:, c % 4, :], aux[:, k % 2, :], par_c[:, 66 + k:67 + k], ogate[:, k, :],
                                             ALU.mult, ALU.mult).then_inc(t_ready, 1)
                else:
                    dve.tensor_tensor(tmp[:, c % 4, :], aux[:, k % 2, :], az[:, k - 8, :], ALU.mult).then_inc(t_ready, 1)
            st = S["mix_out"]

            def x_chunk(k):
                c = CH["xg"] + k
                free_tmp(c)
                dve.wait_ge(xt_ps, XT["xg"] + k + 1)
                dve.tensor_copy(tmp[:, c % 4, :], XG_BANKS[k % 2]).then_inc(t_ready, 1)
            for g in range(st.groups):
                wait_sums(dve, st, g // 2, g % 2)
                part = x_tok[:, :, g * COLS:(g + 1) * COLS]
                dve.tensor_tensor(part, part, sums_tok(g % 2), ALU.add).then_inc(acc_read["dve"], 1)
                for k in range(max(2 * g - 2, 0), 2 * g):
                    x_chunk(k)
            x_chunk(DC - 2)
            x_chunk(DC - 1)
            for k in range(2):
                dve.wait_ge(p_t, k + 1)
                c = CH["pt"] + k
                free_tmp(c)
                dve.tensor_copy(tmp[:, c % 4, :], aux[:, k, :]).then_inc(t_ready, 1)
            st = S["ple"]
            for i in range(st.iters):
                dve.wait_ge(sg_ready, 2 * FC + i + 1)
                dve.nop().then_inc(acc_read["dve"], 1)
                dve.drain()
                wait_sums(dve, st, i, 1)
                dve.tensor_tensor(tmp[:, 2:4, :], sums(1), tmp[:, 0:2, :], ALU.mult).then_inc(acc_read["dve"], 1)
                dve.drain()
                part = x_tok[:, :, i * COLS:(i + 1) * COLS]
                dve.tensor_tensor(part, part, tmp[:, 2:4, :].rearrange("p a (b n) -> p (a b) n", b=2), ALU.add).then_inc(x_ready, 1)
                add_square_sums(4, i)
            inverse_deviation(5)
            dve.wait_ge(p_landed, 32)
            for b in range(NB):
                dve.scalar_tensor_tensor(x_tok[:, b, :], x_tok[:, b, :], small[:, 4 + b:5 + b], gain_row[:], ALU.mult, ALU.mult).then_inc(out_ready, 1)


INPUTS = ["x", "c", "ada_w", "ada_b", "pre_mix_g", "post_mix_g", "pre_ffn_g", "post_ffn_g", "ffn_w_gu", "ffn_w_down", "a_w_in",
          "a_b_in", "a_ln_g", "a_ln_b", "a_w_s", "a_b_s", "a_w_out", "kv_ada_w", "kv_ada_b", "kv_norm_g", "kv_w", "kv_b_f",
          "k_norm_g", "b_w_qg", "b_q_norm_g", "b_w_o", "p_2", "w_in_2", "b_gate_2", "conv_w_2", "w_out_2", "norm_in_2",
          "m_norm_2", "rel_bias_2", "w_ple_2", "w_ple_gate_2", "norm_final_2"]


def kernel(**inputs):
    import concourse.bacc as bacc
    from concourse.bass_utils import run_bass_kernel_spmd

    nc = bacc.Bacc("TRN2", target_bir_lowering=False, num_devices=1)
    arrays = {name: np.ascontiguousarray(inputs[name]) for name in INPUTS}
    arrays["one_hot"] = distance_buckets()
    io = {}
    for name, a in arrays.items():
        io[name.removesuffix("_2") if name in ("w_ple_2", "w_ple_gate_2") else name] = \
            nc.dram_tensor(f"in_{name}", a.shape, F32, kind="ExternalInput").ap()
    io["out"] = nc.dram_tensor("out", (1, T, D), F32, kind="ExternalOutput").ap()
    io["fox_nd"] = nc.dram_tensor("fox_nd", (NH, T), F32, kind="Internal").ap()
    io["rel_u"] = nc.dram_tensor("rel_u", (AH, P, UROW), F32, kind="Internal").ap()
    build_program(nc, io)
    result = run_bass_kernel_spmd(nc, [{f"in_{name}": a for name, a in arrays.items()}], core_ids=[0])
    return result.results[0]["out"]
```
